# Optimizing a Trainium2 kernel written in Bass

```python
import math
import jax, jax.numpy as jnp
from jax import lax
import numpy as np

D_MODEL = 1024
BATCH = 1
SEQ = 1024
DEPTH = 2
DEC_BATCH = 1
DEC_SEQ = 32
PAST_LEN = 256

CHUNK = 64
N_MIXERS = 2
N_GDN_LAYERS = (DEPTH + 1) // 2
N_MLSTM_LAYERS = DEPTH // 2

GDN_HEADS = 8
GDN_DK = 128
GDN_DV = 128
GDN_KW = GDN_HEADS * GDN_DK
GDN_VW = GDN_HEADS * GDN_DV
GDN_QKV = 2 * GDN_KW + GDN_VW
GDN_IN = GDN_QKV + GDN_VW + 2 * GDN_HEADS
CONV_W = 4
DT_MIN = 1e-3
DT_MAX = 0.1

ML_HEADS = 8
ML_DK = 64
ML_DV = 128
ML_KW = ML_HEADS * ML_DK
ML_VW = ML_HEADS * ML_DV
ML_IN = 2 * ML_KW + 2 * ML_VW + 2 * ML_HEADS

FFN_HIDDEN = ((-(-8 * D_MODEL // 3)) + 255) // 256 * 256

RMS_EPS = 1e-6
L2_EPS = 1e-6
NEG = -1e30

kernel_name = "hybrid_gdn_mlstm_streaming_step"

def rmsnorm(x, g):
    xf = x.astype(jnp.float32)
    y = xf * lax.rsqrt(jnp.mean(xf * xf, -1, keepdims=True) + RMS_EPS)
    return (y * g.astype(jnp.float32)).astype(x.dtype)

def _l2norm(t):
    return t * lax.rsqrt(jnp.sum(t * t, -1, keepdims=True) + L2_EPS)

def _to_chunks(t, L):
    B, T, H, d = t.shape
    return t.reshape(B, T // L, L, H, d).transpose(1, 0, 3, 2, 4)

def _gate_chunks(t, L):
    B, T, H = t.shape
    return t.reshape(B, T // L, L, H).transpose(1, 0, 3, 2)

def _from_chunks(t):
    nc, B, H, L, d = t.shape
    return t.transpose(1, 0, 3, 2, 4).reshape(B, nc * L, H, d)

def causal_dwconv(x, buf, w):
    xp = jnp.concatenate([buf.astype(x.dtype), x], axis=1)
    y = lax.conv_general_dilated(xp, w[:, None, :].astype(x.dtype), (1,), 'VALID',
                                 dimension_numbers=('NWC', 'WIO', 'NWC'),
                                 feature_group_count=x.shape[-1])
    return y, xp[:, -(CONV_W - 1):]

def gated_deltanet(h, conv_buf, S0, w_in, conv_w, a_log, dt_bias, g_norm, w_out, L):
    f32 = jnp.float32
    B, T, _ = h.shape
    H = GDN_HEADS
    proj = h @ w_in
    qkv = proj[..., :GDN_QKV]
    z = proj[..., GDN_QKV:GDN_QKV + GDN_VW]
    a = proj[..., GDN_QKV + GDN_VW:GDN_QKV + GDN_VW + H]
    bb = proj[..., GDN_QKV + GDN_VW + H:]
    qkv_c, new_buf = causal_dwconv(qkv, conv_buf, conv_w)
    qkv_c = jax.nn.silu(qkv_c.astype(f32))
    q = _l2norm(qkv_c[..., :GDN_KW].reshape(B, T, H, GDN_DK)) * (GDN_DK ** -0.5)
    k = _l2norm(qkv_c[..., GDN_KW:2 * GDN_KW].reshape(B, T, H, GDN_DK))
    v = qkv_c[..., 2 * GDN_KW:].reshape(B, T, H, GDN_DV)
    beta = jax.nn.sigmoid(bb.astype(f32))
    g = -jnp.exp(a_log.astype(f32)) * jax.nn.softplus(a.astype(f32) + dt_bias.astype(f32))

    qc, kc, vc = _to_chunks(q, L), _to_chunks(k, L), _to_chunks(v, L)
    bc, gc = _gate_chunks(beta, L), _gate_chunks(g, L)
    decay = jnp.cumsum(gc, axis=-1)
    causal = jnp.tril(jnp.ones((L, L), bool))
    strict = jnp.tril(jnp.ones((L, L), bool), -1)
    diff = decay[..., :, None] - decay[..., None, :]
    gamma = jnp.where(causal, jnp.exp(jnp.where(causal, diff, 0.0)), 0.0)
    kk = jnp.einsum('cbhik,cbhjk->cbhij', kc, kc)
    A = jnp.where(strict, bc[..., :, None] * kk * gamma, 0.0)
    eye = jnp.eye(L, dtype=f32)
    Tm = lax.linalg.triangular_solve(eye + A, jnp.broadcast_to(eye, A.shape),
                                     left_side=True, lower=True, unit_diagonal=True)
    u = jnp.einsum('cbhij,cbhjv->cbhiv', Tm, vc * bc[..., None])
    w = jnp.einsum('cbhij,cbhjk->cbhik', Tm, kc * (bc * jnp.exp(decay))[..., None])
    attn = jnp.einsum('cbhik,cbhjk->cbhij', qc, kc) * gamma
    q_dec = qc * jnp.exp(decay)[..., None]
    k_tail = kc * jnp.exp(decay[..., -1:] - decay)[..., None]
    d_last = jnp.exp(decay[..., -1])

    def step(S, xs):
        u_c, w_c, attn_c, qd_c, kt_c, dl_c = xs
        v_new = u_c - jnp.einsum('bhlk,bhkv->bhlv', w_c, S)
        o = jnp.einsum('bhlk,bhkv->bhlv', qd_c, S) + jnp.einsum('bhij,bhjv->bhiv', attn_c, v_new)
        S = S * dl_c[..., None, None] + jnp.einsum('bhlk,bhlv->bhkv', kt_c, v_new)
        return S, o

    S_fin, o = lax.scan(step, S0.astype(f32), (u, w, attn, q_dec, k_tail, d_last))
    o = _from_chunks(o)
    o = o * lax.rsqrt(jnp.mean(o * o, -1, keepdims=True) + RMS_EPS) * g_norm.astype(f32)
    o = o * jax.nn.silu(z.astype(f32).reshape(B, T, H, GDN_DV))
    y = o.reshape(B, T, GDN_VW).astype(h.dtype) @ w_out
    return y, new_buf, S_fin

def mlstm(h, C0, n0, m0, w_in, b_i, b_f, g_norm, w_out, L):
    f32 = jnp.float32
    B, T, _ = h.shape
    H = ML_HEADS
    proj = h @ w_in
    q = proj[..., :ML_KW].astype(f32).reshape(B, T, H, ML_DK)
    k = proj[..., ML_KW:2 * ML_KW].astype(f32).reshape(B, T, H, ML_DK) * (ML_DK ** -0.5)
    v = proj[..., 2 * ML_KW:2 * ML_KW + ML_VW].astype(f32).reshape(B, T, H, ML_DV)
    o_pre = proj[..., 2 * ML_KW + ML_VW:2 * ML_KW + 2 * ML_VW]
    i_pre = proj[..., 2 * ML_KW + 2 * ML_VW:2 * ML_KW + 2 * ML_VW + H]
    f_pre = proj[..., 2 * ML_KW + 2 * ML_VW + H:]
    ig = i_pre.astype(f32) + b_i.astype(f32)
    lf = jax.nn.log_sigmoid(f_pre.astype(f32) + b_f.astype(f32))

    qc, kc, vc = _to_chunks(q, L), _to_chunks(k, L), _to_chunks(v, L)
    igc, lfc = _gate_chunks(ig, L), _gate_chunks(lf, L)
    b = jnp.cumsum(lfc, axis=-1)
    causal = jnp.tril(jnp.ones((L, L), bool))
    log_d = jnp.where(causal, b[..., :, None] - b[..., None, :] + igc[..., None, :], NEG)
    m_intra = jnp.max(log_d, axis=-1)
    d_hat = jnp.exp(log_d - m_intra[..., None])
    s_hat = jnp.einsum('cbhik,cbhjk->cbhij', qc, kc) * d_hat
    num_hat = jnp.einsum('cbhij,cbhjv->cbhiv', s_hat, vc)
    qn_hat = jnp.sum(s_hat, axis=-1)
    log_w = b[..., -1:] - b + igc
    m_w = jnp.max(log_w, axis=-1)
    w_hat = jnp.exp(log_w - m_w[..., None])
    ckv_hat = jnp.einsum('cbhl,cbhlk,cbhlv->cbhkv', w_hat, kc, vc)
    n_hat = jnp.einsum('cbhl,cbhlk->cbhk', w_hat, kc)
    b_last = b[..., -1]

    def step(carry, xs):
        C, n, m = carry
        q_c, b_c, mi_c, num_c, qn_c, bl_c, mw_c, ckv_c, nh_c = xs
        log_inter = b_c + m[..., None]
        m_t = jnp.maximum(log_inter, mi_c)
        s_inter = jnp.exp(log_inter - m_t)
        s_intra = jnp.exp(mi_c - m_t)
        num = s_inter[..., None] * jnp.einsum('bhlk,bhkv->bhlv', q_c, C) + s_intra[..., None] * num_c
        qn = s_inter * jnp.einsum('bhlk,bhk->bhl', q_c, n) + s_intra * qn_c
        hcell = num / jnp.maximum(jnp.abs(qn), jnp.exp(-m_t))[..., None]
        m_new = jnp.maximum(bl_c + m, mw_c)
        a_old = jnp.exp(bl_c + m - m_new)
        a_new = jnp.exp(mw_c - m_new)
        C = a_old[..., None, None] * C + a_new[..., None, None] * ckv_c
        n = a_old[..., None] * n + a_new[..., None] * nh_c
        return (C, n, m_new), hcell

    (C_f, n_f, m_f), hc = lax.scan(step, (C0.astype(f32), n0.astype(f32), m0.astype(f32)),
                                   (qc, b, m_intra, num_hat, qn_hat, b_last, m_w, ckv_hat, n_hat))
    hc = _from_chunks(hc)
    hc = hc * lax.rsqrt(jnp.mean(hc * hc, -1, keepdims=True) + RMS_EPS)
    hc = hc.reshape(B, T, ML_VW) * g_norm.astype(f32) * jax.nn.sigmoid(o_pre.astype(f32))
    y = hc.astype(h.dtype) @ w_out
    return y, C_f, n_f, m_f

def swiglu(h, w_gu, w_down):
    gu = h @ w_gu
    return (jax.nn.silu(gu[..., :FFN_HIDDEN]) * gu[..., FFN_HIDDEN:]) @ w_down

def _trunk(x, conv0, S0, C0, n0, m0, L, norm_mix, gdn_w_in, gdn_conv_w, gdn_a_log, gdn_dt_bias,
           gdn_norm, gdn_w_out, ml_w_in, ml_b_i, ml_b_f, ml_norm, ml_w_out, norm_ffn, ffn_w_gu,
           ffn_w_down, norm_final):
    convs, Ss, Cs, ns, ms = [], [], [], [], []
    for i in range(DEPTH):
        j = i // N_MIXERS
        hn = rmsnorm(x, norm_mix[i])
        if i % N_MIXERS == 0:
            y, cb, S = gated_deltanet(hn, conv0[j], S0[j], gdn_w_in[j], gdn_conv_w[j], gdn_a_log[j],
                                      gdn_dt_bias[j], gdn_norm[j], gdn_w_out[j], L)
            convs.append(cb)
            Ss.append(S)
        else:
            y, C, n, m = mlstm(hn, C0[j], n0[j], m0[j], ml_w_in[j], ml_b_i[j], ml_b_f[j],
                               ml_norm[j], ml_w_out[j], L)
            Cs.append(C)
            ns.append(n)
            ms.append(m)
        x = x + y
        x = x + swiglu(rmsnorm(x, norm_ffn[i]), ffn_w_gu[i], ffn_w_down[i])
    return (rmsnorm(x, norm_final), jnp.stack(convs), jnp.stack(Ss), jnp.stack(Cs),
            jnp.stack(ns), jnp.stack(ms))

def setup_inputs(seed: int = 0) -> dict:
    key = jax.random.key(seed)
    ks = jax.random.split(key, 24)
    f32 = jnp.float32
    NG, NM = N_GDN_LAYERS, N_MLSTM_LAYERS

    def nrm(k, shape, s):
        return s * jax.random.normal(k, shape, f32)

    dt = jnp.exp(jax.random.uniform(ks[10], (NG, GDN_HEADS), f32, math.log(DT_MIN), math.log(DT_MAX)))
    return {
        "x_prompt": nrm(ks[0], (BATCH, SEQ, D_MODEL), 1.0),
        "x_sample": nrm(ks[1], (DEC_BATCH, DEC_SEQ, D_MODEL), 1.0),
        "state_gdn_conv": nrm(ks[2], (NG, DEC_BATCH, CONV_W - 1, GDN_QKV), 1.0),
        "state_gdn_S": nrm(ks[3], (NG, DEC_BATCH, GDN_HEADS, GDN_DK, GDN_DV), 0.1),
        "state_mlstm_C": nrm(ks[4], (NM, DEC_BATCH, ML_HEADS, ML_DK, ML_DV), 0.3),
        "state_mlstm_n": nrm(ks[5], (NM, DEC_BATCH, ML_HEADS, ML_DK), 0.3),
        "state_mlstm_m": nrm(ks[6], (NM, DEC_BATCH, ML_HEADS), 1.0),
        "norm_mix": 1.0 + nrm(ks[7], (DEPTH, D_MODEL), 0.01),
        "gdn_w_in": nrm(ks[8], (NG, D_MODEL, GDN_IN), D_MODEL ** -0.5),
        "gdn_conv_w": nrm(ks[9], (NG, CONV_W, GDN_QKV), CONV_W ** -0.5),
        "gdn_a_log": jnp.log(jax.random.uniform(ks[11], (NG, GDN_HEADS), f32, 1.0, 16.0)),
        "gdn_dt_bias": dt + jnp.log(-jnp.expm1(-dt)),
        "gdn_norm": 1.0 + nrm(ks[12], (NG, GDN_DV), 0.01),
        "gdn_w_out": nrm(ks[13], (NG, GDN_VW, D_MODEL), GDN_VW ** -0.5),
        "ml_w_in": nrm(ks[14], (NM, D_MODEL, ML_IN), D_MODEL ** -0.5),
        "ml_b_i": nrm(ks[15], (NM, ML_HEADS), 0.1),
        "ml_b_f": 3.0 + nrm(ks[16], (NM, ML_HEADS), 0.5),
        "ml_norm": 1.0 + nrm(ks[17], (NM, ML_VW), 0.01),
        "ml_w_out": nrm(ks[18], (NM, ML_VW, D_MODEL), ML_VW ** -0.5),
        "norm_ffn": 1.0 + nrm(ks[19], (DEPTH, D_MODEL), 0.01),
        "ffn_w_gu": nrm(ks[20], (DEPTH, D_MODEL, 2 * FFN_HIDDEN), D_MODEL ** -0.5),
        "ffn_w_down": nrm(ks[21], (DEPTH, FFN_HIDDEN, D_MODEL), FFN_HIDDEN ** -0.5),
        "norm_final": 1.0 + nrm(ks[22], (D_MODEL,), 0.01),
    }

def reference(x_prompt, x_sample, state_gdn_conv, state_gdn_S, state_mlstm_C, state_mlstm_n,
              state_mlstm_m, norm_mix, gdn_w_in, gdn_conv_w, gdn_a_log, gdn_dt_bias, gdn_norm,
              gdn_w_out, ml_w_in, ml_b_i, ml_b_f, ml_norm, ml_w_out, norm_ffn, ffn_w_gu,
              ffn_w_down, norm_final):
    f32 = jnp.float32
    Bp = x_prompt.shape[0]
    NG, NM = N_GDN_LAYERS, N_MLSTM_LAYERS
    p_conv0 = jnp.zeros((NG, Bp, CONV_W - 1, GDN_QKV), x_prompt.dtype)
    p_S0 = jnp.zeros((NG, Bp, GDN_HEADS, GDN_DK, GDN_DV), f32)
    p_C0 = jnp.zeros((NM, Bp, ML_HEADS, ML_DK, ML_DV), f32)
    p_n0 = jnp.zeros((NM, Bp, ML_HEADS, ML_DK), f32)
    p_m0 = jnp.zeros((NM, Bp, ML_HEADS), f32)
    y_prompt, p_conv, p_S, p_C, p_n, p_m = _trunk(
        x_prompt, p_conv0, p_S0, p_C0, p_n0, p_m0, CHUNK, norm_mix, gdn_w_in, gdn_conv_w,
        gdn_a_log, gdn_dt_bias, gdn_norm, gdn_w_out, ml_w_in, ml_b_i, ml_b_f, ml_norm, ml_w_out,
        norm_ffn, ffn_w_gu, ffn_w_down, norm_final)
    y_sample, s_conv, s_S, s_C, s_n, s_m = _trunk(
        x_sample, state_gdn_conv, state_gdn_S, state_mlstm_C, state_mlstm_n, state_mlstm_m,
        x_sample.shape[1], norm_mix, gdn_w_in, gdn_conv_w, gdn_a_log, gdn_dt_bias, gdn_norm,
        gdn_w_out, ml_w_in, ml_b_i, ml_b_f, ml_norm, ml_w_out, norm_ffn, ffn_w_gu, ffn_w_down,
        norm_final)
    return (y_prompt, y_sample, p_conv, p_S, p_C, p_n, p_m, s_conv, s_S, s_C, s_n, s_m)


_drawn_inputs = setup_inputs


def setup_inputs(seed=0):
    import zlib

    import numpy as np

    out = dict(_drawn_inputs(seed))
    spreads = {}
    factors = {'gdn_norm': 5.902, 'ml_norm': 8.0, 'norm_ffn': 4.747, 'norm_final': 5.652}
    for name, (base, spread) in spreads.items():
        noise = np.random.default_rng([zlib.crc32(name.encode()), seed]).standard_normal(out[name].shape)
        drawn = base * np.exp(spread * noise) if base else spread * noise
        out[name] = __import__('jax').numpy.asarray(drawn.astype(out[name].dtype))
    for name, factor in factors.items():
        out[name] = (out[name] * factor).astype(out[name].dtype)
    return out
```

```python
import math
from contextlib import ExitStack

import concourse.bass as bass
from concourse import mybir

ALU = mybir.AluOpType
ACT = mybir.ActivationFunctionType
AX = mybir.AxisListType
F32 = mybir.dt.float32
F32R = mybir.dt.float32r
BF16 = mybir.dt.bfloat16

P = 128
PROMPT = 1024
SAMPLE = 32
TOK = PROMPT + SAMPLE
D = 1024
KB = D // P
NU = 3
UNIT = TOK // NU
HEADS = 8
DK, DV = 128, 128
MDK = 64
FFN = 2816
FB = FFN // P
TILES = 9
BATCHES = 3
HIST = 3
TAPS = 4
GCOL = PROMPT + HIST
CW = GCOL + SAMPLE
CPAD = GCOL + P
CU = CW // NU
LEVELS = 7
RMS_EPS = 1e-6
L2_EPS = 1e-6
NEG = -1e30


def tile_cols(c):
    start = c * P if c < TILES - 1 else GCOL
    return slice(start, start + P)


def unit_cols(n):
    return slice(n * UNIT, (n + 1) * UNIT)


def semaphores(nc, ctx, tag, again=False):
    made = []

    def sem(name):
        if again:
            made.append(nc.alloc_semaphore(name=f"{tag}_{name}"))
            return made[-1]
        return ctx.enter_context(nc.semaphore(f"{tag}_{name}"))

    def zero():
        if made:
            nc.clear_and_free_semaphores(made)
            nc.all_engine_barrier()

    ctx.callback(zero)
    return sem


def split_product(pe, out, w_hi, w_lo, rhs_hi, rhs_lo, first, last):
    pe.matmul(out, w_hi, rhs_hi, start=first, stop=False)
    pe.matmul(out, w_hi, rhs_lo, start=False, stop=False)
    return pe.matmul(out, w_lo, rhs_hi, start=False, stop=last)


class Trunk:
    pass


class WeightStream:

    def __init__(self, nc, tk, ctx, sem, name, ring, stages=2):
        self.nc, self.ring, self.stages, self.one = nc, ring, stages, tk.one
        buf = lambda s, *a: ctx.enter_context(nc.sbuf_tensor(f"{name}_{s}", *a))
        self.stage = buf("stage", [P, stages, KB, P], F32)
        self.hi = buf("hi", [P, ring, KB, P], F32R)
        self.lo = buf("lo", [P, ring, KB, P], F32R)
        self.landed = [sem(f"w_landed{s}") for s in range(stages)]
        self.hi_done = sem("w_hi_done")
        self.split_done = sem("w_split_done")

        self.checked = sem("w_checked")

    def start(self, pool):
        pool.sem_inc(self.split_done, self.stages)

    def wait_stage(self, sp, j):
        sp.wait_ge(self.split_done, j + 1)
        sp.sem_inc(self.checked, 1)

    def load(self, sp, j, slot, src):
        self.wait_stage(sp, j)
        sp.dma_start(self.stage[:, slot], src).then_inc(self.landed[slot], 16)

    def split(self, pool, j, stage_slot, landed_count, ring_slot):
        nc = self.nc
        st = self.stage[:, stage_slot]
        hi, lo = self.hi[:, ring_slot], self.lo[:, ring_slot]
        pool.wait_ge(self.landed[stage_slot], landed_count)
        one = self.one[:][:, :, None].to_broadcast([P, KB, P])
        nc.gpsimd.tensor_tensor(hi, st, one, ALU.mult).then_inc(self.hi_done, 1)
        pool.wait_ge(self.hi_done, j + 1)
        nc.gpsimd.tensor_tensor(lo, st, hi.bitcast(F32), ALU.subtract).then_inc(self.split_done, 1)

    def wait_ready(self, pe, j):
        pe.wait_ge(self.split_done, j + self.stages + 1)


def ffn_phase(nc, tk, w_gu, w_down, tag):
    TURN = FB // 2
    B = 6
    U = 4 * NU + NU * KB
    ps, x = tk.ps, tk.x
    with ExitStack() as ctx:
        sem = semaphores(nc, ctx, tag)
        buf = lambda s, *a: ctx.enter_context(nc.sbuf_tensor(f"{tag}_{s}", *a))
        ws = WeightStream(nc, tk, ctx, sem, tag, B)
        silu = buf("silu", [P, NU, UNIT], F32)
        hid = buf("hid", [P, NU, UNIT], F32)
        hid_hi = buf("hid_hi", [P, 2, NU, UNIT], F32R)
        hid_lo = buf("hid_lo", [P, 2, NU, UNIT], F32R)
        unit_done = sem("unit_done")
        silu_done = sem("silu_done")
        hid_done = sem("hid_done")
        hi_done = sem("hid_hi_done")
        lo_done = sem("hid_lo_done")
        added = sem("added")
        gu = w_gu.rearrange("(k p) f -> p k f", p=P)
        dn = w_down.rearrange("(j p) (m c) -> p j m c", p=P, c=P)
        block = ctx.enter_context(nc.Block())

        @block.sync
        def _(sp):
            with sp.Fori(0, TURN) as t:
                for b in range(4):
                    ws.load(sp, t * B + b, b % 2,
                            gu[:, :, bass.ds(t * (2 * P) + (b // 2 * P + b % 2 * FFN), P)])
                for j in range(2):
                    ws.load(sp, t * B + (4 + j), j, dn[:, t * 2 + j])

        @block.gpsimd
        def _(pool):
            ws.start(pool)
            pool.sem_inc(unit_done, U)
            pool.sem_inc(silu_done, NU)
            pool.sem_inc(hid_done, NU)
            pool.sem_inc(lo_done, NU)
            pool.sem_inc(added, 2)
            with pool.Fori(0, TURN) as t:
                for b in range(B):
                    pool.wait_ge(unit_done, t * U + (NU * (b + 1) if b < 4 else U))
                    ws.split(pool, t * B + b, b % 2, t * 48 + (b // 2 * 16 + 16), b)

        @block.tensor
        def _(pe):
            with pe.Fori(0, TURN) as t:
                for b in range(4):
                    ws.wait_ready(pe, t * B + b)
                    for n in range(NU):
                        pe.wait_ge(hid_done if b % 2 else silu_done, t * 6 + (b // 2 * NU + n + 1))
                        out = ps[:, b % 2 * NU + n, 0:UNIT]
                        for k in range(KB):
                            mm = split_product(pe, out, ws.hi[:, b, k], ws.lo[:, b, k],
                                               tk.hi[:, k, unit_cols(n)], tk.lo[:, k, unit_cols(n)],
                                               k == 0, k == KB - 1)
                        mm.then_inc(unit_done, 1)
                ws.wait_ready(pe, t * B + 5)
                for n in range(NU):
                    pe.wait_ge(hi_done, t * 6 + (NU + n + 1))
                    pe.wait_ge(lo_done, t * 6 + (2 * NU + n + 1))
                    for m in range(KB):
                        pe.wait_ge(added, t * (NU * KB) + (n * KB + m + 1))
                        for j in range(2):
                            mm = split_product(pe, ps[:, 6 + m % 2, 0:UNIT],
                                               ws.hi[:, 4 + j, m], ws.lo[:, 4 + j, m],
                                               hid_hi[:, j, n], hid_lo[:, j, n], j == 0, j == 1)
                        mm.then_inc(unit_done, 1)

        @block.scalar
        def _(act):
            with act.Fori(0, TURN) as t:
                for j in range(2):
                    for n in range(NU):
                        act.wait_ge(unit_done, t * U + (U + 6 * j + n + 1))
                        act.wait_ge(hid_done, t * 6 + (j * NU + n + 1))
                        nc.scalar.activation(silu[:, n], ps[:, n, 0:UNIT], ACT.Silu).then_inc(silu_done, 1)
                    for n in range(NU):
                        act.wait_ge(hid_done, t * 6 + (j * NU + NU + n + 1))
                        act.wait_ge(unit_done, t * U + U)
                        nc.scalar.copy(hid_hi[:, j, n], hid[:, n]).then_inc(hi_done, 1)

        @block.vector
        def _(dve):
            with dve.Fori(0, TURN) as t:
                for j in range(2):
                    for n in range(NU):
                        dve.wait_ge(unit_done, t * U + (U + 6 * j + NU + n + 1))
                        dve.wait_ge(silu_done, t * 6 + (j * NU + NU + n + 1))
                        dve.wait_ge(lo_done, t * 6 + (j * NU + n + 1))
                        nc.vector.tensor_tensor(hid[:, n], silu[:, n], ps[:, NU + n, 0:UNIT],
                                                ALU.mult).then_inc(hid_done, 1)
                        dve.wait_ge(hi_done, t * 6 + (j * NU + n + 1))
                        nc.vector.tensor_tensor(hid_lo[:, j, n], hid[:, n], hid_hi[:, j, n].bitcast(F32),
                                                ALU.subtract).then_inc(lo_done, 1)
                for n in range(NU):
                    for m in range(KB):
                        dve.wait_ge(unit_done, t * U + (U + 4 * NU + n * KB + m + 1))
                        dve.wait_ge(added, t * (NU * KB) + 2)
                        nc.vector.tensor_tensor(x[:, m, unit_cols(n)], x[:, m, unit_cols(n)],
                                                ps[:, 6 + m % 2, 0:UNIT], ALU.add).then_inc(added, 1)


def norm_phase(nc, tk, gain, tag, spill):
    ps, x = tk.ps, tk.x
    with ExitStack() as ctx:
        sem = semaphores(nc, ctx, tag)
        buf = lambda s, *a: ctx.enter_context(nc.sbuf_tensor(f"{tag}_{s}", *a))
        g = buf("g", [P, KB], F32)
        sq = buf("sq", [P, KB, UNIT], F32)
        r = buf("r", [P, NU, UNIT], F32)
        h = buf("h", [P, KB, UNIT], F32)
        g_in, spilled = sem("gain_landed"), sem("x_spilled")
        sq_done, ss_done, ln_done, r_done = sem("sq_done"), sem("ss_done"), sem("ln_done"), sem("r_done")
        h_done, hi_done, lo_done = sem("h_done"), sem("hi_done"), sem("lo_done")
        block = ctx.enter_context(nc.Block())

        @block.sync
        def _(sp):
            sp.dma_start(g[:], gain.rearrange("(k p) -> p k", p=P), allow_slow_non_contiguous=True).then_inc(g_in, 16)
            if spill:
                sp.dma_start(tk.x_dram, x[:]).then_inc(spilled, 16)
                sp.wait_ge(spilled, 16)

        @block.tensor
        def _(pe):
            for n in range(NU):
                pe.wait_ge(sq_done, n + 1)
                for k in range(KB):
                    mm = pe.matmul(ps[:, n, 0:UNIT], tk.ones[:], sq[:, k], start=k == 0, stop=k == KB - 1)
                mm.then_inc(ss_done, 1)

        @block.scalar
        def _(act):
            nc.scalar.preload_act_table_set("natural_log_exp_and_others")

            def scale(n):
                act.wait_ge(ss_done, n + 1)
                nc.scalar.activation(r[:, n], ps[:, n, 0:UNIT], ACT.Ln, bias=tk.eps[:, 0:1],
                                     scale=1.0 / D).then_inc(ln_done, 1)
                act.wait_ge(ln_done, n + 1)
                nc.scalar.activation(r[:, n], r[:, n], ACT.Exp, scale=-0.5).then_inc(r_done, 1)

            for n in range(NU):
                if n >= 1:
                    act.wait_ge(ss_done, n)
                nc.scalar.activation(sq[:], x[:, :, unit_cols(n)], ACT.Square).then_inc(sq_done, 1)
                scale(n)
                act.wait_ge(h_done, n + 1)
                nc.scalar.copy(tk.hi[:, :, unit_cols(n)], h[:]).then_inc(hi_done, 1)

        @block.vector
        def _(dve):
            dve.wait_ge(g_in, 16)
            for n in range(NU):
                dve.wait_ge(r_done, n + 1)
                if n >= 1:
                    dve.wait_ge(lo_done, n)
                for k in range(KB):
                    op = nc.vector.scalar_tensor_tensor(out=h[:, k], in0=x[:, k, unit_cols(n)], scalar=g[:, k:k + 1],
                                                        in1=r[:, n], op0=ALU.mult, op1=ALU.mult)
                op.then_inc(h_done, 1)
                dve.wait_ge(hi_done, n + 1)
                nc.vector.tensor_tensor(tk.lo[:, :, unit_cols(n)], h[:], tk.hi[:, :, unit_cols(n)].bitcast(F32),
                                        ALU.subtract).then_inc(lo_done, 1)
            dve.wait_ge(lo_done, NU)


def load_phase(nc, tk, x_prompt, x_sample):
    ps, x = tk.ps, tk.x
    with ExitStack() as ctx:
        sem = semaphores(nc, ctx, "load")
        buf = lambda s, *a: ctx.enter_context(nc.sbuf_tensor(f"load_{s}", *a))
        rows = buf("rows", [P, 3, D], F32)
        landed = [sem(f"rows_landed{s}") for s in range(3)]
        made, turned, copied = sem("constants_made"), sem("turned"), sem("copied")
        block = ctx.enter_context(nc.Block())

        def size(c):
            return P if c < TILES - 1 else SAMPLE

        @block.sync
        def _(sp):
            for c in range(TILES):
                if c >= 3:
                    sp.wait_ge(turned, 2 * (c - 2))
                src = x_prompt[0, c * P:(c + 1) * P] if c < TILES - 1 else x_sample[0]
                sp.dma_start(rows[0:size(c), c % 3], src).then_inc(landed[c % 3], 16)

        @block.gpsimd
        def _(pool):
            n = 0
            def step(op):
                nonlocal n
                n += 1
                op.then_inc(made, 1)
                pool.wait_ge(made, n)
            step(nc.gpsimd.memset(tk.ones[:], 1.0))
            step(nc.gpsimd.memset(tk.eps[:], RMS_EPS))
            step(nc.gpsimd.memset(tk.one[:], 1.0))
            step(nc.gpsimd.memset(tk.log_dk[:], -0.5 * math.log(DK)))
            step(nc.gpsimd.affine_select(out=tk.ident[:], in_=tk.ones[:], compare_op=ALU.is_equal, fill=0.0,
                                         base=0, pattern=[[1, P]], channel_multiplier=-1))
            step(nc.gpsimd.affine_select(out=tk.upto[:], in_=tk.ones[:], compare_op=ALU.is_ge, fill=0.0,
                                         base=0, pattern=[[1, P]], channel_multiplier=-1))
            step(nc.gpsimd.memset(tk.later_neg[:], 0.0))
            step(nc.gpsimd.affine_select(out=tk.later_neg[:], in_=tk.later_neg[:], compare_op=ALU.is_ge, fill=NEG,
                                         base=0, pattern=[[1, P]], channel_multiplier=-1))
            step(nc.gpsimd.memset(tk.earlier_neg[:], 0.0))
            step(nc.gpsimd.affine_select(out=tk.earlier_neg[:], in_=tk.earlier_neg[:], compare_op=ALU.is_ge, fill=NEG,
                                         base=0, pattern=[[-1, P]], channel_multiplier=1))
            step(nc.gpsimd.memset(tk.joins[:], 0.0))
            for l in range(LEVELS):
                s = 1 << l
                blocks = P // (2 * s)
                view = tk.joins[:, l].rearrange("p (b h c) -> p b h c", b=blocks, h=2)
                step(nc.gpsimd.memset(view[:, :, 1], 1.0))
                step(nc.gpsimd.affine_select(out=view[:, :, 1], in_=view[:, :, 1], compare_op=ALU.is_ge, fill=0.0,
                                             base=0, pattern=[[-2 * s, blocks], [0, s]], channel_multiplier=1))
                step(nc.gpsimd.affine_select(out=view[:, :, 1], in_=view[:, :, 1], compare_op=ALU.is_ge, fill=0.0,
                                             base=s - 1, pattern=[[2 * s, blocks], [0, s]], channel_multiplier=-1))

        @block.tensor
        def _(pe):
            pe.wait_ge(made, 5)
            for c in range(TILES):
                pe.wait_ge(landed[c % 3], 16 * (c // 3 + 1))
                for half in range(2):
                    if c >= 2:
                        pe.wait_ge(copied, 2 * (c - 2) + half + 1)
                    for k in range(4):
                        mm = pe.transpose(ps[:, (c % 2) * 2 + half, k * P:k * P + size(c)],
                                          rows[0:size(c), c % 3, (half * 4 + k) * P:(half * 4 + k + 1) * P],
                                          tk.ident[0:size(c), 0:size(c)])
                    mm.then_inc(turned, 1)

        @block.vector
        def _(dve):
            for c in range(TILES):
                for half in range(2):
                    dve.wait_ge(turned, 2 * c + half + 1)
                    src = ps[:, (c % 2) * 2 + half].rearrange("p (k t) -> p k t", k=4)[:, :, 0:size(c)]
                    nc.vector.tensor_copy(x[:, half * 4:half * 4 + 4, c * P:c * P + size(c)], src).then_inc(copied, 1)
            dve.wait_ge(copied, 2 * TILES)


def store_phase(nc, tk, gain, y_prompt, y_sample):
    ps, x = tk.ps, tk.x
    with ExitStack() as ctx:
        sem = semaphores(nc, ctx, "store")
        buf = lambda s, *a: ctx.enter_context(nc.sbuf_tensor(f"store_{s}", *a))
        g = buf("g", [P, KB], F32)
        sq = buf("sq", [P, KB, UNIT], F32)
        r = buf("r", [P, TOK], F32)
        rows = buf("rows", [P, 2, D], F32)
        g_in, sq_done, ss_done, ln_done, r_done, y_done = (
            sem("gain_landed"), sem("sq_done"), sem("ss_done"), sem("ln_done"), sem("r_done"), sem("y_done"))
        turned, copied, stored = sem("turned"), sem("copied"), [sem("stored0"), sem("stored1")]
        block = ctx.enter_context(nc.Block())

        def size(c):
            return P if c < TILES - 1 else SAMPLE

        def unit_of(c):
            return (c * P + size(c) - 1) // UNIT

        @block.sync
        def _(sp):
            sp.dma_start(g[:], gain.rearrange("(k p) -> p k", p=P), allow_slow_non_contiguous=True).then_inc(g_in, 16)
            for c in range(TILES):
                sp.wait_ge(copied, 2 * (c + 1))
                dst = y_prompt[0, c * P:(c + 1) * P] if c < TILES - 1 else y_sample[0]
                sp.dma_start(dst, rows[0:size(c), c % 2]).then_inc(stored[c % 2], 16)
            sp.wait_ge(stored[0], 16 * 5)
            sp.wait_ge(stored[1], 16 * 4)

        @block.tensor
        def _(pe):
            for n in range(NU):
                pe.wait_ge(sq_done, n + 1)
                for k in range(KB):
                    mm = pe.matmul(ps[:, 4 + n, 0:UNIT], tk.ones[:], sq[:, k], start=k == 0, stop=k == KB - 1)
                mm.then_inc(ss_done, 1)
            for c in range(TILES):
                if c == 0 or unit_of(c) != unit_of(c - 1):
                    pe.wait_ge(y_done, unit_of(c) + 1)
                for half in range(2):
                    if c >= 2:
                        pe.wait_ge(copied, 2 * (c - 2) + half + 1)
                    for k in range(4):
                        mm = pe.transpose(ps[0:size(c), (c % 2) * 2 + half, k * P:(k + 1) * P],
                                          x[:, half * 4 + k, c * P:c * P + size(c)], tk.ident[:])
                    mm.then_inc(turned, 1)

        @block.scalar
        def _(act):
            nc.scalar.preload_act_table_set("natural_log_exp_and_others")
            for n in range(NU):
                if n >= 1:
                    act.wait_ge(ss_done, n)
                nc.scalar.activation(sq[:], x[:, :, unit_cols(n)], ACT.Square).then_inc(sq_done, 1)
                act.wait_ge(ss_done, n + 1)
                nc.scalar.activation(r[:, unit_cols(n)], ps[:, 4 + n, 0:UNIT], ACT.Ln, bias=tk.eps[:, 0:1],
                                     scale=1.0 / D).then_inc(ln_done, 1)
                act.wait_ge(ln_done, n + 1)
                nc.scalar.activation(r[:, unit_cols(n)], r[:, unit_cols(n)], ACT.Exp, scale=-0.5).then_inc(r_done, 1)
            for c in range(TILES):
                if c >= 2:
                    act.wait_ge(stored[c % 2], 16 * (c // 2))
                for half in range(2):
                    act.wait_ge(turned, 2 * c + half + 1)
                    nc.scalar.copy(rows[0:size(c), c % 2, half * 512:(half + 1) * 512],
                                   ps[0:size(c), (c % 2) * 2 + half]).then_inc(copied, 1)

        @block.vector
        def _(dve):
            dve.wait_ge(g_in, 16)
            for n in range(NU):
                dve.wait_ge(r_done, n + 1)
                for k in range(KB):
                    op = nc.vector.scalar_tensor_tensor(out=x[:, k, unit_cols(n)], in0=x[:, k, unit_cols(n)],
                                                        scalar=g[:, k:k + 1], in1=r[:, unit_cols(n)],
                                                        op0=ALU.mult, op1=ALU.mult)
                op.then_inc(y_done, 1)


def out_phase(nc, tk, w_out, tag):
    ps, x = tk.ps, tk.x
    with ExitStack() as ctx:
        sem = semaphores(nc, ctx, tag)
        buf = lambda s, *a: ctx.enter_context(nc.sbuf_tensor(f"{tag}_{s}", *a))
        ws = WeightStream(nc, tk, ctx, sem, tag, 2)
        x_in = sem("x_landed")
        unit_done = sem("unit_done")
        added = sem("added")
        hi_done, lo_done = sem("o_hi_done"), sem("o_lo_done")
        w = w_out.rearrange("(k p) f -> p k f", p=P)
        block = ctx.enter_context(nc.Block())

        @block.sync
        def _(sp):
            sp.wait_ge(lo_done, KB)
            sp.dma_start(x[:], tk.x_dram).then_inc(x_in, 16)
            with sp.Fori(0, KB // 2) as t:
                for b in range(2):
                    ws.load(sp, t * 2 + b, b, w[:, :, bass.ds(t * (2 * P) + b * P, P)])

        @block.gpsimd
        def _(pool):
            ws.start(pool)
            pool.sem_inc(unit_done, 6)
            pool.sem_inc(added, 6)
            with pool.Fori(0, KB // 2) as t:
                for b in range(2):
                    pool.wait_ge(unit_done, t * 6 + (3 * b + 3))
                    ws.split(pool, t * 2 + b, b, t * 16 + 16, b)

        @block.scalar
        def _(act):
            for k in range(KB):
                nc.scalar.copy(tk.hi[:, k], x[:, k]).then_inc(hi_done, 1)

        @block.tensor
        def _(pe):
            pe.wait_ge(lo_done, KB)
            with pe.Fori(0, KB // 2) as t:
                for b in range(2):
                    ws.wait_ready(pe, t * 2 + b)
                    for n in range(NU):
                        pe.wait_ge(added, t * 6 + (3 * b + n + 1))
                        for k in range(KB):
                            mm = split_product(pe, ps[:, 3 * b + n, 0:UNIT], ws.hi[:, b, k], ws.lo[:, b, k],
                                               tk.hi[:, k, unit_cols(n)], tk.lo[:, k, unit_cols(n)],
                                               k == 0, k == KB - 1)
                        mm.then_inc(unit_done, 1)

        @block.vector
        def _(dve):
            for k in range(KB):
                dve.wait_ge(hi_done, k + 1)
                nc.vector.tensor_tensor(tk.lo[:, k], x[:, k], tk.hi[:, k].bitcast(F32),
                                        ALU.subtract).then_inc(lo_done, 1)
            dve.wait_ge(x_in, 16)
            with dve.Fori(0, KB // 2) as t:
                for b in range(2):
                    for n in range(NU):
                        dve.wait_ge(unit_done, t * 6 + (6 + 3 * b + n + 1))
                        cols = x[:, bass.ds(t * 2 + b, 1), unit_cols(n)].rearrange("p a t -> p (a t)")
                        nc.vector.tensor_tensor(cols, cols, ps[:, 3 * b + n, 0:UNIT],
                                                ALU.add).then_inc(added, 1)


def gdn_phase(nc, tk, a):
    ps = tk.ps
    B = 4
    U = B * NU
    w_in = a["gdn_w_in"][0].rearrange("(k p) f -> p k f", p=P)
    section = (3 * D, 0, D, 2 * D)
    NQ = 5
    with ExitStack() as ctx:
        sem = semaphores(nc, ctx, "gdn", again=True)
        buf = lambda s, *a: ctx.enter_context(nc.sbuf_tensor(f"gdn_{s}", *a))
        ws = WeightStream(nc, tk, ctx, sem, "gdn", 2)
        gates = buf("gates", [P, NQ + 1, TILES, HEADS], F32)
        conv_w = buf("conv_w", [P, TAPS * 3, HEADS], F32)
        hist = buf("hist", [P, HIST * 3, HEADS], F32)
        tails = buf("tails", [P, 2, HIST * 3, HEADS], F32)
        tail_rows = buf("tail_rows", [P, 2, P], F32)
        R = HIST * 3 * HEADS
        tails_turned, tails_copied, tails_out = sem("tails_turned"), sem("tails_copied"), sem("tails_out")
        gain = buf("gain", [P, 1], F32)
        raw = buf("raw", [P, 3, PROMPT + 2 * HIST + SAMPLE], F32)
        qkv = buf("qkv", [P, 3, CPAD], F32)
        hw = buf("head_conv_w", [P, TAPS * 3], F32)
        hg = buf("head_gates", [P, NQ + 1, TILES], F32)
        sq = buf("sq", [P, 2, CU], F32)
        rs = buf("rs", [P, 2, CU], F32)
        gam = buf("gam", [P, BATCHES, P], F32)
        exp_d = buf("exp_d", [P, BATCHES, P], F32)
        mt = buf("mt", [P, BATCHES, P], F32)
        mt_l = buf("mt_level", [P, 2, BATCHES, P], F32)
        wz = buf("wz", [P, BATCHES, P], F32)
        z = buf("z", [P, 2, BATCHES, 2, P], F32)
        att = buf("att", [P, 2, BATCHES, P], F32)
        qd = buf("qd", [P, 2, BATCHES, P], F32)
        k_tail = buf("k_tail", [P, 2, BATCHES, P], F32)
        v_tok = buf("v_tok", [P, 2, BATCHES, P], F32)
        y = buf("y", [P, P], F32)
        v_new = buf("v_new", [P, P], F32)
        state = buf("state", [P, 2, DV], F32)

        gdn_prologue(nc, tk, a, w_in, ws, gates, conv_w, hist, gain, raw, qkv)
        unit_done, evacuated = sem("unit_done"), sem("evacuated")
        conv_done, silu_done = sem("conv_done"), sem("silu_done")
        cols_done = sem("cols_done")
        conv_steps = sem("conv_steps")
        sq_done, ss_done, ln_done, rs_done, unit_len = (sem("sq_done"), sem("ss_done"), sem("ln_done"),
                                                        sem("rs_done"), sem("unit_len_done"))
        prep_done, expd_done, e_done, gam_done = sem("prep_done"), sem("expd_done"), sem("e_done"), sem("gam_done")
        made = sem("att_mt_qd_done")
        tok_done = sem("tok_done")
        level_masked, z_done = sem("level_masked"), sem("z_done")
        wz_done, wz_copied, pz_done = sem("wz_done"), sem("wz_copied"), sem("pz_done")
        chain, y_done, vn_done, o_done, s_done = (sem("chain"), sem("y_done"), sem("vn_done"), sem("o_done"),
                                                  sem("s_done"))
        s_in, s_out, s_init = sem("state_landed"), sem("state_stored"), sem("state_zeroed")
        o_normed, final_done = sem("o_normed"), sem("final_done")
        block = ctx.enter_context(nc.Block())

        def head_weights(t, b):
            return w_in[:, :, bass.ds(t * P + section[b], P)]

        @block.sync
        def _(sp):
            def states(t):
                sp.wait_ge(s_out, t * 32)
                sp.sem_inc(ws.checked, 1)
                sp.dma_start(state[:, 1], a["state_gdn_S"][0, 0, t]).then_inc(s_in, 16)

            def store(t):
                sp.wait_ge(s_done, t * 9 + 9)
                sp.sem_inc(ws.checked, 1)
                sp.dma_start(a["p_S"][0, 0, t], state[:, 0]).then_inc(s_out, 16)
                sp.dma_start(a["s_S"][0, 0, t], state[:, 1]).then_inc(s_out, 16)

            for b in range(B):
                ws.load(sp, b, b % 2, head_weights(0, b))
            states(0)
            with sp.Fori(0, HEADS - 1) as t:
                for b in range(B):
                    ws.load(sp, t * B + (B + b), b % 2, head_weights(t + 1, b))
                store(t)
                states(t + 1)
            store(HEADS - 1)
            for g, dst in enumerate((a["p_conv"], a["s_conv"])):
                sp.wait_ge(tails_copied, g + 1)
                sp.dma_start(dst[0, 0].rearrange("f (r c) -> (f r) c", c=P), tail_rows[0:R, g]).then_inc(tails_out, 16)
            sp.wait_ge(s_out, HEADS * 32)
            sp.wait_ge(tails_out, 32)

        @block.gpsimd
        def _(pool):
            ws.start(pool)
            pool.sem_inc(evacuated, 2)

            def weights(t, b, first):
                if not (first and b < 2):
                    pool.wait_ge(unit_done, t * U + NU * (b - 1))
                ws.split(pool, t * B + b, b % 2, t * 32 + (b // 2 * 16 + 16), b % 2)

            def mask(t, r, l):
                i = r * LEVELS + l
                pool.wait_ge(made, t * 9 + 3 * r + 3)
                if r > 0 or l >= 2:
                    pool.wait_ge(wz_done, t * 21 + (i - 1))
                nc.gpsimd.tensor_tensor(mt_l[:, i % 2], mt[:],
                                        tk.joins[:, l][:, None, :].to_broadcast([P, BATCHES, P]),
                                        ALU.mult).then_inc(level_masked, 1)

            for b in range(B):
                weights(0, b, True)

            def head(t, more):
                if more:
                    weights(t + 1, 0, False)
                    weights(t + 1, 1, False)
                for r in range(BATCHES):
                    for l in range(LEVELS):
                        mask(t, r, l)
                        if more and (r, l) in ((0, 3), (1, 4)):
                            weights(t + 1, 2 + r, False)

            with pool.Fori(0, HEADS - 1) as t:
                head(t, True)
            head(HEADS - 1, False)

        @block.tensor
        def _(pe):
            def piece(t, n, only_third=None):
                u, third = n // 3, n % 3
                b, cols = u // NU, unit_cols(u % NU)
                if n % 9 == 0:
                    ws.wait_ready(pe, t * B + b)
                if third == 0:
                    pe.wait_ge(evacuated, t * U + (u + 1))
                for k in range(3 * third, min(3 * third + 3, KB)):
                    mm = split_product(pe, ps[:, u % 2, 0:UNIT], ws.hi[:, b % 2, k], ws.lo[:, b % 2, k],
                                       tk.hi[:, k, cols], tk.lo[:, k, cols], k == 0, k == KB - 1)
                if third == 2:
                    mm.then_inc(unit_done, 1)

            def sums(t, i):
                pe.wait_ge(sq_done, t * 9 + (i + 1))
                if i >= 2:
                    pe.wait_ge(ln_done, t * 9 + (i - 1))
                pe.matmul(ps[:, 2 + i % 2, 0:CU], tk.ones[:], sq[:, i % 2], start=True, stop=True).then_inc(ss_done, 1)

            def prepare(t, r):
                if r > 0:
                    pe.wait_ge(tok_done, t * 6 + 2 * r)
                    pe.wait_ge(z_done, t * 24 + 8 * r)
                for i in range(BATCHES):
                    mm = pe.matmul(ps[:, 2, i * P:(i + 1) * P],
                                   hg[:, NQ, 3 * r + i:3 * r + i + 1].to_broadcast([P, P]), tk.upto[:],
                                   start=True, stop=True)
                mm.then_inc(prep_done, 1)
                for bank, ch in ((3, 1), (4, 0)):
                    for i in range(BATCHES):
                        cols = tile_cols(3 * r + i)
                        mm = pe.matmul(ps[:, bank, i * P:(i + 1) * P], qkv[:, 1, cols], qkv[:, ch, cols],
                                       start=True, stop=True)
                    mm.then_inc(prep_done, 1)
                for i in range(BATCHES):
                    mm = pe.transpose(ps[:, 5, i * P:(i + 1) * P], qkv[:, 1, tile_cols(3 * r + i)], tk.ident[:])
                mm.then_inc(prep_done, 1)
                pe.wait_ge(expd_done, t * 3 + (r + 1))
                pe.wait_ge(e_done, t * 3 + (r + 1))
                for i in range(BATCHES):
                    mm = pe.transpose(ps[:, 2, i * P:(i + 1) * P], qkv[:, 2, tile_cols(3 * r + i)], tk.ident[:])
                mm.then_inc(prep_done, 1)

            def join_w(t, r, l):
                par, i = r % 2, r * LEVELS + l
                pe.wait_ge(level_masked, t * 21 + (i + 1))
                pe.wait_ge(z_done, t * 24 + (r * 8 + l + 1))
                if l == 0:
                    pe.wait_ge(made, t * 9 + (3 * r + 3))
                for i in range(BATCHES):
                    mm = pe.matmul(ps[:, 3, i * P:(i + 1) * P], mt_l[:, (r * LEVELS + l) % 2, i], z[:, par, i, 0],
                                   start=True, stop=True)
                mm.then_inc(wz_done, 1)

            def join_z(t, r, l):
                par, i = r % 2, r * LEVELS + l
                pe.wait_ge(wz_copied, t * 21 + (i + 1))
                if l == 0:
                    pe.wait_ge(tok_done, t * 6 + (2 * r + 2))
                for i in range(BATCHES):
                    at = (4 + i // 2, i % 2 * 256)
                    pe.matmul(ps[:, at[0], at[1]:at[1] + P], z[:, par, i, 1], wz[:, i], start=True, stop=True)
                    mm = pe.matmul(ps[:, at[0], at[1] + P:at[1] + 2 * P], wz[:, i], z[:, par, i, 1],
                                   start=True, stop=True)
                mm.then_inc(pz_done, 1)

            def chain_step(t, r, s):
                par, i = r % 2, s // 3
                c = 3 * r + i
                g = c // 8
                if s % 3 == 0:
                    if c == 0:
                        pe.wait_ge(s_init, t + 1)
                    elif c < 8:
                        pe.wait_ge(s_done, t * 9 + c)
                    else:
                        pe.wait_ge(s_in, t * 16 + 16)
                        pe.wait_ge(s_done, t * 9 + c)
                    pe.matmul(ps[:, 6, 0:P], qkv[:, 1, tile_cols(c)], state[:, g],
                              start=True, stop=True).then_inc(chain, 1)
                elif s % 3 == 1:
                    pe.wait_ge(y_done, t * 9 + (c + 1))
                    pe.matmul(ps[:, 6, P:2 * P], z[:, par, i, 1], y[:], start=True, stop=True).then_inc(chain, 1)
                else:
                    if c >= 1:
                        pe.wait_ge(o_done, t * 9 + c)
                    pe.matmul(ps[:, 7, 0:P], state[:, g], qd[:, par, i], start=True, stop=False)
                    pe.wait_ge(vn_done, t * 9 + (c + 1))
                    pe.matmul(ps[:, 7, 0:P], v_new[:], att[:, par, i], start=False, stop=True)
                    pe.matmul(ps[:, 6, 2 * P:3 * P], k_tail[:, par, i], v_new[:],
                              start=True, stop=True).then_inc(chain, 1)

            def head(t, more):
                for n in range(9):
                    if more:
                        piece(t + 1, n)
                for i in range(6):
                    sums(t, i)
                pe.wait_ge(cols_done, t + 1)
                pe.wait_ge(unit_len, t * 6 + 6)
                pe.wait_ge(silu_done, t * 3 + 3)
                n = 9
                for r in range(BATCHES + 1):
                    if r < BATCHES:
                        prepare(t, r)
                    for l in range(LEVELS):
                        if r < BATCHES:
                            join_w(t, r, l)
                        if more and n < 36:
                            piece(t + 1, n)
                            n += 1
                        if r > 0 and 2 * l < 9:
                            chain_step(t, r - 1, 2 * l)
                        if r < BATCHES:
                            join_z(t, r, l)
                        if r > 0 and 2 * l + 1 < 9:
                            chain_step(t, r - 1, 2 * l + 1)
                for i in range(6, 9):
                    sums(t, i)

            for n in range(36):
                piece(0, n)
            with pe.Fori(0, HEADS - 1) as t:
                head(t, True)
            head(HEADS - 1, False)
            pe.wait_ge(cols_done, HEADS * 11)
            for g in range(2):
                pe.transpose(ps[0:R, g, 0:P], tails[:, g].rearrange("p f h -> p (f h)"), tk.ident[:]).then_inc(tails_turned, 1)

        @block.scalar
        def _(act):
            def evacuate(t, u, first):
                act.wait_ge(unit_done, t * U + (u + 1))
                b, n = u // NU, u % NU
                src = ps[:, u % 2, 0:UNIT]
                if b == 0:
                    dst = tk.x[:, bass.ds(t, 1), unit_cols(n)].rearrange("p a t -> p (a t)")
                    act.wait_ge(evacuated, 2)
                    nc.scalar.activation(dst, src, ACT.Silu).then_inc(evacuated, 1)
                    return
                if not first:
                    act.wait_ge(conv_done, (t - 1) * 3 + b)
                start = HIST + n * UNIT
                if n < NU - 1:
                    nc.scalar.copy(raw[:, b - 1, start:start + UNIT], src).then_inc(evacuated, 1)
                else:
                    cut = PROMPT - n * UNIT
                    nc.scalar.copy(raw[:, b - 1, start:start + cut], src[:, 0:cut])
                    nc.scalar.copy(raw[:, b - 1, PROMPT + 2 * HIST:], src[:, cut:]).then_inc(evacuated, 1)

            def rsqrt(t, i):
                act.wait_ge(ss_done, t * 9 + (i + 1))
                if i >= 2:
                    act.wait_ge(unit_len, t * 6 + (i - 1)) if i < 8 else act.wait_ge(final_done, t * 3 + 1)
                src, dst = ps[:, 2 + i % 2, 0:CU], rs[:, i % 2]
                nc.scalar.activation(dst, src, ACT.Ln, bias=tk.eps[:, 0:1],
                                     scale=1.0 if i < 6 else 1.0 / DV).then_inc(ln_done, 1)
                act.wait_ge(ln_done, t * 9 + (i + 1))
                if i < 3:
                    nc.scalar.activation(dst, dst, ACT.Exp, scale=-0.5, bias=tk.log_dk[:, 0:1]).then_inc(rs_done, 1)
                else:
                    nc.scalar.activation(dst, dst, ACT.Exp, scale=-0.5).then_inc(rs_done, 1)

            def square(t, i):
                ch, n = (i // 3) % 2, i % 3
                if i >= 2:
                    act.wait_ge(ss_done, t * 9 + (i - 1))
                nc.scalar.activation(sq[:, i % 2], qkv[:, ch if i < 6 else 0, n * CU:(n + 1) * CU],
                                     ACT.Square).then_inc(sq_done, 1)

            def prepare(t, r):
                act.wait_ge(prep_done, t * 15 + (5 * r + 1))
                if r > 0:
                    act.wait_ge(made, t * 9 + 3 * r)
                if r == 2:
                    act.wait_ge(chain, t * 27 + 9)
                    act.wait_ge(y_done, t * 9 + 3)
                d = ps[:, 2, 0:3 * P].rearrange("p (i c) -> p i c", i=3)
                nc.scalar.activation(exp_d[:], d, ACT.Exp).then_inc(expd_done, 1)
                act.wait_ge(e_done, t * 3 + (r + 1))
                nc.scalar.activation(gam[:], gam[:], ACT.Exp).then_inc(gam_done, 1)
                act.wait_ge(prep_done, t * 15 + (5 * r + 4))
                par = r % 2
                for i in range(BATCHES):
                    op = nc.scalar.mul(k_tail[:, par, i], ps[:, 5, i * P:(i + 1) * P],
                                       hg[:, 3, 3 * r + i:3 * r + i + 1])
                op.then_inc(tok_done, 1)
                act.wait_ge(prep_done, t * 15 + (5 * r + 5))
                nc.scalar.copy(v_tok[:, par], ps[:, 2, 0:3 * P].rearrange("p (i c) -> p i c", i=3)).then_inc(tok_done, 1)

            def copy_w(t, r, l):
                i = r * LEVELS + l
                act.wait_ge(wz_done, t * 21 + (i + 1))
                nc.scalar.copy(wz[:], ps[:, 3, 0:3 * P].rearrange("p (i c) -> p i c", i=3)).then_inc(wz_copied, 1)

            def chain_step(t, r, s):
                c = 3 * r + s // 3
                if s % 3 == 1:
                    act.wait_ge(chain, t * 27 + (3 * c + 2))
                    nc.scalar.copy(v_new[:], ps[:, 6, P:2 * P]).then_inc(vn_done, 1)
                elif s % 3 == 2:
                    act.wait_ge(chain, t * 27 + (3 * c + 3))
                    w = P if c < 8 else SAMPLE
                    start = tile_cols(c).start
                    nc.scalar.copy(qkv[:, 0, start:start + w], ps[:, 7, 0:w]).then_inc(o_done, 1)

            def head(t, more):
                for ch in range(3):
                    act.wait_ge(conv_done, t * 3 + (ch + 1))
                    nc.scalar.activation(qkv[:, ch, 0:CW], qkv[:, ch, 0:CW], ACT.Silu).then_inc(silu_done, 1)
                    if more:
                        evacuate(t + 1, ch, False)
                nc.scalar.preload_act_table_set("natural_log_exp_and_others")
                for i in range(6):
                    if i == 0:
                        act.wait_ge(silu_done, t * 3 + 3)
                    square(t, i)
                    if i >= 1:
                        rsqrt(t, i - 1)
                rsqrt(t, 5)
                n = 9
                for r in range(BATCHES + 1):
                    if r < BATCHES:
                        prepare(t, r)
                    for l in range(LEVELS):
                        if r < BATCHES:
                            copy_w(t, r, l)
                        if more and n < 36:
                            if n % 3 == 2:
                                evacuate(t + 1, n // 3, False)
                            n += 1
                        if r > 0 and 2 * l < 9:
                            chain_step(t, r - 1, 2 * l)
                        if r > 0 and 2 * l + 1 < 9:
                            chain_step(t, r - 1, 2 * l + 1)
                act.wait_ge(o_done, t * 9 + 9)
                for i in range(6, 9):
                    square(t, i)
                    if i >= 7:
                        rsqrt(t, i - 1)
                rsqrt(t, 8)

            for u in range(U):
                evacuate(0, u, True)
            with act.Fori(0, HEADS - 1) as t:
                head(t, True)
            head(HEADS - 1, False)

        @block.vector
        def _(dve):
            def take(dst, src):
                return nc.vector.tensor_scalar(dst, src, 1.0, None, ALU.mult)

            def convolve(t, ch):
                dve.wait_ge(evacuated, t * U + (2 + NU * (ch + 2)))
                src = hist[:, :, bass.ds(t, 1)].rearrange("p (f c) a -> p c (f a)", c=3)[:, ch]
                take(raw[:, ch, GCOL:GCOL + HIST], src).then_inc(cols_done, 1)
                for g, start in ((0, PROMPT), (1, PROMPT + HIST + SAMPLE)):
                    dst = tails[:, g, :, bass.ds(t, 1)].rearrange("p (f c) a -> p c (f a)", c=3)[:, ch]
                    take(dst, raw[:, ch, start:start + HIST]).then_inc(cols_done, 1)
                dve.wait_ge(cols_done, t * 11 + (2 + 3 * (ch + 1)))
                out = qkv[:, ch, 0:CW]
                nc.vector.tensor_scalar(out, raw[:, ch, 0:CW], hw[:, ch:ch + 1], None,
                                        ALU.mult).then_inc(conv_steps, 1)
                for tap in range(1, TAPS):
                    dve.wait_ge(conv_steps, t * 9 + (3 * ch + tap))
                    nc.vector.scalar_tensor_tensor(
                        out=out, in0=raw[:, ch, tap:tap + CW], scalar=hw[:, tap * 3 + ch:tap * 3 + ch + 1],
                        in1=out, op0=ALU.mult, op1=ALU.add).then_inc(conv_done if tap == TAPS - 1 else conv_steps, 1)

            def prepare(t, r):
                par = r % 2
                dve.wait_ge(prep_done, t * 15 + (5 * r + 1))
                dve.wait_ge(expd_done, t * 3 + (r + 1))
                for i in range(BATCHES):
                    c = 3 * r + i
                    op = nc.vector.scalar_tensor_tensor(out=gam[:, i], in0=ps[:, 2, i * P:(i + 1) * P],
                                                        scalar=hg[:, 1, c:c + 1], in1=tk.later_neg[:],
                                                        op0=ALU.subtract, op1=ALU.add)
                op.then_inc(e_done, 1)
                if r == 2:
                    dve.wait_ge(chain, t * 27 + 9)
                for i in range(BATCHES):
                    c = 3 * r + i
                    op = nc.vector.tensor_scalar(z[:, par, i], tk.ident[:][:, None, :].to_broadcast([P, 2, P]),
                                                 hg[:, 0, c:c + 1], None, ALU.mult)
                op.then_inc(z_done, 1)
                dve.wait_ge(gam_done, t * 3 + (r + 1))
                dve.wait_ge(prep_done, t * 15 + (5 * r + 3))
                if r > 0:
                    dve.wait_ge(level_masked, t * 21 + 7 * r)
                grid = lambda bank: ps[:, bank, 0:3 * P].rearrange("p (i c) -> p i c", i=3)
                nc.vector.tensor_tensor(mt[:], grid(3), gam[:], ALU.mult).then_inc(made, 1)
                nc.vector.tensor_tensor(att[:, par], grid(4), gam[:], ALU.mult).then_inc(made, 1)
                if r < 2:
                    op = nc.vector.tensor_tensor(qd[:, par].rearrange("p i c -> p (i c)"),
                                                 qkv[:, 0, 3 * r * P:(3 * r + 3) * P],
                                                 exp_d[:].rearrange("p i c -> p (i c)"), ALU.mult)
                else:
                    for i in range(BATCHES):
                        op = nc.vector.tensor_tensor(qd[:, par, i], qkv[:, 0, tile_cols(3 * r + i)], exp_d[:, i], ALU.mult)
                op.then_inc(made, 1)

            def join(t, r, l):
                par, i = r % 2, r * LEVELS + l
                dve.wait_ge(pz_done, t * 21 + (i + 1))
                dve.wait_ge(z_done, t * 24 + (8 * r + l + 1))
                z01 = z[:, par, 0:2].rearrange("p i h c -> p (i h c)")
                z2 = z[:, par, 2].rearrange("p h c -> p (h c)")
                nc.vector.tensor_tensor(z01, z01, ps[:, 4], ALU.subtract)
                nc.vector.tensor_tensor(z2, z2, ps[:, 5, 0:2 * P], ALU.subtract).then_inc(z_done, 1)

            def chain_step(t, r, s):
                par, i = r % 2, s // 3
                c = 3 * r + i
                g = c // 8
                if s % 3 == 0:
                    dve.wait_ge(chain, t * 27 + (3 * c + 1))
                    dve.wait_ge(tok_done, t * 6 + (2 * r + 2))
                    nc.vector.scalar_tensor_tensor(out=y[:], in0=ps[:, 6, 0:P], scalar=hg[:, 2, c:c + 1],
                                                   in1=v_tok[:, par, i], op0=ALU.mult, op1=ALU.add).then_inc(y_done, 1)
                elif s % 3 == 2:
                    dve.wait_ge(chain, t * 27 + (3 * c + 3))
                    dve.wait_ge(s_done, t * 9 + c) if c else dve.wait_ge(s_init, t + 1)
                    nc.vector.scalar_tensor_tensor(out=state[:, g], in0=state[:, g], scalar=hg[:, 4, c:c + 1],
                                                   in1=ps[:, 6, 2 * P:3 * P], op0=ALU.mult, op1=ALU.add).then_inc(s_done, 1)

            def head(t):
                dve.wait_ge(prep_done, t * 15)
                dve.wait_ge(tok_done, t * 6)
                dve.wait_ge(chain, t * 27)
                dve.wait_ge(sq_done, t * 9)
                dve.wait_ge(final_done, t * 3)
                take(hw[:], conv_w[:, :, bass.ds(t, 1)].rearrange("p k a -> p (k a)")).then_inc(cols_done, 1)
                take(hg[:].rearrange("p q c -> p (q c)"),
                                      gates[:, :, :, bass.ds(t, 1)].rearrange("p q c a -> p (q c a)")).then_inc(cols_done, 1)
                dve.wait_ge(s_out, t * 32)
                nc.vector.memset(state[:, 0], 0.0).then_inc(s_init, 1)
                for ch in range(3):
                    convolve(t, ch)
                for i in range(6):
                    cols = qkv[:, i // 3, i % 3 * CU:(i % 3 + 1) * CU]
                    dve.wait_ge(rs_done, t * 9 + (i + 1))
                    nc.vector.tensor_tensor(cols, cols, rs[:, i % 2], ALU.mult).then_inc(unit_len, 1)
                dve.wait_ge(unit_len, t * 6 + 6)
                for r in range(BATCHES + 1):
                    if r < BATCHES:
                        prepare(t, r)
                    for l in range(LEVELS):
                        if r > 0 and 2 * l < 9:
                            chain_step(t, r - 1, 2 * l)
                        if r < BATCHES:
                            join(t, r, l)
                        if r > 0 and 2 * l + 1 < 9:
                            chain_step(t, r - 1, 2 * l + 1)
                for n in range(NU):
                    dve.wait_ge(rs_done, t * 9 + (7 + n))
                    cols = qkv[:, 0, n * CU:(n + 1) * CU]
                    nc.vector.scalar_tensor_tensor(out=cols, in0=cols, scalar=gain[:, 0:1], in1=rs[:, n % 2],
                                                   op0=ALU.mult, op1=ALU.mult).then_inc(o_normed, 1)
                    dve.wait_ge(o_normed, t * 3 + (n + 1))
                    parts = [(n * CU, min((n + 1) * CU, PROMPT), n * CU)]
                    if n == NU - 1:
                        parts.append((GCOL, CW, PROMPT))
                    for start, end, to in parts:
                        dst = tk.x[:, bass.ds(t, 1), to:to + end - start].rearrange("p a t -> p (a t)")
                        op = nc.vector.tensor_tensor(dst, dst, qkv[:, 0, start:end], ALU.mult)
                    op.then_inc(final_done, 1)

            with dve.Fori(0, HEADS) as t:
                head(t)

            for g in range(2):
                dve.wait_ge(tails_turned, g + 1)
                nc.vector.tensor_copy(tail_rows[0:R, g], ps[0:R, g, 0:P]).then_inc(tails_copied, 1)


def gdn_prologue(nc, tk, a, w_in, ws, gates, conv_w, hist, gain, raw, qkv):
    ps = tk.ps
    R, RH = TAPS * 3 * HEADS, HIST * 3 * HEADS
    with ExitStack() as ctx:
        sem = semaphores(nc, ctx, "gdnp")
        buf = lambda s, *sh: ctx.enter_context(nc.sbuf_tensor(f"gdnp_{s}", *sh))
        rows = buf("rows", [P, 2, P], F32)
        ab_t = buf("ab_t", [2 * HEADS, TILES * P], F32)
        ab = buf("ab", [P, TILES, 2 * HEADS], F32)
        rate = buf("rate", [P, HEADS], F32)
        dtb = buf("dtb", [P, HEADS], F32)
        tmp = buf("tmp", [P, 4, TILES, HEADS], F32)
        small_in, w_landed = sem("small_in"), sem("w_landed")
        zeroed, w_hi, w_split = sem("zeroed"), sem("w_hi"), sem("w_split")
        turned, copied, ab_done, ab_copied = sem("turned"), sem("copied"), sem("ab_done"), sem("ab_copied")
        step = sem("gate_steps")
        H = HEADS
        block = ctx.enter_context(nc.Block())

        @block.sync
        def _(sp):
            sp.wait_ge(zeroed, 5)
            sp.dma_start(ws.stage[:, 0, :, 0:2 * H], w_in[:, :, 4 * D:4 * D + 2 * H]).then_inc(w_landed, 16)
            sp.dma_start(rows[0:R, 0], a["gdn_conv_w"][0].rearrange("f (r c) -> (f r) c", c=P)).then_inc(small_in, 16)
            sp.dma_start(rows[0:RH, 1], a["state_gdn_conv"][0, 0].rearrange("f (r c) -> (f r) c", c=P)).then_inc(small_in, 16)
            sp.dma_start(gain[:], a["gdn_norm"].rearrange("a p -> p a"), allow_slow_non_contiguous=True).then_inc(small_in, 16)
            sp.dma_start(rate[:], a["gdn_a_log"].to_broadcast([P, H])).then_inc(small_in, 16)
            sp.dma_start(dtb[:], a["gdn_dt_bias"].to_broadcast([P, H])).then_inc(small_in, 16)
            sp.wait_ge(small_in, 80)

        @block.gpsimd
        def _(pool):
            nc.gpsimd.memset(raw[:, :, 0:HIST], 0.0).then_inc(zeroed, 1)
            nc.gpsimd.memset(qkv[:, :, CW:CPAD], 0.0).then_inc(zeroed, 1)
            nc.gpsimd.memset(ab_t[:, TOK:TILES * P], -80.0).then_inc(zeroed, 1)
            nc.gpsimd.memset(ws.hi[:, 0].bitcast(F32), 0.0).then_inc(zeroed, 1)
            nc.gpsimd.memset(ws.lo[:, 0].bitcast(F32), 0.0).then_inc(zeroed, 1)
            pool.wait_ge(zeroed, 5)
            pool.wait_ge(w_landed, 16)
            st = ws.stage[:, 0, :, 0:2 * H]
            nc.gpsimd.tensor_tensor(ws.hi[:, 0, :, 0:2 * H], st,
                                    tk.one[:][:, :, None].to_broadcast([P, KB, 2 * H]), ALU.mult).then_inc(w_hi, 1)
            pool.wait_ge(w_hi, 1)
            nc.gpsimd.tensor_tensor(ws.lo[:, 0, :, 0:2 * H], st, ws.hi[:, 0, :, 0:2 * H].bitcast(F32),
                                    ALU.subtract).then_inc(w_split, 1)

        @block.tensor
        def _(pe):
            pe.wait_ge(small_in, 80)
            pe.transpose(ps[:, 4, 0:R], rows[0:R, 0], tk.ident[0:R, 0:R]).then_inc(turned, 1)
            pe.transpose(ps[:, 5, 0:RH], rows[0:RH, 1], tk.ident[0:RH, 0:RH]).then_inc(turned, 1)
            pe.wait_ge(w_split, 1)
            for n in range(NU):
                for k in range(KB):
                    mm = split_product(pe, ps[:, n, 0:UNIT], ws.hi[:, 0, k], ws.lo[:, 0, k],
                                       tk.hi[:, k, unit_cols(n)], tk.lo[:, k, unit_cols(n)], k == 0, k == KB - 1)
                mm.then_inc(ab_done, 1)
            pe.wait_ge(ab_copied, NU)
            pe.wait_ge(zeroed, 5)
            for c in range(TILES):
                mm = pe.transpose(ps[:, 3, c * 2 * H:(c + 1) * 2 * H], ab_t[:, c * P:(c + 1) * P],
                                  tk.ident[0:2 * H, 0:2 * H])
            mm.then_inc(step, 1)
            pe.wait_ge(step, 15)
            g = gates[:, 5].rearrange("p c h -> p (c h)")
            pe.matmul(ps[:, 6, 0:TILES * H], tk.upto[:], g, start=True, stop=True)
            pe.matmul(ps[:, 7, 0:TILES * H], tk.ones[:], g, start=True, stop=True).then_inc(step, 1)

        @block.scalar
        def _(act):
            def do(n, *args, **kw):
                if n == 5:
                    nc.scalar.preload_act_table_set("natural_log_exp_and_others")
                act.wait_ge(step, n - 1)
                nc.scalar.activation(*args, **kw).then_inc(step, 1)
            do(5, tmp[:, 1], tmp[:, 1], ACT.Exp)
            do(6, tmp[:, 1], tmp[:, 1], ACT.Ln, bias=tk.one[:, 0:1])
            do(8, rate[:], rate[:], ACT.Exp)
            do(11, tmp[:, 2], ab[:, :, H:2 * H], ACT.Exp, scale=-1.0)
            do(19, tmp[:, 0], gates[:, 1], ACT.Exp)
            do(20, gates[:, 3], gates[:, 3], ACT.Exp)
            do(22, gates[:, 4], ps[:, 7, 0:TILES * H].rearrange("p (c h) -> p c h", c=TILES), ACT.Exp)

        @block.vector
        def _(dve):
            def after(n):
                dve.wait_ge(step, n - 1)
            dve.wait_ge(turned, 2)
            nc.vector.tensor_copy(conv_w[:].rearrange("p f h -> p (f h)"), ps[:, 4, 0:R]).then_inc(copied, 1)
            nc.vector.tensor_copy(hist[:].rearrange("p f h -> p (f h)"), ps[:, 5, 0:RH]).then_inc(copied, 1)
            for n in range(NU):
                dve.wait_ge(ab_done, n + 1)
                nc.vector.tensor_copy(ab_t[:, unit_cols(n)], ps[0:2 * H, n, 0:UNIT]).then_inc(ab_copied, 1)
            dve.wait_ge(small_in, 80)
            after(2)
            nc.vector.tensor_copy(ab[:].rearrange("p c h -> p (c h)"), ps[:, 3, 0:TILES * 2 * H]).then_inc(step, 1)
            after(3)
            nc.vector.tensor_tensor(tmp[:, 0], ab[:, :, 0:H], dtb[:][:, None, :].to_broadcast([P, TILES, H]),
                                    ALU.add).then_inc(step, 1)
            after(4)
            nc.vector.tensor_scalar(tmp[:, 3], tmp[:, 0], 0.0, None, ALU.max).then_inc(copied, 1)
            dve.wait_ge(copied, 3)
            nc.vector.scalar_tensor_tensor(out=tmp[:, 1], in0=tmp[:, 3], scalar=-2.0, in1=tmp[:, 0],
                                           op0=ALU.mult, op1=ALU.add).then_inc(step, 1)
            after(7)
            nc.vector.tensor_tensor(tmp[:, 0], tmp[:, 3], tmp[:, 1], ALU.add).then_inc(step, 1)
            after(9)
            nc.vector.scalar_tensor_tensor(out=gates[:, 5], in0=tmp[:, 0], scalar=-1.0,
                                           in1=rate[:][:, None, :].to_broadcast([P, TILES, H]),
                                           op0=ALU.mult, op1=ALU.mult).then_inc(step, 1)
            after(10)
            nc.vector.tensor_scalar(gates[:, 5, TILES - 1], gates[:, 5, TILES - 1],
                                    tk.upto[:, SAMPLE - 1:SAMPLE], None, ALU.mult).then_inc(step, 1)
            after(12)
            nc.vector.tensor_scalar(tmp[:, 3], tmp[:, 2], 1.0, None, ALU.add).then_inc(step, 1)
            after(13)
            nc.vector.reciprocal(gates[:, 0], tmp[:, 3]).then_inc(step, 1)
            after(14)
            nc.vector.tensor_scalar(gates[:, 0, TILES - 1], gates[:, 0, TILES - 1],
                                    tk.upto[:, SAMPLE - 1:SAMPLE], None, ALU.mult).then_inc(step, 2)
            after(17)
            nc.vector.tensor_copy(gates[:, 1].rearrange("p c h -> p (c h)"), ps[:, 6, 0:TILES * H]).then_inc(step, 1)
            after(18)
            nc.vector.scalar_tensor_tensor(out=gates[:, 3].rearrange("p c h -> p (c h)"),
                                           in0=gates[:, 1].rearrange("p c h -> p (c h)"), scalar=-1.0,
                                           in1=ps[:, 7, 0:TILES * H], op0=ALU.mult, op1=ALU.add).then_inc(step, 1)
            after(21)
            nc.vector.tensor_scalar(gates[:, 2], tmp[:, 0], -1.0, None, ALU.mult).then_inc(step, 1)
            dve.wait_ge(step, 22)


def mlstm_phase(nc, tk, a):
    ps = tk.ps
    B = 3
    U = B * NU
    W_QK = HEADS * MDK
    w_in = a["ml_w_in"][0].rearrange("(k p) f -> p k f", p=P)
    NQ = 5
    with ExitStack() as ctx:
        sem = semaphores(nc, ctx, "ml")
        buf = lambda s, *sh: ctx.enter_context(nc.sbuf_tensor(f"ml_{s}", *sh))
        ws = WeightStream(nc, tk, ctx, sem, "ml", 3, stages=3)
        gates = buf("gates", [P, NQ + 1, TILES, HEADS], F32)
        gain = buf("gain", [P, HEADS], F32)
        m_end = buf("m_end", [P, 2, HEADS], F32)
        raw = buf("raw", [P, 3, TOK], F32)
        qkv = buf("qkv", [P, 3, TILES * P], F32)
        hg = buf("head_gates", [P, NQ + 1, TILES], F32)
        hgain = buf("head_gain", [P, 1], F32)
        num = buf("num", [P, TILES * P], F32)
        den = buf("den", [P, TILES * P], F32)
        sq = buf("sq", [P, 2, UNIT], F32)
        rs = buf("rs", [P, NU, UNIT], F32)
        pe_exp = buf("exponents", [P, BATCHES, P], F32)
        q_scale = buf("q_scale", [P, BATCHES, P], F32)
        floor = buf("floor", [P, 2, BATCHES, P], F32)
        pt = buf("pt", [P, 2, BATCHES, P], F32)
        qs = buf("qs", [MDK, 2, BATCHES, P], F32)
        kw = buf("kw", [P, 2, BATCHES, MDK], F32)
        v_tok = buf("v_tok", [P, 2, BATCHES, DV + 1], F32)
        state = buf("state", [MDK, 2, DV + 1], F32)

        mlstm_prologue(nc, tk, a, w_in, ws, gates, gain, m_end, qkv, v_tok, num[0:2 * HEADS])
        unit_done, evacuated = sem("unit_done"), sem("evacuated")
        taken, cols_done = sem("raw_taken"), sem("cols_done")
        prep_done, qsc_done, e_done, exp_done = sem("prep_done"), sem("q_scale_done"), sem("e_done"), sem("exp_done")
        floor_done, tok_done, made = sem("floor_done"), sem("tok_done"), sem("p_and_q_made")
        chain, num_done, den_done, s_done = sem("chain"), sem("num_done"), sem("den_done"), sem("s_done")
        s_in, s_out, s_init = sem("state_landed"), sem("state_stored"), sem("state_zeroed")
        sq_done, ss_done, v_done, ln_done, rs_done = (sem("sq_done"), sem("ss_done"), sem("v_done"), sem("ln_done"),
                                                      sem("rs_done"))
        negative_done, den2_done, clamped = sem("negative_done"), sem("den2_done"), sem("clamped")
        o_normed, final_done, m_out = sem("o_normed"), sem("final_done"), sem("m_stored")
        block = ctx.enter_context(nc.Block())

        @block.sync
        def _(sp):
            def weights(t, b):
                if b == 1:
                    ws.wait_stage(sp, t * B + 1)
                    for h in range(2):
                        sp.dma_start(ws.stage[:, 1, :, h * MDK:(h + 1) * MDK],
                                     w_in[:, :, bass.ds(t * MDK + h * W_QK, MDK)]).then_inc(ws.landed[1], 16)
                else:
                    start = 2 * W_QK + (D if b == 0 else 0)
                    ws.load(sp, t * B + b, b, w_in[:, :, bass.ds(t * P + start, P)])

            def states(t):
                sp.wait_ge(s_out, t * 64)
                sp.sem_inc(ws.checked, 1)
                sp.dma_start(state[:, 1, 0:DV], a["state_mlstm_C"][0, 0, t]).then_inc(s_in, 16)
                sp.dma_start(state[:, 1, DV:DV + 1], a["state_mlstm_n"][0, 0, t][:, None]).then_inc(s_in, 16)

            def store(t):
                sp.wait_ge(s_done, t * 9 + 9)
                sp.sem_inc(ws.checked, 1)
                for g, name in enumerate(("p", "s")):
                    sp.dma_start(a[f"{name}_C"][0, 0, t], state[:, g, 0:DV]).then_inc(s_out, 16)
                    sp.dma_start(a[f"{name}_n"][0, 0, t][:, None], state[:, g, DV:DV + 1]).then_inc(s_out, 16)

            for g, name in enumerate(("p", "s")):
                sp.dma_start(a[f"{name}_m"][0], m_end[0:1, g]).then_inc(m_out, 16)
            for b in range(B):
                weights(0, b)
            states(0)
            with sp.Fori(0, HEADS - 1) as t:
                for b in range(B):
                    weights(t + 1, b)
                store(t)
                states(t + 1)
            store(HEADS - 1)
            sp.wait_ge(s_out, HEADS * 64)
            sp.wait_ge(m_out, 32)

        @block.gpsimd
        def _(pool):
            ws.start(pool)
            pool.sem_inc(evacuated, 2)
            pool.sem_inc(unit_done, U)
            with pool.Fori(0, HEADS) as t:
                for b in range(B):
                    pool.wait_ge(unit_done, t * U + NU * (b + 1))
                    dmas = 32 if b == 1 else 16
                    ws.split(pool, t * B + b, b, t * dmas + dmas, b)

        @block.tensor
        def _(pe):
            def piece(t, n):
                u, third = n // 3, n % 3
                b, cols = u // NU, unit_cols(u % NU)
                if n % 9 == 0:
                    ws.wait_ready(pe, t * B + b)
                if third == 0:
                    pe.wait_ge(evacuated, t * U + max(u + 1, 2))
                for k in range(3 * third, min(3 * third + 3, KB)):
                    mm = split_product(pe, ps[:, u % 2, 0:UNIT], ws.hi[:, b, k], ws.lo[:, b, k],
                                       tk.hi[:, k, cols], tk.lo[:, k, cols], k == 0, k == KB - 1)
                if third == 2:
                    mm.then_inc(unit_done, 1)

            def rows_of(bank, q, r):
                for i in range(BATCHES):
                    c = 3 * r + i
                    mm = pe.matmul(ps[:, bank, i * P:(i + 1) * P], hg[:, q, c:c + 1].to_broadcast([P, P]),
                                   tk.ident[:], start=True, stop=True)
                mm.then_inc(prep_done, 1)

            def prepare(t, r):
                if r > 0:
                    pe.wait_ge(tok_done, t * 6 + 2 * r)
                rows_of(2, 1, r)
                if r > 0:
                    pe.wait_ge(made, t * 6 + 2 * r)
                for i in range(BATCHES):
                    cols = slice((3 * r + i) * P, (3 * r + i + 1) * P)
                    mm = pe.matmul(ps[:, 3, i * P:(i + 1) * P], qkv[0:MDK, 1, cols], qkv[0:MDK, 0, cols],
                                   start=True, stop=True)
                mm.then_inc(prep_done, 1)
                if r > 0:
                    pe.wait_ge(floor_done, t * 3 + r)
                rows_of(4, 2, r)
                for i in range(BATCHES):
                    mm = pe.transpose(ps[:, 5, i * MDK:(i + 1) * MDK], qkv[0:MDK, 1, (3 * r + i) * P:(3 * r + i + 1) * P],
                                      tk.ident[0:MDK, 0:MDK])
                mm.then_inc(prep_done, 1)
                pe.wait_ge(qsc_done, t * 3 + (r + 1))
                pe.wait_ge(e_done, t * 3 + (r + 1))
                for i in range(BATCHES):
                    mm = pe.transpose(ps[:, 2, i * P:(i + 1) * P], qkv[:, 2, (3 * r + i) * P:(3 * r + i + 1) * P], tk.ident[:])
                mm.then_inc(prep_done, 1)

            def chunk(t, r, i):
                par, c = r % 2, 3 * r + i
                g = c // 8
                if i == 0:
                    pe.wait_ge(made, t * 6 + (2 * r + 2))
                    pe.wait_ge(tok_done, t * 6 + (2 * r + 2))
                if c == 0:
                    pe.wait_ge(s_init, t + 1)
                else:
                    pe.wait_ge(s_done, t * 9 + c)
                    pe.wait_ge(num_done, t * 9 + c)
                if c == 8:
                    pe.wait_ge(s_in, t * 32 + 32)
                pe.matmul(ps[:, 6, 0:P], state[:, g, 0:DV], qs[:, par, i], start=True, stop=False)
                pe.matmul(ps[:, 6, 0:P], v_tok[:, par, i, 0:DV], pt[:, par, i], start=False, stop=True).then_inc(chain, 1)
                pe.matmul(ps[:, 7, 0:P], state[:, g, DV:DV + 1].to_broadcast([MDK, P]), qs[:, par, i],
                          start=True, stop=False)
                pe.matmul(ps[:, 7, 0:P], tk.ones[:], pt[:, par, i], start=False, stop=True)
                pe.matmul(ps[0:MDK, 7, P:2 * P + 1], kw[:, par, i], v_tok[:, par, i],
                          start=True, stop=True).then_inc(chain, 1)

            def sums(t, n):
                pe.wait_ge(sq_done, t * 3 + (n + 1))
                pe.matmul(ps[:, 2 + n, 0:UNIT], tk.ones[:], sq[:, n % 2], start=True, stop=True).then_inc(ss_done, 1)

            def head(t, more):
                for n in range(9):
                    if more:
                        piece(t + 1, n)
                pe.wait_ge(cols_done, t * 2 + 2)
                pe.wait_ge(taken, t * 3 + 3)
                n = 9
                for r in range(BATCHES + 1):
                    if r < BATCHES:
                        prepare(t, r)
                    for i in range(BATCHES):
                        for _ in range(2 if r in (0, 3) else 1):
                            if more and n < 27:
                                piece(t + 1, n)
                                n += 1
                        if r > 0:
                            chunk(t, r - 1, i)
                if more:
                    while n < 27:
                        piece(t + 1, n)
                        n += 1
                for n in range(NU):
                    sums(t, n)

            for n in range(27):
                piece(0, n)
            with pe.Fori(0, HEADS - 1) as t:
                head(t, True)
            head(HEADS - 1, False)

        @block.scalar
        def _(act):
            def evacuate(t, u, first):
                act.wait_ge(unit_done, t * U + (U + u + 1))
                b, n = u // NU, u % NU
                src = ps[:, u % 2, 0:UNIT]
                if b == 0:
                    dst = tk.x[:, bass.ds(t, 1), unit_cols(n)].rearrange("p a t -> p (a t)")
                    act.wait_ge(evacuated, 2)
                    nc.scalar.activation(dst, src, ACT.Sigmoid).then_inc(evacuated, 1)
                    return
                if not first:
                    act.wait_ge(taken, t * 3)
                if b == 1:
                    nc.scalar.copy(raw[0:MDK, 0, unit_cols(n)], src[0:MDK])
                    nc.scalar.copy(raw[0:MDK, 1, unit_cols(n)], src[MDK:P]).then_inc(evacuated, 1)
                else:
                    nc.scalar.copy(raw[:, 2, unit_cols(n)], src).then_inc(evacuated, 1)

            def prepare(t, r):
                par = r % 2
                grid = lambda bank: ps[:, bank, 0:3 * P].rearrange("p (i c) -> p i c", i=3)
                act.wait_ge(prep_done, t * 15 + (5 * r + 1))
                if r > 0:
                    act.wait_ge(made, t * 6 + 2 * r)
                for i in range(BATCHES):
                    c = 3 * r + i
                    op = nc.scalar.activation(q_scale[:, i], ps[:, 2, i * P:(i + 1) * P], ACT.Exp,
                                              bias=hg[:, 4, c:c + 1], scale=-1.0)
                op.then_inc(qsc_done, 1)
                act.wait_ge(e_done, t * 3 + (r + 1))
                nc.scalar.activation(pe_exp[:], pe_exp[:], ACT.Exp, scale=-1.0).then_inc(exp_done, 1)
                act.wait_ge(prep_done, t * 15 + (5 * r + 3))
                if r == 2:
                    act.wait_ge(den_done, t * 9 + 3)
                    act.wait_ge(chain, t * 18 + 6)
                nc.scalar.activation(floor[:, par], grid(4), ACT.Exp, scale=-1.0).then_inc(floor_done, 1)
                act.wait_ge(prep_done, t * 15 + (5 * r + 4))
                for i in range(BATCHES):
                    c = 3 * r + i
                    op = nc.scalar.mul(kw[:, par, i], ps[:, 5, i * MDK:(i + 1) * MDK], hg[:, 3, c:c + 1])
                op.then_inc(tok_done, 1)
                act.wait_ge(prep_done, t * 15 + (5 * r + 5))
                nc.scalar.copy(v_tok[:, par, :, 0:DV], grid(2)).then_inc(tok_done, 1)

            def chunk(t, r, i):
                c = 3 * r + i
                act.wait_ge(chain, t * 18 + (2 * c + 1))
                nc.scalar.copy(num[:, c * P:(c + 1) * P], ps[:, 6, 0:P]).then_inc(num_done, 1)

            def head(t, more):
                if more:
                    for u in range(3):
                        evacuate(t + 1, u, False)
                nc.scalar.preload_act_table_set("natural_log_exp_and_others")
                act.wait_ge(cols_done, t * 2 + 2)
                n = 9
                for r in range(BATCHES + 1):
                    if r < BATCHES:
                        prepare(t, r)
                    for i in range(BATCHES):
                        for _ in range(2 if r in (0, 3) else 1):
                            if more and n < 27:
                                if n % 3 == 2:
                                    evacuate(t + 1, n // 3, False)
                                n += 1
                        if r > 0:
                            chunk(t, r - 1, i)
                if more:
                    while n < 27:
                        if n % 3 == 2:
                            evacuate(t + 1, n // 3, False)
                        n += 1
                act.wait_ge(num_done, t * 9 + 9)
                act.wait_ge(den_done, t * 9 + 9)
                nc.scalar.activation(den[:, 0:TOK], den[:, 0:TOK], ACT.Square,
                                     scale=math.sqrt(DV * RMS_EPS)).then_inc(den2_done, 1)
                for n in range(NU):
                    if n >= 2:
                        act.wait_ge(ss_done, t * 3 + (n - 1))
                    nc.scalar.activation(sq[:, n % 2], num[:, unit_cols(n)], ACT.Square).then_inc(sq_done, 1)
                for n in range(NU):
                    act.wait_ge(clamped, t * 3 + (n + 1))
                    nc.scalar.activation(rs[:, n], rs[:, n], ACT.Ln, scale=1.0 / DV).then_inc(ln_done, 1)
                    act.wait_ge(ln_done, t * 3 + (n + 1))
                    nc.scalar.activation(rs[:, n], rs[:, n], ACT.Exp, scale=-0.5).then_inc(rs_done, 1)

            for u in range(U):
                evacuate(0, u, True)
            with act.Fori(0, HEADS - 1) as t:
                head(t, True)
            head(HEADS - 1, False)

        @block.vector
        def _(dve):
            def take(dst, src):
                return nc.vector.tensor_scalar(dst, src, 1.0, None, ALU.mult)

            def prepare(t, r):
                par = r % 2
                dve.wait_ge(prep_done, t * 15 + (5 * r + 1))
                dve.wait_ge(qsc_done, t * 3 + (r + 1))
                for i in range(BATCHES):
                    c = 3 * r + i
                    op = nc.vector.scalar_tensor_tensor(out=pe_exp[:, i], in0=ps[:, 2, i * P:(i + 1) * P],
                                                        scalar=hg[:, 0, c:c + 1], in1=tk.later_neg[:],
                                                        op0=ALU.subtract, op1=ALU.subtract)
                op.then_inc(e_done, 1)
                dve.wait_ge(exp_done, t * 3 + (r + 1))
                dve.wait_ge(prep_done, t * 15 + (5 * r + 2))
                if r == 2:
                    dve.wait_ge(chain, t * 18 + 6)
                nc.vector.scalar_tensor_tensor(out=pt[:, par].rearrange("p i c -> p (i c)"), in0=ps[:, 3, 0:3 * P],
                                               scalar=MDK ** -0.5, in1=pe_exp[:].rearrange("p i c -> p (i c)"),
                                               op0=ALU.mult, op1=ALU.mult).then_inc(made, 1)
                nc.vector.tensor_tensor(qs[:, par].rearrange("p i c -> p (i c)"),
                                        qkv[0:MDK, 0, 3 * r * P:(3 * r + 3) * P],
                                        q_scale[0:MDK].rearrange("p i c -> p (i c)"), ALU.mult).then_inc(made, 1)

            def chunk(t, r, i):
                par, c = r % 2, 3 * r + i
                g = c // 8
                dve.wait_ge(chain, t * 18 + (2 * c + 2))
                dve.wait_ge(s_done, t * 9 + c) if c else dve.wait_ge(s_init, t + 1)
                nc.vector.scalar_tensor_tensor(out=state[:, g], in0=state[:, g], scalar=hg[0:MDK, 5, c:c + 1],
                                               in1=ps[0:MDK, 7, P:2 * P + 1], op0=ALU.mult, op1=ALU.add)
                dve.wait_ge(floor_done, t * 3 + (r + 1))
                part = den[:, c * P:(c + 1) * P]
                nc.vector.scalar_tensor_tensor(out=part, in0=ps[:, 7, 0:P], scalar=-1.0, in1=floor[:, par, i],
                                               op0=ALU.mult, op1=ALU.max).then_inc(negative_done, 1)
                dve.wait_ge(negative_done, t * 9 + (c + 1))
                nc.vector.tensor_tensor(part, part, ps[:, 7, 0:P], ALU.max).then_inc(den_done, 1)
                dve.wait_ge(den_done, t * 9 + (c + 1))
                dve.sem_inc(s_done, 1)

            with dve.Fori(0, HEADS) as t:
                dve.wait_ge(prep_done, t * 15)
                dve.wait_ge(tok_done, t * 6)
                dve.wait_ge(chain, t * 18)
                take(hg[:].rearrange("p q c -> p (q c)"),
                     gates[:, :, :, bass.ds(t, 1)].rearrange("p q c a -> p (q c a)")).then_inc(cols_done, 1)
                take(hgain[:], gain[:, bass.ds(t, 1)]).then_inc(cols_done, 1)
                dve.wait_ge(cols_done, t * 2 + 2)
                dve.wait_ge(s_out, t * 64)
                nc.vector.memset(state[:, 0], 0.0).then_inc(s_init, 1)
                for j in range(3):
                    rows = P if j == 2 else MDK
                    dve.wait_ge(evacuated, t * U + (2 + (NU * 3 if j == 2 else NU * 2)))
                    nc.vector.tensor_copy(qkv[0:rows, j, 0:TOK], raw[0:rows, j]).then_inc(taken, 1)
                dve.wait_ge(taken, t * 3 + 3)
                for r in range(BATCHES + 1):
                    if r < BATCHES:
                        prepare(t, r)
                    if r > 0:
                        for i in range(BATCHES):
                            chunk(t, r - 1, i)
                for n in range(NU):
                    dve.wait_ge(ss_done, t * 3 + (n + 1))
                    dve.wait_ge(den2_done, t + 1)
                    nc.vector.tensor_tensor(rs[:, n], ps[:, 2 + n, 0:UNIT], den[:, unit_cols(n)], ALU.add).then_inc(v_done, 1)
                    dve.wait_ge(v_done, t * 3 + (n + 1))
                    nc.vector.tensor_scalar(rs[:, n], rs[:, n], 1e-16, 1e19, ALU.max, ALU.min).then_inc(clamped, 1)
                for n in range(NU):
                    dve.wait_ge(rs_done, t * 3 + (n + 1))
                    cols = num[:, unit_cols(n)]
                    nc.vector.scalar_tensor_tensor(out=cols, in0=cols, scalar=hgain[:, 0:1], in1=rs[:, n],
                                                   op0=ALU.mult, op1=ALU.mult).then_inc(o_normed, 1)
                    dve.wait_ge(o_normed, t * 3 + (n + 1))
                    dst = tk.x[:, bass.ds(t, 1), unit_cols(n)].rearrange("p a t -> p (a t)")
                    nc.vector.tensor_tensor(dst, dst, cols, ALU.mult).then_inc(final_done, 1)


def mlstm_prologue(nc, tk, a, w_in, ws, gates, gain, m_end, qkv, v_tok, ab_t):
    ps = tk.ps
    H = HEADS
    R = TILES * H
    with ExitStack() as ctx:
        sem = semaphores(nc, ctx, "mlp")
        buf = lambda s, *sh: ctx.enter_context(nc.sbuf_tensor(f"mlp_{s}", *sh))
        ab = buf("if", [P, TILES, 2 * H], F32)
        bias_i, bias_f = buf("bias_i", [P, H], F32), buf("bias_f", [P, H], F32)
        out_of = buf("out_of", [P, 1], F32)
        x, e, mn, lf = buf("x", [P, TILES, H], F32), buf("e", [P, TILES, H], F32), buf("mn", [P, TILES, H], F32), buf("lf", [P, TILES, H], F32)
        b, last = buf("b", [P, TILES, H], F32), buf("last", [P, TILES, H], F32)
        rows = buf("rows", [R, 2, P], F32)
        end = buf("end", [P, TILES, H], F32)
        small_in, w_landed = sem("small_in"), sem("w_landed")
        zeroed, w_hi, w_split = sem("zeroed"), sem("w_hi"), sem("w_split")
        ab_done, ab_copied, step = sem("if_done"), sem("if_copied"), sem("steps")
        flat = lambda t: t.rearrange("p c h -> p (c h)")
        block = ctx.enter_context(nc.Block())

        @block.sync
        def _(sp):
            sp.wait_ge(zeroed, 5)
            sp.dma_start(ws.stage[:, 0, :, 0:2 * H], w_in[:, :, 3 * D:3 * D + 2 * H]).then_inc(w_landed, 16)
            sp.dma_start(gain[:], a["ml_norm"][0].rearrange("(h p) -> p h", p=P), allow_slow_non_contiguous=True).then_inc(small_in, 16)
            sp.dma_start(bias_i[:], a["ml_b_i"].to_broadcast([P, H])).then_inc(small_in, 16)
            sp.dma_start(bias_f[:], a["ml_b_f"].to_broadcast([P, H])).then_inc(small_in, 16)
            sp.dma_start(m_end[:, 1], a["state_mlstm_m"][0].to_broadcast([P, H])).then_inc(small_in, 16)
            sp.wait_ge(small_in, 64)

        @block.gpsimd
        def _(pool):
            nc.gpsimd.memset(qkv[:, :, TOK:TILES * P], 0.0).then_inc(zeroed, 1)
            nc.gpsimd.memset(ab_t[:, TOK:TILES * P], 0.0).then_inc(zeroed, 1)
            nc.gpsimd.memset(ws.hi[:, 0].bitcast(F32), 0.0).then_inc(zeroed, 1)
            nc.gpsimd.memset(ws.lo[:, 0].bitcast(F32), 0.0).then_inc(zeroed, 1)
            nc.gpsimd.memset(v_tok[:, :, :, DV:DV + 1], 1.0).then_inc(zeroed, 1)
            pool.wait_ge(zeroed, 5)
            pool.wait_ge(w_landed, 16)
            st = ws.stage[:, 0, :, 0:2 * H]
            nc.gpsimd.tensor_tensor(ws.hi[:, 0, :, 0:2 * H], st,
                                    tk.one[:][:, :, None].to_broadcast([P, KB, 2 * H]), ALU.mult).then_inc(w_hi, 1)
            pool.wait_ge(w_hi, 1)
            nc.gpsimd.tensor_tensor(ws.lo[:, 0, :, 0:2 * H], st, ws.hi[:, 0, :, 0:2 * H].bitcast(F32),
                                    ALU.subtract).then_inc(w_split, 1)

        @block.tensor
        def _(pe):
            pe.wait_ge(w_split, 1)
            for n in range(NU):
                for k in range(KB):
                    mm = split_product(pe, ps[:, n, 0:UNIT], ws.hi[:, 0, k], ws.lo[:, 0, k],
                                       tk.hi[:, k, unit_cols(n)], tk.lo[:, k, unit_cols(n)], k == 0, k == KB - 1)
                mm.then_inc(ab_done, 1)
            pe.wait_ge(ab_copied, NU)
            pe.wait_ge(zeroed, 5)
            for c in range(TILES):
                mm = pe.transpose(ps[:, 3, c * 2 * H:(c + 1) * 2 * H], ab_t[:, c * P:(c + 1) * P],
                                  tk.ident[0:2 * H, 0:2 * H])
            mm.then_inc(step, 1)
            pe.wait_ge(step, 11)
            pe.matmul(ps[:, 4, 0:R], tk.upto[:], flat(lf[:]), start=True, stop=True)
            pe.matmul(ps[:, 5, 0:R], tk.ones[:], flat(lf[:]), start=True, stop=True).then_inc(step, 1)
            pe.wait_ge(step, 15)
            pe.transpose(ps[0:R, 6, 0:P], flat(gates[:, 0]), tk.ident[:]).then_inc(step, 1)
            pe.wait_ge(step, 24)
            pe.transpose(ps[:, 7, 0:R], rows[:, 1], tk.ident[0:R, 0:R]).then_inc(step, 1)
            pe.wait_ge(step, 26)
            pe.matmul(ps[:, 0, 0:R], tk.ident[:, P - 1:P].to_broadcast([P, P]), flat(gates[:, 1]),
                      start=True, stop=True).then_inc(step, 1)

        @block.scalar
        def _(act):
            def do(n, *args, **kw):
                act.wait_ge(step, n - 1)
                nc.scalar.activation(*args, **kw).then_inc(step, 1)
            nc.scalar.preload_act_table_set("natural_log_exp_and_others")
            do(6, e[:], e[:], ACT.Exp)
            do(7, e[:], e[:], ACT.Ln, bias=tk.one[:, 0:1])
            do(51, gates[:, 5], gates[:, 5], ACT.Exp)
            do(53, gates[:, 3], gates[:, 3], ACT.Exp)

        @block.vector
        def _(dve):
            def do(n, op, *args, **kw):
                dve.wait_ge(step, n - 1)
                op(*args, **kw).then_inc(step, 1)
            tt, stt, ts, cp = nc.vector.tensor_tensor, nc.vector.scalar_tensor_tensor, nc.vector.tensor_scalar, nc.vector.tensor_copy
            over = lambda t: t[:][:, None, :].to_broadcast([P, TILES, H])
            for n in range(NU):
                dve.wait_ge(ab_done, n + 1)
                cp(ab_t[:, unit_cols(n)], ps[0:2 * H, n, 0:UNIT]).then_inc(ab_copied, 1)
            dve.wait_ge(small_in, 64)
            do(2, cp, flat(ab[:]), ps[:, 3, 0:TILES * 2 * H])
            do(3, tt, x[:], ab[:, :, H:2 * H], over(bias_f), ALU.add)
            do(4, ts, mn[:], x[:], 0.0, None, ALU.min)
            do(5, stt, out=e[:], in0=mn[:], scalar=2.0, in1=x[:], op0=ALU.mult, op1=ALU.subtract)
            do(8, tt, lf[:], mn[:], e[:], ALU.subtract)
            do(9, ts, out_of[:], tk.upto[:, SAMPLE - 1:SAMPLE], 1.0, -NEG, ALU.subtract, ALU.mult)
            do(10, tt, x[:], ab[:, :, 0:H], over(bias_i), ALU.add)
            do(11, ts, lf[:, TILES - 1], lf[:, TILES - 1], tk.upto[:, SAMPLE - 1:SAMPLE], None, ALU.mult)
            do(13, cp, flat(b[:]), ps[:, 4, 0:R])
            do(14, ts, x[:, TILES - 1], x[:, TILES - 1], out_of[:, 0:1], None, ALU.add)
            do(15, tt, gates[:, 0], x[:], b[:], ALU.subtract)
            do(17, cp, rows[:, 0], ps[0:R, 6, 0:P])
            for l in range(LEVELS):
                w, src, dst = 1 << l, rows[:, l % 2], rows[:, (l + 1) % 2]
                dve.wait_ge(step, 17 + l)
                cp(dst[:, 0:w], src[:, 0:w])
                tt(dst[:, w:], src[:, w:], src[:, 0:P - w], ALU.max).then_inc(step, 1)
            do(26, cp, flat(gates[:, 1]), ps[:, 7, 0:R])
            do(28, cp, flat(last[:]), ps[:, 5, 0:R])
            do(29, cp, flat(end[:]), ps[:, 0, 0:R])
            do(30, nc.vector.memset, gates[:, 4, 0], 0.0)
            n = 31
            for c in range(TILES):
                if c == TILES - 1:
                    do(n, cp, gates[:, 4, c], m_end[:, 1]); n += 1
                do(n, tt, end[:, c], end[:, c], gates[:, 4, c], ALU.max); n += 1
                m_next = gates[:, 4, c + 1] if c < TILES - 2 else m_end[:, c - TILES + 2]
                do(n, tt, m_next, last[:, c], end[:, c], ALU.add); n += 1
            assert n == 50
            do(50, tt, gates[:, 5], gates[:, 4], end[:], ALU.subtract)
            do(52, tt, gates[:, 3], gates[:, 0], end[:], ALU.subtract)
            do(54, tt, gates[:, 1], gates[:, 1], gates[:, 4], ALU.max)
            do(55, tt, gates[:, 2], gates[:, 1], b[:], ALU.add)
            do(56, ts, gates[:, 3], gates[:, 3], MDK ** -0.5, None, ALU.mult)
            dve.wait_ge(step, 56)


def build_trunk(nc, a):
    with ExitStack() as ctx:
        buf = lambda s, *sh: ctx.enter_context(nc.sbuf_tensor(s, *sh))
        tk = Trunk()
        tk.ps = ctx.enter_context(nc.psum_tensor("ps", [P, 8, 512], F32))
        tk.x_dram = nc.dram_tensor("x_kept", (P, KB, TOK), F32).ap()
        tk.ones, tk.ident, tk.upto = buf("ones", [P, P], F32), buf("ident", [P, P], F32), buf("upto", [P, P], F32)
        tk.later_neg, tk.earlier_neg = buf("later_neg", [P, P], F32), buf("earlier_neg", [P, P], F32)
        tk.joins = buf("joins", [P, LEVELS, P], BF16)
        tk.eps, tk.one, tk.log_dk = buf("eps", [P, 1], F32), buf("one", [P, 1], F32), buf("log_dk", [P, 1], F32)
        tk.hi, tk.lo = buf("act_hi", [P, KB, TOK], F32R), buf("act_lo", [P, KB, TOK], F32R)

        tk.x = buf("x", [P, KB, TOK], F32)

        load_phase(nc, tk, a["x_prompt"], a["x_sample"])
        norm_phase(nc, tk, a["norm_mix"][0], "norm0", True)
        gdn_phase(nc, tk, a)
        out_phase(nc, tk, a["gdn_w_out"][0], "gdn_out")
        norm_phase(nc, tk, a["norm_ffn"][0], "norm1", False)
        ffn_phase(nc, tk, a["ffn_w_gu"][0], a["ffn_w_down"][0], "ffn0")
        norm_phase(nc, tk, a["norm_mix"][1], "norm2", True)
        mlstm_phase(nc, tk, a)
        out_phase(nc, tk, a["ml_w_out"][0], "ml_out")
        norm_phase(nc, tk, a["norm_ffn"][1], "norm3", False)
        ffn_phase(nc, tk, a["ffn_w_gu"][1], a["ffn_w_down"][1], "ffn1")
        store_phase(nc, tk, a["norm_final"], a["y_prompt"], a["y_sample"])


INPUTS = ["x_prompt", "x_sample", "state_gdn_conv", "state_gdn_S", "state_mlstm_C", "state_mlstm_n", "state_mlstm_m",
          "norm_mix", "gdn_w_in", "gdn_conv_w", "gdn_a_log", "gdn_dt_bias", "gdn_norm", "gdn_w_out", "ml_w_in",
          "ml_b_i", "ml_b_f", "ml_norm", "ml_w_out", "norm_ffn", "ffn_w_gu", "ffn_w_down", "norm_final"]
OUTPUTS = [("y_prompt", (1, PROMPT, D)), ("y_sample", (1, SAMPLE, D)),
           ("p_conv", (1, 1, HIST, 3 * D)), ("p_S", (1, 1, HEADS, DK, DV)), ("p_C", (1, 1, HEADS, MDK, DV)),
           ("p_n", (1, 1, HEADS, MDK)), ("p_m", (1, 1, HEADS)),
           ("s_conv", (1, 1, HIST, 3 * D)), ("s_S", (1, 1, HEADS, DK, DV)), ("s_C", (1, 1, HEADS, MDK, DV)),
           ("s_n", (1, 1, HEADS, MDK)), ("s_m", (1, 1, HEADS))]


def kernel(**inputs):
    import numpy as np
    import concourse.bacc as bacc
    from concourse.bass_utils import run_bass_kernel_spmd

    nc = bacc.Bacc("TRN2", target_bir_lowering=False, num_devices=1)
    arrays, a = {}, {}
    for name in INPUTS:
        arrays[f"in_{name}"] = np.ascontiguousarray(inputs[name])
        a[name] = nc.dram_tensor(f"in_{name}", arrays[f"in_{name}"].shape, F32, kind="ExternalInput").ap()
    for name, shape in OUTPUTS:
        a[name] = nc.dram_tensor(f"out_{name}", shape, F32, kind="ExternalOutput").ap()
    build_trunk(nc, a)
    got = run_bass_kernel_spmd(nc, [arrays], core_ids=[0]).results[0]
    return tuple(got[f"out_{name}"] for name, _ in OUTPUTS)
```

```python
import math
from contextlib import ExitStack

import concourse.bass as bass
from concourse import mybir

ALU = mybir.AluOpType
ACT = mybir.ActivationFunctionType
AX = mybir.AxisListType
F32 = mybir.dt.float32
F32R = mybir.dt.float32r
BF16 = mybir.dt.bfloat16

P = 128
PROMPT = 1024
SAMPLE = 32
TOK = PROMPT + SAMPLE
D = 1024
KB = D // P
NU = 3
UNIT = TOK // NU
HEADS = 8
DK, DV = 128, 128
MDK = 64
FFN = 2816
FB = FFN // P
TILES = 9
BATCHES = 3
HIST = 3
TAPS = 4
GCOL = PROMPT + HIST
CW = GCOL + SAMPLE
CPAD = GCOL + P
CU = CW // NU
LEVELS = 7
RMS_EPS = 1e-6
L2_EPS = 1e-6
NEG = -1e30


def tile_cols(c):
    start = c * P if c < TILES - 1 else GCOL
    return slice(start, start + P)


def unit_cols(n):
    return slice(n * UNIT, (n + 1) * UNIT)


def semaphores(nc, ctx, tag, again=False):
    made = []

    def sem(name):
        if again:
            made.append(nc.alloc_semaphore(name=f"{tag}_{name}"))
            return made[-1]
        return ctx.enter_context(nc.semaphore(f"{tag}_{name}"))

    def zero():
        if made:
            nc.clear_and_free_semaphores(made)
            nc.all_engine_barrier()

    ctx.callback(zero)
    return sem


def split_product(pe, out, w_hi, w_lo, rhs_hi, rhs_lo, first, last):
    pe.matmul(out, w_hi, rhs_hi, start=first, stop=False)
    pe.matmul(out, w_hi, rhs_lo, start=False, stop=False)
    return pe.matmul(out, w_lo, rhs_hi, start=False, stop=last)


class Trunk:
    pass


class WeightStream:

    def __init__(self, nc, tk, ctx, sem, name, ring, stages=2):
        self.nc, self.ring, self.stages, self.one = nc, ring, stages, tk.one
        buf = lambda s, *a: ctx.enter_context(nc.sbuf_tensor(f"{name}_{s}", *a))
        self.stage = buf("stage", [P, stages, KB, P], F32)
        self.hi = buf("hi", [P, ring, KB, P], F32R)
        self.lo = buf("lo", [P, ring, KB, P], F32R)
        self.landed = [sem(f"w_landed{s}") for s in range(stages)]
        self.hi_done = sem("w_hi_done")
        self.split_done = sem("w_split_done")

        self.checked, self.act_checked = sem("w_checked"), sem("act_checked")

    def start(self, pool):
        pool.sem_inc(self.split_done, self.stages)

    def wait_stage(self, sp, j):
        sp.wait_ge(self.split_done, j + 1)
        sp.sem_inc(self.checked, 1)

    def load(self, sp, j, slot, src):
        self.wait_stage(sp, j)
        sp.dma_start(self.stage[:, slot], src).then_inc(self.landed[slot], 16)

    def split(self, pool, j, stage_slot, landed_count, ring_slot, halves=(0, 1)):
        nc = self.nc
        pool.wait_ge(self.landed[stage_slot], landed_count)
        for h in halves:
            part = slice(h * KB // 2, (h + 1) * KB // 2)
            st, hi, lo = (t[:, s, part] for t, s in ((self.stage, stage_slot), (self.hi, ring_slot), (self.lo, ring_slot)))
            one = self.one[:][:, :, None].to_broadcast([P, KB // 2, P])
            nc.gpsimd.tensor_tensor(hi, st, one, ALU.mult).then_inc(self.hi_done, 1)
            pool.wait_ge(self.hi_done, j * 2 + (h + 1))
            op = nc.gpsimd.tensor_tensor(lo, st, hi.bitcast(F32), ALU.subtract)
        if 1 in halves:
            op.then_inc(self.split_done, 1)

    def wait_ready(self, pe, j):
        pe.wait_ge(self.split_done, j + self.stages + 1)


def ffn_phase(nc, tk, gain, w_gu, w_down, tag):
    TURN = FB // 2
    B = 6
    U = 4 * NU + NU * KB
    ps, x = tk.ps, tk.x
    with ExitStack() as ctx:
        sem = semaphores(nc, ctx, tag)
        buf = lambda s, *a: ctx.enter_context(nc.sbuf_tensor(f"{tag}_{s}", *a))
        ws = WeightStream(nc, tk, ctx, sem, tag, B)
        gu = w_gu.rearrange("(k p) f -> p k f", p=P)
        dn = w_down.rearrange("(j p) (m c) -> p j m c", p=P, c=P)

        def load(sp, t):
            for b in range(4):
                ws.load(sp, t * B + b, b % 2, gu[:, :, bass.ds(t * (2 * P) + (b // 2 * P + b % 2 * FFN), P)])
            for j in range(2):
                ws.load(sp, t * B + (4 + j), j, dn[:, t * 2 + j])

        def split(pool, t, b):
            ws.split(pool, t * B + b, b % 2, t * 48 + (b // 2 * 16 + 16), b)

        def split_first(pool):
            ws.start(pool)
            for b in range(B):
                split(pool, 0, b)

        norm_phase(nc, tk, gain, f"{tag}n", False, (lambda sp: load(sp, 0), split_first))
        silu = buf("silu", [P, NU, UNIT], F32)
        hid = buf("hid", [P, NU, UNIT], F32)
        hid_hi = buf("hid_hi", [P, 2, NU, UNIT], F32R)
        hid_lo = buf("hid_lo", [P, 2, NU, UNIT], F32R)
        unit_done = sem("unit_done")
        silu_done = sem("silu_done")
        hid_done = sem("hid_done")
        hi_done = sem("hid_hi_done")
        lo_done = sem("hid_lo_done")
        added = sem("added")
        block = ctx.enter_context(nc.Block())

        @block.sync
        def _(sp):
            with sp.Fori(1, TURN) as t:
                load(sp, t)

        @block.gpsimd
        def _(pool):
            pool.sem_inc(unit_done, U)
            pool.sem_inc(silu_done, NU)
            pool.sem_inc(hid_done, NU)
            pool.sem_inc(lo_done, NU)
            pool.sem_inc(added, 2)
            with pool.Fori(1, TURN) as t:
                for b in range(B):
                    pool.wait_ge(unit_done, t * U + (NU * (b + 1) if b < 4 else U))
                    split(pool, t, b)

        @block.tensor
        def _(pe):
            with pe.Fori(0, TURN) as t:
                for b in range(4):
                    ws.wait_ready(pe, t * B + b)
                    for n in range(NU):
                        pe.wait_ge(hid_done if b % 2 else silu_done, t * 6 + (b // 2 * NU + n + 1))
                        out = ps[:, b % 2 * NU + n, 0:UNIT]
                        for k in range(KB):
                            mm = split_product(pe, out, ws.hi[:, b, k], ws.lo[:, b, k],
                                               tk.hi[:, k, unit_cols(n)], tk.lo[:, k, unit_cols(n)],
                                               k == 0, k == KB - 1)
                        mm.then_inc(unit_done, 1)
                ws.wait_ready(pe, t * B + 5)
                for n in range(NU):
                    pe.wait_ge(hi_done, t * 6 + (NU + n + 1))
                    pe.wait_ge(lo_done, t * 6 + (2 * NU + n + 1))
                    for m in range(KB):
                        pe.wait_ge(added, t * (NU * KB) + (n * KB + m + 1))
                        for j in range(2):
                            mm = split_product(pe, ps[:, 6 + m % 2, 0:UNIT],
                                               ws.hi[:, 4 + j, m], ws.lo[:, 4 + j, m],
                                               hid_hi[:, j, n], hid_lo[:, j, n], j == 0, j == 1)
                        mm.then_inc(unit_done, 1)

        @block.scalar
        def _(act):
            with act.Fori(0, TURN) as t:
                for j in range(2):
                    for n in range(NU):
                        act.wait_ge(unit_done, t * U + (U + 6 * j + n + 1))
                        act.wait_ge(hid_done, t * 6 + (j * NU + n + 1))
                        nc.scalar.activation(silu[:, n], ps[:, n, 0:UNIT], ACT.Silu).then_inc(silu_done, 1)
                    for n in range(NU):
                        act.wait_ge(hid_done, t * 6 + (j * NU + NU + n + 1))
                        act.wait_ge(unit_done, t * U + U)
                        nc.scalar.copy(hid_hi[:, j, n], hid[:, n]).then_inc(hi_done, 1)

        @block.vector
        def _(dve):
            with dve.Fori(0, TURN) as t:
                for j in range(2):
                    for n in range(NU):
                        dve.wait_ge(unit_done, t * U + (U + 6 * j + NU + n + 1))
                        dve.wait_ge(silu_done, t * 6 + (j * NU + NU + n + 1))
                        dve.wait_ge(lo_done, t * 6 + (j * NU + n + 1))
                        nc.vector.tensor_tensor(hid[:, n], silu[:, n], ps[:, NU + n, 0:UNIT],
                                                ALU.mult).then_inc(hid_done, 1)
                        dve.wait_ge(hi_done, t * 6 + (j * NU + n + 1))
                        nc.vector.tensor_tensor(hid_lo[:, j, n], hid[:, n], hid_hi[:, j, n].bitcast(F32),
                                                ALU.subtract).then_inc(lo_done, 1)
                for n in range(NU):
                    for m in range(KB):
                        dve.wait_ge(unit_done, t * U + (U + 4 * NU + n * KB + m + 1))
                        dve.wait_ge(added, t * (NU * KB) + 2)
                        nc.vector.tensor_tensor(x[:, m, unit_cols(n)], x[:, m, unit_cols(n)],
                                                ps[:, 6 + m % 2, 0:UNIT], ALU.add).then_inc(added, 1)


def norm_phase(nc, tk, gain, tag, spill, first=None):
    ps, x = tk.ps, tk.x
    H = KB // 2
    BY_POOL = 5
    with ExitStack() as ctx:
        sem = semaphores(nc, ctx, tag)
        buf = lambda s, *a: ctx.enter_context(nc.sbuf_tensor(f"{tag}_{s}", *a))
        g = buf("g", [P, KB], F32)
        sq = buf("sq", [P, 2, KB, UNIT], F32)
        r = buf("r", [P, NU, UNIT], F32)
        h = buf("h", [P, 2, KB, UNIT], F32)
        g_in, spilled = sem("gain_landed"), sem("x_spilled")
        sq_done, ss_done, ln_done, r_done = sem("sq_done"), sem("ss_done"), sem("ln_done"), sem("r_done")
        h_done, hi_done, lo_done, pool_lo_done = sem("h_done"), sem("hi_done"), sem("lo_done"), sem("pool_lo_done")
        block = ctx.enter_context(nc.Block())

        @block.sync
        def _(sp):
            sp.dma_start(g[:], gain.rearrange("(k p) -> p k", p=P), allow_slow_non_contiguous=True).then_inc(g_in, 16)
            if first:
                first[0](sp)
            if spill:
                sp.dma_start(tk.x_dram, x[:]).then_inc(spilled, 16)
                sp.wait_ge(spilled, 16)

        @block.tensor
        def _(pe):
            for n in range(NU):
                for k in range(KB):
                    if k % H == 0:
                        pe.wait_ge(sq_done, 2 * n + k // H + 1)
                    mm = pe.matmul(ps[:, n, 0:UNIT], tk.ones[:], sq[:, n % 2, k], start=k == 0, stop=k == KB - 1)
                mm.then_inc(ss_done, 1)

        @block.scalar
        def _(act):
            nc.scalar.preload_act_table_set("natural_log_exp_and_others")

            def square(n):
                if n >= 2:
                    act.wait_ge(ss_done, n - 1)
                for half in (slice(0, H), slice(H, KB)):
                    nc.scalar.activation(sq[:, n % 2, half], x[:, half, unit_cols(n)], ACT.Square).then_inc(sq_done, 1)

            def root(n):
                act.wait_ge(ss_done, n + 1)
                nc.scalar.activation(r[:, n], ps[:, n, 0:UNIT], ACT.Ln, bias=tk.eps[:, 0:1],
                                     scale=1.0 / D).then_inc(ln_done, 1)
                act.wait_ge(ln_done, n + 1)
                nc.scalar.activation(r[:, n], r[:, n], ACT.Exp, scale=-0.5).then_inc(r_done, 1)

            def high(n):
                act.wait_ge(h_done, n + 1)
                nc.scalar.copy(tk.hi[:, :, unit_cols(n)], h[:, n % 2]).then_inc(hi_done, 1)

            square(0)
            square(1)
            root(0)
            square(2)
            root(1)
            high(0)
            root(2)
            high(1)
            high(2)

        @block.vector
        def _(dve):
            def low(n):
                dve.wait_ge(hi_done, n + 1)
                cols = unit_cols(n)
                nc.vector.tensor_tensor(tk.lo[:, 0:BY_POOL, cols], h[:, n % 2, 0:BY_POOL],
                                        tk.hi[:, 0:BY_POOL, cols].bitcast(F32), ALU.subtract).then_inc(lo_done, 1)

            dve.wait_ge(g_in, 16)
            for n in range(NU):
                dve.wait_ge(r_done, n + 1)
                if n >= 2:
                    dve.wait_ge(lo_done, n - 1)
                    dve.wait_ge(pool_lo_done, n - 1)
                for k in range(KB):
                    op = nc.vector.scalar_tensor_tensor(out=h[:, n % 2, k], in0=x[:, k, unit_cols(n)],
                                                        scalar=g[:, k:k + 1], in1=r[:, n],
                                                        op0=ALU.mult, op1=ALU.mult)
                op.then_inc(h_done, 1)
                if n >= 1:
                    low(n - 1)
            low(NU - 1)
            dve.wait_ge(lo_done, NU)

        @block.gpsimd
        def _(pool):
            if first:
                first[1](pool)
            for n in range(NU):
                pool.wait_ge(hi_done, n + 1)
                cols = unit_cols(n)
                nc.gpsimd.tensor_tensor(tk.lo[:, BY_POOL:, cols], h[:, n % 2, BY_POOL:],
                                        tk.hi[:, BY_POOL:, cols].bitcast(F32), ALU.subtract).then_inc(pool_lo_done, 1)
            pool.wait_ge(pool_lo_done, NU)


def load_phase(nc, tk, x_prompt, x_sample):
    ps, x = tk.ps, tk.x
    with ExitStack() as ctx:
        sem = semaphores(nc, ctx, "load")
        buf = lambda s, *a: ctx.enter_context(nc.sbuf_tensor(f"load_{s}", *a))
        rows = buf("rows", [P, 3, D], F32)
        landed = [sem(f"rows_landed{s}") for s in range(3)]
        made, turned, copied = sem("constants_made"), sem("turned"), sem("copied")
        block = ctx.enter_context(nc.Block())

        def size(c):
            return P if c < TILES - 1 else SAMPLE

        @block.sync
        def _(sp):
            for c in range(TILES):
                if c >= 3:
                    sp.wait_ge(turned, 2 * (c - 2))
                src = x_prompt[0, c * P:(c + 1) * P] if c < TILES - 1 else x_sample[0]
                sp.dma_start(rows[0:size(c), c % 3], src).then_inc(landed[c % 3], 16)

        @block.gpsimd
        def _(pool):
            n = 0
            def step(op):
                nonlocal n
                n += 1
                op.then_inc(made, 1)
                pool.wait_ge(made, n)
            step(nc.gpsimd.memset(tk.ones[:], 1.0))
            step(nc.gpsimd.memset(tk.eps[:], RMS_EPS))
            step(nc.gpsimd.memset(tk.one[:], 1.0))
            step(nc.gpsimd.memset(tk.log_dk[:], -0.5 * math.log(DK)))
            step(nc.gpsimd.affine_select(out=tk.ident[:], in_=tk.ones[:], compare_op=ALU.is_equal, fill=0.0,
                                         base=0, pattern=[[1, P]], channel_multiplier=-1))
            step(nc.gpsimd.affine_select(out=tk.upto[:], in_=tk.ones[:], compare_op=ALU.is_ge, fill=0.0,
                                         base=0, pattern=[[1, P]], channel_multiplier=-1))
            step(nc.gpsimd.memset(tk.later_neg[:], 0.0))
            step(nc.gpsimd.affine_select(out=tk.later_neg[:], in_=tk.later_neg[:], compare_op=ALU.is_ge, fill=NEG,
                                         base=0, pattern=[[1, P]], channel_multiplier=-1))
            step(nc.gpsimd.memset(tk.joins[:], 0.0))
            for l in range(LEVELS):
                s = 1 << l
                blocks = P // (2 * s)
                view = tk.joins[:, l].rearrange("p (b h c) -> p b h c", b=blocks, h=2)
                step(nc.gpsimd.memset(view[:, :, 1], 1.0))
                step(nc.gpsimd.affine_select(out=view[:, :, 1], in_=view[:, :, 1], compare_op=ALU.is_ge, fill=0.0,
                                             base=0, pattern=[[-2 * s, blocks], [0, s]], channel_multiplier=1))
                step(nc.gpsimd.affine_select(out=view[:, :, 1], in_=view[:, :, 1], compare_op=ALU.is_ge, fill=0.0,
                                             base=s - 1, pattern=[[2 * s, blocks], [0, s]], channel_multiplier=-1))

        @block.tensor
        def _(pe):
            pe.wait_ge(made, 5)
            for c in range(TILES):
                pe.wait_ge(landed[c % 3], 16 * (c // 3 + 1))
                for half in range(2):
                    if c >= 2:
                        pe.wait_ge(copied, 2 * (c - 2) + half + 1)
                    for k in range(4):
                        mm = pe.transpose(ps[:, (c % 2) * 2 + half, k * P:k * P + size(c)],
                                          rows[0:size(c), c % 3, (half * 4 + k) * P:(half * 4 + k + 1) * P],
                                          tk.ident[0:size(c), 0:size(c)])
                    mm.then_inc(turned, 1)

        @block.vector
        def _(dve):
            for c in range(TILES):
                for half in range(2):
                    dve.wait_ge(turned, 2 * c + half + 1)
                    src = ps[:, (c % 2) * 2 + half].rearrange("p (k t) -> p k t", k=4)[:, :, 0:size(c)]
                    nc.vector.tensor_copy(x[:, half * 4:half * 4 + 4, c * P:c * P + size(c)], src).then_inc(copied, 1)
            dve.wait_ge(copied, 2 * TILES)


def store_phase(nc, tk, gain, y_prompt, y_sample):
    ps, x = tk.ps, tk.x
    with ExitStack() as ctx:
        sem = semaphores(nc, ctx, "store")
        buf = lambda s, *a: ctx.enter_context(nc.sbuf_tensor(f"store_{s}", *a))
        g = buf("g", [P, KB], F32)
        sq = buf("sq", [P, KB, UNIT], F32)
        r = buf("r", [P, TOK], F32)
        rows = buf("rows", [P, 2, D], F32)
        g_in, sq_done, ss_done, ln_done, r_done, y_done = (
            sem("gain_landed"), sem("sq_done"), sem("ss_done"), sem("ln_done"), sem("r_done"), sem("y_done"))
        turned, copied, stored = sem("turned"), sem("copied"), [sem("stored0"), sem("stored1")]
        block = ctx.enter_context(nc.Block())

        def size(c):
            return P if c < TILES - 1 else SAMPLE

        def unit_of(c):
            return (c * P + size(c) - 1) // UNIT

        @block.sync
        def _(sp):
            sp.dma_start(g[:], gain.rearrange("(k p) -> p k", p=P), allow_slow_non_contiguous=True).then_inc(g_in, 16)
            for c in range(TILES):
                sp.wait_ge(copied, 2 * (c + 1))
                dst = y_prompt[0, c * P:(c + 1) * P] if c < TILES - 1 else y_sample[0]
                sp.dma_start(dst, rows[0:size(c), c % 2]).then_inc(stored[c % 2], 16)
            sp.wait_ge(stored[0], 16 * 5)
            sp.wait_ge(stored[1], 16 * 4)

        @block.tensor
        def _(pe):
            for n in range(NU):
                pe.wait_ge(sq_done, n + 1)
                for k in range(KB):
                    mm = pe.matmul(ps[:, 4 + n, 0:UNIT], tk.ones[:], sq[:, k], start=k == 0, stop=k == KB - 1)
                mm.then_inc(ss_done, 1)
            for c in range(TILES):
                if c == 0 or unit_of(c) != unit_of(c - 1):
                    pe.wait_ge(y_done, unit_of(c) + 1)
                for half in range(2):
                    if c >= 2:
                        pe.wait_ge(copied, 2 * (c - 2) + half + 1)
                    for k in range(4):
                        mm = pe.transpose(ps[0:size(c), (c % 2) * 2 + half, k * P:(k + 1) * P],
                                          x[:, half * 4 + k, c * P:c * P + size(c)], tk.ident[:])
                    mm.then_inc(turned, 1)

        @block.scalar
        def _(act):
            nc.scalar.preload_act_table_set("natural_log_exp_and_others")
            for n in range(NU):
                if n >= 1:
                    act.wait_ge(ss_done, n)
                nc.scalar.activation(sq[:], x[:, :, unit_cols(n)], ACT.Square).then_inc(sq_done, 1)
                act.wait_ge(ss_done, n + 1)
                nc.scalar.activation(r[:, unit_cols(n)], ps[:, 4 + n, 0:UNIT], ACT.Ln, bias=tk.eps[:, 0:1],
                                     scale=1.0 / D).then_inc(ln_done, 1)
                act.wait_ge(ln_done, n + 1)
                nc.scalar.activation(r[:, unit_cols(n)], r[:, unit_cols(n)], ACT.Exp, scale=-0.5).then_inc(r_done, 1)
            for c in range(TILES):
                if c >= 2:
                    act.wait_ge(stored[c % 2], 16 * (c // 2))
                for half in range(2):
                    act.wait_ge(turned, 2 * c + half + 1)
                    nc.scalar.copy(rows[0:size(c), c % 2, half * 512:(half + 1) * 512],
                                   ps[0:size(c), (c % 2) * 2 + half]).then_inc(copied, 1)

        @block.vector
        def _(dve):
            dve.wait_ge(g_in, 16)
            for n in range(NU):
                dve.wait_ge(r_done, n + 1)
                for k in range(KB):
                    op = nc.vector.scalar_tensor_tensor(out=x[:, k, unit_cols(n)], in0=x[:, k, unit_cols(n)],
                                                        scalar=g[:, k:k + 1], in1=r[:, unit_cols(n)],
                                                        op0=ALU.mult, op1=ALU.mult)
                op.then_inc(y_done, 1)


def out_phase(nc, tk, w_out, tag):
    ps, x = tk.ps, tk.x
    with ExitStack() as ctx:
        sem = semaphores(nc, ctx, tag)
        buf = lambda s, *a: ctx.enter_context(nc.sbuf_tensor(f"{tag}_{s}", *a))
        ws = WeightStream(nc, tk, ctx, sem, tag, 2)
        x_in = sem("x_landed")
        unit_done = sem("unit_done")
        added = sem("added")
        hi_done, lo_done = sem("o_hi_done"), sem("o_lo_done")
        w = w_out.rearrange("(k p) f -> p k f", p=P)
        block = ctx.enter_context(nc.Block())

        @block.sync
        def _(sp):
            def load(t):
                for b in range(2):
                    ws.load(sp, t * 2 + b, b, w[:, :, bass.ds(t * (2 * P) + b * P, P)])

            load(0)
            sp.wait_ge(lo_done, KB)
            sp.dma_start(x[:], tk.x_dram).then_inc(x_in, 16)
            with sp.Fori(1, KB // 2) as t:
                load(t)

        @block.gpsimd
        def _(pool):
            ws.start(pool)
            pool.sem_inc(unit_done, 6)
            pool.sem_inc(added, 6)
            with pool.Fori(0, KB // 2) as t:
                for b in range(2):
                    pool.wait_ge(unit_done, t * 6 + (3 * b + 3))
                    ws.split(pool, t * 2 + b, b, t * 16 + 16, b)

        @block.scalar
        def _(act):
            for k in range(KB):
                nc.scalar.copy(tk.hi[:, k], x[:, k]).then_inc(hi_done, 1)

        @block.tensor
        def _(pe):
            def turn(t, first):
                for b in range(2):
                    ws.wait_ready(pe, t * 2 + b)
                    for n in range(NU):
                        pe.wait_ge(added, t * 6 + (3 * b + n + 1))
                        for k in range(KB):
                            if first and b == n == 0:
                                pe.wait_ge(lo_done, k + 1)
                            mm = split_product(pe, ps[:, 3 * b + n, 0:UNIT], ws.hi[:, b, k], ws.lo[:, b, k],
                                               tk.hi[:, k, unit_cols(n)], tk.lo[:, k, unit_cols(n)],
                                               k == 0, k == KB - 1)
                        mm.then_inc(unit_done, 1)

            turn(0, True)
            with pe.Fori(1, KB // 2) as t:
                turn(t, False)

        @block.vector
        def _(dve):
            for k in range(KB):
                dve.wait_ge(hi_done, k + 1)
                nc.vector.tensor_tensor(tk.lo[:, k], x[:, k], tk.hi[:, k].bitcast(F32),
                                        ALU.subtract).then_inc(lo_done, 1)
            dve.wait_ge(x_in, 16)
            with dve.Fori(0, KB // 2) as t:
                for b in range(2):
                    for n in range(NU):
                        dve.wait_ge(unit_done, t * 6 + (6 + 3 * b + n + 1))
                        cols = x[:, bass.ds(t * 2 + b, 1), unit_cols(n)].rearrange("p a t -> p (a t)")
                        nc.vector.tensor_tensor(cols, cols, ps[:, 3 * b + n, 0:UNIT],
                                                ALU.add).then_inc(added, 1)


def gdn_phase(nc, tk, a):
    ps = tk.ps
    B = 4
    U = B * NU
    w_in = a["gdn_w_in"][0].rearrange("(k p) f -> p k f", p=P)
    

    def fill(r, l, place):
        if r == BATCHES:
            return {"A": 1, "B": 1, "T": 5}[place] if l < 4 else 0
        return {"P": (10, 5, 5)[r], "A": 2, "B": 1}[place]

    taps = {}
    for ch, start in enumerate((LEVELS, 2 * LEVELS, 2 * LEVELS + 4)):
        for tap in range(TAPS):
            taps[divmod(start + tap, LEVELS)] = (ch, tap)
    SUMS = ((0, 1), (2, 3), (), (4,), (5,), (), ())
    SQUARES = ((2, 3), (), (4, 5), (), (), (), ())
    ROOTS = ((), (0,), (1,), (2, 3), (4,), (5,), ())
    SCALED = ((), (), (0,), (1,), (2, 3), (4,), (5,))
    O_SUMS = ((), (), (), (), (), (0, 1), ())
    O_SQUARES = ((0,), (1,), (), (), (), (), ())
    O_ROOTS = ((), (), (), (), (), (0,), (1,))
    NQ = 5
    with ExitStack() as ctx:
        sem = semaphores(nc, ctx, "gdn", again=True)
        buf = lambda s, *a: ctx.enter_context(nc.sbuf_tensor(f"gdn_{s}", *a))
        ws = WeightStream(nc, tk, ctx, sem, "gdn", 2)
        gates = buf("gates", [P, NQ + 1, TILES, HEADS], F32)
        conv_w = buf("conv_w", [P, TAPS * 3, HEADS], F32)
        hist = buf("hist", [P, HIST * 3, HEADS], F32)
        tails = buf("tails", [P, 2, HIST * 3, HEADS], F32)
        tail_rows = buf("tail_rows", [P, 2, P], F32)
        R = HIST * 3 * HEADS
        tails_turned, tails_copied, tails_out = sem("tails_turned"), sem("tails_copied"), sem("tails_out")
        gain = buf("gain", [P, 1], F32)
        raw = buf("raw", [P, 2, PROMPT + 2 * HIST + SAMPLE], F32)
        qkv = buf("qkv", [P, 3, CPAD], F32)
        conv = buf("conv", [P, 2, CW], F32)
        o = buf("o", [P, TOK], F32)
        hw = buf("head_conv_w", [P, TAPS * 3], F32)
        hg = buf("head_gates", [P, NQ + 1, TILES], F32)
        sq = buf("sq", [P, 2, CU], F32)
        rs = buf("rs", [P, 2, CU], F32)
        gam = buf("gam", [P, BATCHES, P], F32)
        exp_d = buf("exp_d", [P, BATCHES, P], F32)
        mt = buf("mt", [P, BATCHES, P], F32)
        mt_l = buf("mt_level", [P, 2, BATCHES, P], F32)
        wz = buf("wz", [P, BATCHES, P], F32)
        z = buf("z", [P, 2, 2, BATCHES, P], F32)
        att = buf("att", [P, 2, BATCHES, P], F32)
        qd = buf("qd", [P, 2, BATCHES, P], F32)
        k_tail = buf("k_tail", [P, 2, BATCHES, P], F32)
        v_tok = buf("v_tok", [P, 2, BATCHES, P], F32)
        y = buf("y", [P, P], F32)
        v_new = buf("v_new", [P, P], F32)
        state = buf("state", [P, 2, DV], F32)

        o_work = [b.rearrange("p i c -> p (i c)")[:, 0:UNIT] for b in (mt[:], mt_l[:, 0], mt_l[:, 1])]

        gdn_prologue(nc, tk, a, w_in, ws, gates, conv_w, hist, gain, raw, qkv, tail_rows, conv[0:2 * HEADS].rearrange("p a c -> p (a c)"))
        unit_done, evacuated = sem("unit_done"), sem("evacuated")
        conv_steps, conv_done, silu_done, z_silu_done = (sem("conv_steps"), sem("conv_done"), sem("silu_done"),
                                                         sem("z_silu_done"))
        taps_taken, frames_taken, cols_taken = sem("taps_taken"), sem("frames_taken"), sem("cols_taken")
        sq_done, ss_done, ln_done, rs_done, unit_len = (sem("sq_done"), sem("ss_done"), sem("ln_done"),
                                                        sem("rs_done"), sem("unit_len_done"))
        osq_done, oss_done, oln_done, ors_done = sem("osq_done"), sem("oss_done"), sem("oln_done"), sem("ors_done")
        prep_done, expd_done, e_done, gam_done = sem("prep_done"), sem("expd_done"), sem("e_done"), sem("gam_done")
        made = sem("att_mt_qd_done")
        tok_done = sem("tok_done")
        level_masked, z_first, z_done = sem("level_masked"), sem("z_first_done"), sem("z_done")
        wz_done, wz_copied, pz_done = sem("wz_done"), sem("wz_copied"), sem("pz_done")
        chain, y_done, vn_done, o_done, s_done = (sem("chain"), sem("y_done"), sem("vn_done"), sem("o_done"),
                                                  sem("s_done"))
        s_in, s_out, s_init = sem("state_landed"), sem("state_stored"), sem("state_zeroed")
        o_normed, final_done = sem("o_normed"), sem("final_done")
        block = ctx.enter_context(nc.Block())

        @block.sync
        def _(sp):
            def weights(t, ahead, b):
                ws.load(sp, t * B + (ahead * B + b), b % 2, w_in[:, :, bass.ds(t * P + (ahead * P + b * D), P)])

            def states(t):
                sp.dma_start(state[:, 1], a["state_gdn_S"][0, 0, t]).then_inc(s_in, 16)

            def store(t):
                sp.wait_ge(s_done, t * 9 + 9)
                sp.sem_inc(ws.checked, 1)
                sp.dma_start(a["p_S"][0, 0, t], state[:, 0]).then_inc(s_out, 16)
                sp.dma_start(a["s_S"][0, 0, t], state[:, 1]).then_inc(s_out, 16)

            def head(t, ahead):
                for b in range(1, B) if ahead >= 1 else ():
                    weights(t, 1, b)
                if ahead == 2:
                    weights(t, 2, 0)
                store(t)
                if ahead >= 1:
                    sp.wait_ge(s_out, t * 32 + 64)
                    sp.sem_inc(ws.checked, 1)
                    states(t + 1)

            for b in range(B):
                weights(0, 0, b)
            states(0)
            weights(0, 1, 0)
            with sp.Fori(0, HEADS - 2) as t:
                head(t, 2)
            head(HEADS - 2, 1)
            head(HEADS - 1, 0)
            for g, dst in enumerate((a["p_conv"], a["s_conv"])):
                sp.wait_ge(tails_copied, g + 1)
                sp.dma_start(dst[0, 0].rearrange("f (r c) -> (f r) c", c=P), tail_rows[0:R, g]).then_inc(tails_out, 16)
            sp.wait_ge(s_out, HEADS * 32 + 32)
            sp.wait_ge(tails_out, 32)

        @block.gpsimd
        def _(pool):
            ws.start(pool)
            pool.sem_inc(evacuated, 2)
            pool.sem_inc(s_out, 32)

            def weights(t, ahead, b, halves):
                if 0 in halves and (b >= 2 or ahead >= 1):
                    pool.wait_ge(unit_done, t * U + (ahead * U + NU * (b - 1)))
                ws.split(pool, t * B + (ahead * B + b), b % 2, t * 32 + (ahead * 32 + b // 2 * 16 + 16), b % 2, halves)

            def mask(t, r, l):
                i = r * LEVELS + l
                pool.wait_ge(made, t * 9 + 3 * r + 3)
                if r > 0 or l >= 2:
                    pool.wait_ge(wz_done, t * 21 + (i - 1))
                nc.gpsimd.tensor_tensor(mt_l[:, i % 2], mt[:],
                                        tk.joins[:, l][:, None, :].to_broadcast([P, BATCHES, P]),
                                        ALU.mult).then_inc(level_masked, 1)

            def head(t, ahead):
                for r in range(BATCHES):
                    for l in range(LEVELS):
                        mask(t, r, l)
                        for first, k, b in ((2, 1, 1), (LEVELS + 1, 1, 2), (2 * LEVELS, 1, 3), (2 * LEVELS + 4, 2, 0)):
                            half = r * LEVELS + l - first
                            if half in (0, 1) and ahead >= k:
                                weights(t, k, b, (half,))

            for b in range(B):
                weights(0, 0, b, (0, 1))
            weights(0, 1, 0, (0, 1))
            with pool.Fori(0, HEADS - 2) as t:
                head(t, 2)
            head(HEADS - 2, 1)
            head(HEADS - 1, 0)

        @block.tensor
        def _(pe):
            def piece(t, n, only_third=None):
                u, k = n // KB, n % KB
                b, cols = u // NU, unit_cols(u % NU)
                if n % (NU * KB) == 0:
                    ws.wait_ready(pe, t * B + b)
                if k == 0:
                    pe.wait_ge(evacuated, t * U + (u + 1))
                mm = split_product(pe, ps[:, u % 2, 0:UNIT], ws.hi[:, b % 2, k], ws.lo[:, b % 2, k],
                                   tk.hi[:, k, cols], tk.lo[:, k, cols], k == 0, k == KB - 1)
                if k == KB - 1:
                    mm.then_inc(unit_done, 1)

            def sums(h, i):
                pe.wait_ge(sq_done, h * 6 + (i + 1))
                if i >= 4:
                    pe.wait_ge(ln_done, h * 6 + (i - 3))
                pe.matmul(ps[:, 2 + i % 4, 0:CU], tk.ones[:], sq[:, i % 2], start=True, stop=True).then_inc(ss_done, 1)

            def o_sums(t, n, more):
                pe.wait_ge(osq_done, t * 3 + (n + 1))
                bank = (4, 5, 6)[n]
                if n == 2:
                    pe.wait_ge(s_done, t * 9 + 9)
                else:
                    pe.wait_ge(z_done, t * 24 + 24)
                    if more:
                        pe.wait_ge(ln_done, t * 6 + (6 + 3 + n))
                pe.matmul(ps[:, bank, 0:UNIT], tk.ones[:], o_work[n], start=True, stop=True).then_inc(oss_done, 1)

            def prepare(t, r, pieces):
                if r > 0:
                    pe.wait_ge(tok_done, t * 6 + 2 * r)
                for i in range(BATCHES):
                    mm = pe.matmul(ps[:, 2, i * P:(i + 1) * P],
                                   hg[:, NQ, 3 * r + i:3 * r + i + 1].to_broadcast([P, P]), tk.upto[:],
                                   start=True, stop=True)
                mm.then_inc(prep_done, 1)
                for bank, ch in ((3, 1), (4, 0)):
                    if r > 0 and bank == 4:
                        pe.wait_ge(z_done, t * 24 + 8 * r)
                    for i in range(BATCHES):
                        cols = tile_cols(3 * r + i)
                        mm = pe.matmul(ps[:, bank, i * P:(i + 1) * P], qkv[:, 1, cols], qkv[:, ch, cols],
                                       start=True, stop=True)
                    mm.then_inc(prep_done, 1)
                for i in range(BATCHES):
                    mm = pe.transpose(ps[:, 5, i * P:(i + 1) * P], qkv[:, 1, tile_cols(3 * r + i)], tk.ident[:])
                mm.then_inc(prep_done, 1)
                pieces(r, 0, "P")
                pe.wait_ge(expd_done, t * 3 + (r + 1))
                pe.wait_ge(e_done, t * 3 + (r + 1))
                for i in range(BATCHES):
                    mm = pe.transpose(ps[:, 2, i * P:(i + 1) * P], qkv[:, 2, tile_cols(3 * r + i)], tk.ident[:])
                mm.then_inc(prep_done, 1)

            def join_w(t, r, l):
                par, i = r % 2, r * LEVELS + l
                pe.wait_ge(level_masked, t * 21 + (i + 1))
                pe.wait_ge(z_first, t * 18 + (r * 6 + l)) if l else pe.wait_ge(z_done, t * 24 + (r * 8 + 1))
                if l == 0:
                    pe.wait_ge(made, t * 9 + (3 * r + 3))
                for i in range(BATCHES):
                    mm = pe.matmul(ps[:, 3, i * P:(i + 1) * P], mt_l[:, (r * LEVELS + l) % 2, i], z[:, par, 0, i],
                                   start=True, stop=True)
                mm.then_inc(wz_done, 1)

            def join_z(t, r, l, pieces):
                par, i = r % 2, r * LEVELS + l
                pe.wait_ge(wz_copied, t * 21 + (i + 1))
                pe.wait_ge(z_done, t * 24 + (r * 8 + l + 1))
                if l == 0:
                    pe.wait_ge(tok_done, t * 6 + (2 * r + 2))
                if 0 < l < LEVELS - 1:
                    for i in range(BATCHES):
                        mm = pe.matmul(ps[:, 4, i * P:(i + 1) * P], z[:, par, 1, i], wz[:, i], start=True, stop=True)
                    mm.then_inc(pz_done, 1)
                for i in range(BATCHES):
                    mm = pe.matmul(ps[:, 5, i * P:(i + 1) * P], wz[:, i], z[:, par, 1, i], start=True, stop=True)
                mm.then_inc(pz_done, 1)
                pieces(r, l, "B")

            def chain_step(t, r, s):
                par, i = r % 2, s // 3
                c = 3 * r + i
                g = c // 8
                if s % 3 == 0:
                    if c == 0:
                        pe.wait_ge(s_init, t + 1)
                    elif c < 8:
                        pe.wait_ge(s_done, t * 9 + c)
                    else:
                        pe.wait_ge(s_in, t * 16 + 16)
                        pe.wait_ge(s_done, t * 9 + c)
                    pe.matmul(ps[:, 6, 0:P], qkv[:, 1, tile_cols(c)], state[:, g],
                              start=True, stop=True).then_inc(chain, 1)
                elif s % 3 == 1:
                    pe.wait_ge(y_done, t * 9 + (c + 1))
                    pe.matmul(ps[:, 6, P:2 * P], z[:, par, 1, i], y[:], start=True, stop=True).then_inc(chain, 1)
                else:
                    if c >= 1:
                        pe.wait_ge(o_done, t * 9 + c)
                    pe.matmul(ps[:, 7, 0:P], state[:, g], qd[:, par, i], start=True, stop=False)
                    pe.wait_ge(vn_done, t * 9 + (c + 1))
                    pe.matmul(ps[:, 7, 0:P], v_new[:], att[:, par, i], start=False, stop=True)
                    pe.matmul(ps[:, 6, 2 * P:3 * P], k_tail[:, par, i], v_new[:],
                              start=True, stop=True).then_inc(chain, 1)

            def head(t, more):
                n = 0

                def pieces(r, l, place):
                    nonlocal n
                    for _ in range(fill(r, l, place) if more else 0):
                        piece(t + 1, n)
                        n += 1

                pe.wait_ge(cols_taken, t + 1)
                pe.wait_ge(unit_len, t * 6 + 6)
                pe.wait_ge(silu_done, t * 3 + 3)
                for r in range(BATCHES + 1):
                    if r < BATCHES:
                        prepare(t, r, pieces)
                    for l in range(LEVELS):
                        if r < BATCHES:
                            join_w(t, r, l)
                        pieces(r, l, "A")
                        if r > 0 and 2 * l < 9:
                            chain_step(t, r - 1, 2 * l)
                        if r < BATCHES:
                            join_z(t, r, l, pieces)
                        else:
                            pieces(r, l, "B")
                        if r > 0 and 2 * l + 1 < 9:
                            chain_step(t, r - 1, 2 * l + 1)
                        if more and r == BATCHES:
                            if l == 0:
                                pe.wait_ge(tok_done, t * 6 + 6)
                                pe.wait_ge(wz_copied, t * 21 + 21)
                                pe.wait_ge(z_done, t * 24 + 24)
                            for i in SUMS[l]:
                                sums(t + 1, i)
                        for u in O_SUMS[l] if r == BATCHES else ():
                            o_sums(t, u, more)
                pieces(BATCHES, 0, "T")
                o_sums(t, 2, more)

            for n in range(U * KB):
                piece(0, n)
            for i in range(6):
                sums(0, i)
            with pe.Fori(0, HEADS - 1) as t:
                head(t, True)
            head(HEADS - 1, False)
            pe.wait_ge(frames_taken, HEADS * 9)
            pe.wait_ge(oln_done, HEADS * 3)
            for g in range(2):
                pe.transpose(ps[0:R, g, 0:P], tails[:, g].rearrange("p f h -> p (f h)"), tk.ident[:]).then_inc(tails_turned, 1)

        @block.scalar
        def _(act):
            def evacuate(t, u, first):
                act.wait_ge(unit_done, t * U + (u + 1))
                b, n = u // NU, u % NU
                src = ps[:, u % 2, 0:UNIT]
                if b == 3:
                    dst = tk.x[:, bass.ds(t, 1), unit_cols(n)].rearrange("p a t -> p (a t)")
                    act.sem_inc(ws.act_checked, 1)
                    nc.scalar.copy(dst, src).then_inc(evacuated, 1)
                    return
                if b == 2:
                    act.wait_ge(conv_done, t * 3 + 1)
                elif not first:
                    act.wait_ge(conv_done, (t - 1) * 3 + (3, 2)[b])
                start = HIST + n * UNIT
                if n < NU - 1:
                    nc.scalar.copy(raw[:, b % 2, start:start + UNIT], src).then_inc(evacuated, 1)
                else:
                    cut = PROMPT - n * UNIT
                    nc.scalar.copy(raw[:, b % 2, start:start + cut], src[:, 0:cut])
                    nc.scalar.copy(raw[:, b % 2, PROMPT + 2 * HIST:], src[:, cut:]).then_inc(evacuated, 1)

            def silu(h, ch):
                act.wait_ge(conv_done, h * 3 + (ch + 1))
                place = conv[:, ch] if ch < 2 else qkv[:, 2, 0:CW]
                nc.scalar.activation(place, place, ACT.Silu).then_inc(silu_done, 1)

            def z_silu(h, n):
                act.wait_ge(evacuated, h * U + (2 + 3 * NU + n + 1))
                act.sem_inc(ws.act_checked, 1)
                place = tk.x[:, bass.ds(h, 1), unit_cols(n)].rearrange("p a t -> p (a t)")
                nc.scalar.activation(place, place, ACT.Silu).then_inc(z_silu_done, 1)

            def square(h, i):
                if i < 2:
                    act.wait_ge(silu_done, h * 3 + 2)
                else:
                    act.wait_ge(ss_done, h * 6 + (i - 1))
                nc.scalar.activation(sq[:, i % 2], conv[:, i // 3, i % 3 * CU:(i % 3 + 1) * CU],
                                     ACT.Square).then_inc(sq_done, 1)

            def root(h, i):
                act.wait_ge(ss_done, h * 6 + (i + 1))
                if i >= 2:
                    act.wait_ge(unit_len, h * 6 + (i - 1))
                dst = rs[:, i % 2]
                nc.scalar.activation(dst, ps[:, 2 + i % 4, 0:CU], ACT.Ln, bias=tk.eps[:, 0:1]).then_inc(ln_done, 1)
                act.wait_ge(ln_done, h * 6 + (i + 1))
                if i < 3:
                    nc.scalar.activation(dst, dst, ACT.Exp, scale=-0.5, bias=tk.log_dk[:, 0:1]).then_inc(rs_done, 1)
                else:
                    nc.scalar.activation(dst, dst, ACT.Exp, scale=-0.5).then_inc(rs_done, 1)

            def o_square(t, n):
                if n == 0:
                    act.wait_ge(wz_done, t * 21 + 21)
                    act.wait_ge(level_masked, t * 21 + 21)
                act.wait_ge(o_done, t * 9 + (3, 6, 9)[n])
                nc.scalar.activation(o_work[n], o[:, unit_cols(n)], ACT.Square).then_inc(osq_done, 1)

            def o_root(t, n):
                act.wait_ge(oss_done, t * 3 + (n + 1))
                nc.scalar.activation(o_work[n], ps[:, 4 + n, 0:UNIT], ACT.Ln, bias=tk.eps[:, 0:1],
                                     scale=1.0 / DV).then_inc(oln_done, 1)
                act.wait_ge(oln_done, t * 3 + (n + 1))
                nc.scalar.activation(o_work[n], o_work[n], ACT.Exp, scale=-0.5).then_inc(ors_done, 1)

            def prepare(t, r, pieces):
                act.wait_ge(e_done, t * 3 + (r + 1))
                nc.scalar.activation(gam[:], gam[:], ACT.Exp).then_inc(gam_done, 1)
                act.wait_ge(prep_done, t * 15 + (5 * r + 1))
                if r > 0:
                    act.wait_ge(made, t * 9 + 3 * r)
                d = ps[:, 2, 0:3 * P].rearrange("p (i c) -> p i c", i=3)
                nc.scalar.activation(exp_d[:], d, ACT.Exp).then_inc(expd_done, 1)
                if r == 2:
                    act.wait_ge(chain, t * 27 + 9)
                    act.wait_ge(y_done, t * 9 + 3)
                act.wait_ge(prep_done, t * 15 + (5 * r + 4))
                par = r % 2
                for i in range(BATCHES):
                    op = nc.scalar.mul(k_tail[:, par, i], ps[:, 5, i * P:(i + 1) * P],
                                       hg[:, 3, 3 * r + i:3 * r + i + 1])
                op.then_inc(tok_done, 1)
                pieces(r, 0, "P")
                act.wait_ge(prep_done, t * 15 + (5 * r + 5))
                nc.scalar.copy(v_tok[:, par], ps[:, 2, 0:3 * P].rearrange("p (i c) -> p i c", i=3)).then_inc(tok_done, 1)

            def copy_w(t, r, l):
                i = r * LEVELS + l
                act.wait_ge(wz_done, t * 21 + (i + 1))
                nc.scalar.copy(wz[:], ps[:, 3, 0:3 * P].rearrange("p (i c) -> p i c", i=3)).then_inc(wz_copied, 1)

            def chain_step(t, r, s):
                c = 3 * r + s // 3
                if s % 3 == 1:
                    act.wait_ge(chain, t * 27 + (3 * c + 2))
                    nc.scalar.copy(v_new[:], ps[:, 6, P:2 * P]).then_inc(vn_done, 1)
                elif s % 3 == 2:
                    act.wait_ge(chain, t * 27 + (3 * c + 3))
                    w = P if c < 8 else SAMPLE
                    nc.scalar.copy(o[:, c * P:c * P + w], ps[:, 7, 0:w]).then_inc(o_done, 1)

            def head(t, more):
                n = 0

                def pieces(r, l, place):
                    nonlocal n
                    for _ in range(fill(r, l, place) if more else 0):
                        if n % KB == KB - 1:
                            evacuate(t + 1, n // KB, False)
                        n += 1

                nc.scalar.preload_act_table_set("natural_log_exp_and_others")
                act.wait_ge(cols_taken, t + 1)
                for r in range(BATCHES + 1):
                    if r < BATCHES:
                        prepare(t, r, pieces)
                    for l in range(LEVELS):
                        if r < BATCHES:
                            copy_w(t, r, l)
                        pieces(r, l, "A")
                        if r > 0 and 2 * l < 9:
                            chain_step(t, r - 1, 2 * l)
                        pieces(r, l, "B")
                        if r > 0 and 2 * l + 1 < 9:
                            chain_step(t, r - 1, 2 * l + 1)
                        if r == 2 and 1 <= l < 1 + NU:
                            z_silu(t, l - 1)
                        if r == BATCHES:
                            for u in O_SQUARES[l]:
                                o_square(t, u)
                        if more and (r, l) == (2, 2):
                            silu(t + 1, 0)
                        if not more and (r, l) == (2, 4):
                            nc.scalar.preload_act_table_set("natural_log_exp_and_others")
                        if more and (r, l) == (2, 4):
                            silu(t + 1, 1)
                        if more and (r, l) == (2, 5):
                            square(t + 1, 0)
                            square(t + 1, 1)
                        if more and r == BATCHES:
                            for i in SQUARES[l]:
                                square(t + 1, i)
                            if l == 1:
                                silu(t + 1, 2)
                                nc.scalar.preload_act_table_set("natural_log_exp_and_others")
                            for i in ROOTS[l]:
                                root(t + 1, i)
                        if r == BATCHES:
                            for u in O_ROOTS[l]:
                                o_root(t, u)
                pieces(BATCHES, 0, "T")
                o_square(t, 2)
                o_root(t, 2)

            for u in range(3 * NU):
                evacuate(0, u, True)
            for ch in range(3):
                silu(0, ch)
                evacuate(0, 3 * NU + ch, True)
            nc.scalar.preload_act_table_set("natural_log_exp_and_others")
            for i in range(6):
                square(0, i)
                if i >= 1:
                    root(0, i - 1)
            root(0, 5)
            with act.Fori(0, HEADS - 1) as t:
                head(t, True)
            head(HEADS - 1, False)

        @block.vector
        def _(dve):
            def take(dst, src):
                return nc.vector.tensor_scalar(dst, src, 1.0, None, ALU.mult)

            def take_taps(h):
                take(hw[:], conv_w[:, :, bass.ds(h, 1)].rearrange("p k a -> p (k a)")).then_inc(taps_taken, 1)

            def take_columns(h):
                take(hg[:].rearrange("p q c -> p (q c)"),
                     gates[:, :, :, bass.ds(h, 1)].rearrange("p q c a -> p (q c a)")).then_inc(cols_taken, 1)

            def convolve(h, ch, tap):
                src, slot = raw[:, ch % 2], ch % 2
                out = conv[:, ch] if ch < 2 else qkv[:, 2, 0:CW]
                if tap == 0:
                    dve.wait_ge(evacuated, h * U + (2 + NU * (ch + 1)))
                    past = hist[:, :, bass.ds(h, 1)].rearrange("p (f c) a -> p c (f a)", c=3)[:, ch]
                    take(raw[:, slot, GCOL:GCOL + HIST], past).then_inc(frames_taken, 1)
                    for g, start in ((0, PROMPT), (1, PROMPT + HIST + SAMPLE)):
                        dst = tails[:, g, :, bass.ds(h, 1)].rearrange("p (f c) a -> p c (f a)", c=3)[:, ch]
                        take(dst, raw[:, slot, start:start + HIST]).then_inc(frames_taken, 1)
                    dve.wait_ge(frames_taken, h * 9 + 3 * (ch + 1))
                    dve.wait_ge(taps_taken, h + 1)
                    nc.vector.tensor_scalar(out, src[:, 0:CW], hw[:, ch:ch + 1], None,
                                            ALU.mult).then_inc(conv_steps, 1)
                    return
                dve.wait_ge(conv_steps, h * 9 + (3 * ch + tap))
                nc.vector.scalar_tensor_tensor(
                    out=out, in0=src[:, tap:tap + CW], scalar=hw[:, tap * 3 + ch:tap * 3 + ch + 1],
                    in1=out, op0=ALU.mult, op1=ALU.add).then_inc(conv_done if tap == TAPS - 1 else conv_steps, 1)

            def scale(h, i):
                cols = slice(i % 3 * CU, (i % 3 + 1) * CU)
                dve.wait_ge(rs_done, h * 6 + (i + 1))
                nc.vector.tensor_tensor(qkv[:, i // 3, cols], conv[:, i // 3, cols], rs[:, i % 2],
                                        ALU.mult).then_inc(unit_len, 1)

            def prepare(t, r):
                par = r % 2
                dve.wait_ge(prep_done, t * 15 + (5 * r + 1))
                for i in range(BATCHES):
                    c = 3 * r + i
                    op = nc.vector.scalar_tensor_tensor(out=gam[:, i], in0=ps[:, 2, i * P:(i + 1) * P],
                                                        scalar=hg[:, 1, c:c + 1], in1=tk.later_neg[:],
                                                        op0=ALU.subtract, op1=ALU.add)
                op.then_inc(e_done, 1)
                if r == 2:
                    dve.wait_ge(chain, t * 27 + 9)
                for i in range(BATCHES):
                    c = 3 * r + i
                    op = nc.vector.tensor_scalar(z[:, par, :, i], tk.ident[:][:, None, :].to_broadcast([P, 2, P]),
                                                 hg[:, 0, c:c + 1], -1.0, ALU.mult, ALU.mult)
                op.then_inc(z_done, 1)
                dve.wait_ge(gam_done, t * 3 + (r + 1))
                dve.wait_ge(prep_done, t * 15 + (5 * r + 3))
                if r > 0:
                    dve.wait_ge(level_masked, t * 21 + 7 * r)
                grid = lambda bank: ps[:, bank, 0:3 * P].rearrange("p (i c) -> p i c", i=3)
                nc.vector.tensor_tensor(mt[:], grid(3), gam[:], ALU.mult).then_inc(made, 1)
                nc.vector.tensor_tensor(att[:, par], grid(4), gam[:], ALU.mult).then_inc(made, 1)
                dve.wait_ge(expd_done, t * 3 + (r + 1))
                if r < 2:
                    op = nc.vector.tensor_tensor(qd[:, par].rearrange("p i c -> p (i c)"),
                                                 qkv[:, 0, 3 * r * P:(3 * r + 3) * P],
                                                 exp_d[:].rearrange("p i c -> p (i c)"), ALU.mult)
                else:
                    for i in range(BATCHES):
                        op = nc.vector.tensor_tensor(qd[:, par, i], qkv[:, 0, tile_cols(3 * r + i)], exp_d[:, i], ALU.mult)
                op.then_inc(made, 1)

            def join(t, r, l):
                par, i = r % 2, r * LEVELS + l
                flat = lambda h: z[:, par, h].rearrange("p i c -> p (i c)")
                dve.wait_ge(z_done, t * 24 + (8 * r + l + 1))
                if l == 0:
                    dve.wait_ge(wz_copied, t * 21 + (i + 1))
                    for j in range(BATCHES):
                        c = 3 * r + j
                        op = nc.vector.scalar_tensor_tensor(out=z[:, par, 0, j], in0=wz[:, j], scalar=hg[:, 0, c:c + 1],
                                                            in1=z[:, par, 0, j], op0=ALU.mult, op1=ALU.add)
                    op.then_inc(z_first, 1)
                elif l < LEVELS - 1:
                    dve.wait_ge(pz_done, t * 36 + (12 * r + 2 * l))
                    nc.vector.tensor_tensor(flat(0), flat(0), ps[:, 4, 0:3 * P], ALU.subtract).then_inc(z_first, 1)
                dve.wait_ge(pz_done, t * 36 + (12 * r + min(2 * l + 1, 12)))
                nc.vector.tensor_tensor(flat(1), flat(1), ps[:, 5, 0:3 * P], ALU.subtract).then_inc(z_done, 1)

            def chain_step(t, r, s):
                par, i = r % 2, s // 3
                c = 3 * r + i
                g = c // 8
                if s % 3 == 0:
                    dve.wait_ge(chain, t * 27 + (3 * c + 1))
                    dve.wait_ge(tok_done, t * 6 + (2 * r + 2))
                    nc.vector.scalar_tensor_tensor(out=y[:], in0=ps[:, 6, 0:P], scalar=hg[:, 2, c:c + 1],
                                                   in1=v_tok[:, par, i], op0=ALU.mult, op1=ALU.add).then_inc(y_done, 1)
                elif s % 3 == 2:
                    dve.wait_ge(chain, t * 27 + (3 * c + 3))
                    dve.wait_ge(s_done, t * 9 + c) if c else dve.wait_ge(s_init, t + 1)
                    nc.vector.scalar_tensor_tensor(out=state[:, g], in0=state[:, g], scalar=hg[:, 4, c:c + 1],
                                                   in1=ps[:, 6, 2 * P:3 * P], op0=ALU.mult, op1=ALU.add).then_inc(s_done, 1)

            def finish(t, n):
                dve.wait_ge(ors_done, t * 3 + (n + 1))
                cols = o[:, unit_cols(n)]
                nc.vector.scalar_tensor_tensor(out=cols, in0=cols, scalar=gain[:, 0:1], in1=o_work[n],
                                               op0=ALU.mult, op1=ALU.mult).then_inc(o_normed, 1)
                dve.wait_ge(z_silu_done, t * 3 + (n + 1))
                dve.wait_ge(o_normed, t * 3 + (n + 1))
                dst = tk.x[:, bass.ds(t, 1), unit_cols(n)].rearrange("p a t -> p (a t)")
                nc.vector.tensor_tensor(dst, dst, cols, ALU.mult).then_inc(final_done, 1)

            def head(t, more):
                for r in range(BATCHES + 1):
                    if r < BATCHES:
                        prepare(t, r)
                    for l in range(LEVELS):
                        if r > 0 and 2 * l < 9:
                            chain_step(t, r - 1, 2 * l)
                        if r < BATCHES:
                            join(t, r, l)
                        if r > 0 and 2 * l + 1 < 9:
                            chain_step(t, r - 1, 2 * l + 1)
                        if (r, l) == (0, 2):
                            dve.wait_ge(s_out, t * 32 + 32)
                            nc.vector.memset(state[:, 0], 0.0).then_inc(s_init, 1)
                            if more:
                                take_taps(t + 1)
                        if more and (r, l) in taps:
                            if (r, l) == (2, 1):
                                dve.wait_ge(prep_done, t * 15 + 15)
                            convolve(t + 1, *taps[r, l])
                        if more and r == BATCHES:
                            for i in SCALED[l]:
                                if i == 3:
                                    dve.wait_ge(chain, t * 27 + 25)
                                scale(t + 1, i)
                finish(t, 0)
                if more:
                    dve.wait_ge(tok_done, t * 6 + 6)
                    take_columns(t + 1)
                finish(t, 1)
                finish(t, 2)

            take_taps(0)
            take_columns(0)
            for ch in range(3):
                for tap in range(TAPS):
                    convolve(0, ch, tap)
            for i in range(6):
                scale(0, i)
            with dve.Fori(0, HEADS - 1) as t:
                head(t, True)
            head(HEADS - 1, False)

            for g in range(2):
                dve.wait_ge(tails_turned, g + 1)
                nc.vector.tensor_copy(tail_rows[0:R, g], ps[0:R, g, 0:P]).then_inc(tails_copied, 1)


def gdn_prologue(nc, tk, a, w_in, ws, gates, conv_w, hist, gain, raw, qkv, rows, ab_t):
    ps = tk.ps
    R, RH = TAPS * 3 * HEADS, HIST * 3 * HEADS
    with ExitStack() as ctx:
        sem = semaphores(nc, ctx, "gdnp")
        buf = lambda s, *sh: ctx.enter_context(nc.sbuf_tensor(f"gdnp_{s}", *sh))
        ab = buf("ab", [P, TILES, 2 * HEADS], F32)
        rate = buf("rate", [P, HEADS], F32)
        dtb = buf("dtb", [P, HEADS], F32)
        tmp = buf("tmp", [P, 4, TILES, HEADS], F32)
        small_in, w_landed = sem("small_in"), sem("w_landed")
        zeroed, w_hi, w_split = sem("zeroed"), sem("w_hi"), sem("w_split")
        turned, copied, ab_done, ab_copied = sem("turned"), sem("copied"), sem("ab_done"), sem("ab_copied")
        step = sem("gate_steps")
        H = HEADS
        block = ctx.enter_context(nc.Block())

        @block.sync
        def _(sp):
            sp.wait_ge(zeroed, 5)
            sp.dma_start(ws.stage[:, 0, :, 0:2 * H], w_in[:, :, 4 * D:4 * D + 2 * H]).then_inc(w_landed, 16)
            sp.dma_start(rows[0:R, 0], a["gdn_conv_w"][0].rearrange("f (r c) -> (f r) c", c=P)).then_inc(small_in, 16)
            sp.dma_start(rows[0:RH, 1], a["state_gdn_conv"][0, 0].rearrange("f (r c) -> (f r) c", c=P)).then_inc(small_in, 16)
            sp.dma_start(gain[:], a["gdn_norm"].rearrange("a p -> p a"), allow_slow_non_contiguous=True).then_inc(small_in, 16)
            sp.dma_start(rate[:], a["gdn_a_log"].to_broadcast([P, H])).then_inc(small_in, 16)
            sp.dma_start(dtb[:], a["gdn_dt_bias"].to_broadcast([P, H])).then_inc(small_in, 16)
            sp.wait_ge(small_in, 80)

        @block.gpsimd
        def _(pool):
            nc.gpsimd.memset(raw[:, :, 0:HIST], 0.0).then_inc(zeroed, 1)
            nc.gpsimd.memset(qkv[:, :, CW:CPAD], 0.0).then_inc(zeroed, 1)
            nc.gpsimd.memset(ab_t[:, TOK:TILES * P], -80.0).then_inc(zeroed, 1)
            nc.gpsimd.memset(ws.hi[:, 0].bitcast(F32), 0.0).then_inc(zeroed, 1)
            nc.gpsimd.memset(ws.lo[:, 0].bitcast(F32), 0.0).then_inc(zeroed, 1)
            pool.wait_ge(zeroed, 5)
            pool.wait_ge(w_landed, 16)
            st = ws.stage[:, 0, :, 0:2 * H]
            nc.gpsimd.tensor_tensor(ws.hi[:, 0, :, 0:2 * H], st,
                                    tk.one[:][:, :, None].to_broadcast([P, KB, 2 * H]), ALU.mult).then_inc(w_hi, 1)
            pool.wait_ge(w_hi, 1)
            nc.gpsimd.tensor_tensor(ws.lo[:, 0, :, 0:2 * H], st, ws.hi[:, 0, :, 0:2 * H].bitcast(F32),
                                    ALU.subtract).then_inc(w_split, 1)

        @block.tensor
        def _(pe):
            pe.wait_ge(small_in, 80)
            pe.transpose(ps[:, 4, 0:R], rows[0:R, 0], tk.ident[0:R, 0:R]).then_inc(turned, 1)
            pe.transpose(ps[:, 5, 0:RH], rows[0:RH, 1], tk.ident[0:RH, 0:RH]).then_inc(turned, 1)
            pe.wait_ge(w_split, 1)
            for n in range(NU):
                for k in range(KB):
                    mm = split_product(pe, ps[:, n, 0:UNIT], ws.hi[:, 0, k], ws.lo[:, 0, k],
                                       tk.hi[:, k, unit_cols(n)], tk.lo[:, k, unit_cols(n)], k == 0, k == KB - 1)
                mm.then_inc(ab_done, 1)
            pe.wait_ge(ab_copied, NU)
            pe.wait_ge(zeroed, 5)
            for c in range(TILES):
                mm = pe.transpose(ps[:, 3, c * 2 * H:(c + 1) * 2 * H], ab_t[:, c * P:(c + 1) * P],
                                  tk.ident[0:2 * H, 0:2 * H])
            mm.then_inc(step, 1)
            pe.wait_ge(step, 15)
            g = gates[:, 5].rearrange("p c h -> p (c h)")
            pe.matmul(ps[:, 6, 0:TILES * H], tk.upto[:], g, start=True, stop=True)
            pe.matmul(ps[:, 7, 0:TILES * H], tk.ones[:], g, start=True, stop=True).then_inc(step, 1)

        @block.scalar
        def _(act):
            def do(n, *args, **kw):
                if n == 5:
                    nc.scalar.preload_act_table_set("natural_log_exp_and_others")
                act.wait_ge(step, n - 1)
                nc.scalar.activation(*args, **kw).then_inc(step, 1)
            do(5, tmp[:, 1], tmp[:, 1], ACT.Exp)
            do(6, tmp[:, 1], tmp[:, 1], ACT.Ln, bias=tk.one[:, 0:1])
            do(8, rate[:], rate[:], ACT.Exp)
            do(11, tmp[:, 2], ab[:, :, H:2 * H], ACT.Exp, scale=-1.0)
            do(19, tmp[:, 0], gates[:, 1], ACT.Exp)
            do(20, gates[:, 3], gates[:, 3], ACT.Exp)
            do(22, gates[:, 4], ps[:, 7, 0:TILES * H].rearrange("p (c h) -> p c h", c=TILES), ACT.Exp)

        @block.vector
        def _(dve):
            def after(n):
                dve.wait_ge(step, n - 1)
            dve.wait_ge(turned, 2)
            nc.vector.tensor_copy(conv_w[:].rearrange("p f h -> p (f h)"), ps[:, 4, 0:R]).then_inc(copied, 1)
            nc.vector.tensor_copy(hist[:].rearrange("p f h -> p (f h)"), ps[:, 5, 0:RH]).then_inc(copied, 1)
            for n in range(NU):
                dve.wait_ge(ab_done, n + 1)
                nc.vector.tensor_copy(ab_t[:, unit_cols(n)], ps[0:2 * H, n, 0:UNIT]).then_inc(ab_copied, 1)
            dve.wait_ge(small_in, 80)
            after(2)
            nc.vector.tensor_copy(ab[:].rearrange("p c h -> p (c h)"), ps[:, 3, 0:TILES * 2 * H]).then_inc(step, 1)
            after(3)
            nc.vector.tensor_tensor(tmp[:, 0], ab[:, :, 0:H], dtb[:][:, None, :].to_broadcast([P, TILES, H]),
                                    ALU.add).then_inc(step, 1)
            after(4)
            nc.vector.tensor_scalar(tmp[:, 3], tmp[:, 0], 0.0, None, ALU.max).then_inc(copied, 1)
            dve.wait_ge(copied, 3)
            nc.vector.scalar_tensor_tensor(out=tmp[:, 1], in0=tmp[:, 3], scalar=-2.0, in1=tmp[:, 0],
                                           op0=ALU.mult, op1=ALU.add).then_inc(step, 1)
            after(7)
            nc.vector.tensor_tensor(tmp[:, 0], tmp[:, 3], tmp[:, 1], ALU.add).then_inc(step, 1)
            after(9)
            nc.vector.scalar_tensor_tensor(out=gates[:, 5], in0=tmp[:, 0], scalar=-1.0,
                                           in1=rate[:][:, None, :].to_broadcast([P, TILES, H]),
                                           op0=ALU.mult, op1=ALU.mult).then_inc(step, 1)
            after(10)
            nc.vector.tensor_scalar(gates[:, 5, TILES - 1], gates[:, 5, TILES - 1],
                                    tk.upto[:, SAMPLE - 1:SAMPLE], None, ALU.mult).then_inc(step, 1)
            after(12)
            nc.vector.tensor_scalar(tmp[:, 3], tmp[:, 2], 1.0, -1.0, ALU.add, ALU.mult).then_inc(step, 1)
            after(13)
            nc.vector.reciprocal(gates[:, 0], tmp[:, 3]).then_inc(step, 1)
            after(14)
            nc.vector.tensor_scalar(gates[:, 0, TILES - 1], gates[:, 0, TILES - 1],
                                    tk.upto[:, SAMPLE - 1:SAMPLE], None, ALU.mult).then_inc(step, 2)
            after(17)
            nc.vector.tensor_copy(gates[:, 1].rearrange("p c h -> p (c h)"), ps[:, 6, 0:TILES * H]).then_inc(step, 1)
            after(18)
            nc.vector.scalar_tensor_tensor(out=gates[:, 3].rearrange("p c h -> p (c h)"),
                                           in0=gates[:, 1].rearrange("p c h -> p (c h)"), scalar=-1.0,
                                           in1=ps[:, 7, 0:TILES * H], op0=ALU.mult, op1=ALU.add).then_inc(step, 1)
            after(21)
            nc.vector.tensor_scalar(gates[:, 2], tmp[:, 0], -1.0, None, ALU.mult).then_inc(step, 1)
            dve.wait_ge(step, 22)


def mlstm_phase(nc, tk, a):
    ps = tk.ps
    B = 3
    U = B * NU
    FILL = (3, 4, 4, 4)
    W_QK = HEADS * MDK
    w_in = a["ml_w_in"][0].rearrange("(k p) f -> p k f", p=P)
    NQ = 5
    with ExitStack() as ctx:
        sem = semaphores(nc, ctx, "ml", again=True)
        buf = lambda s, *sh: ctx.enter_context(nc.sbuf_tensor(f"ml_{s}", *sh))
        ws = WeightStream(nc, tk, ctx, sem, "ml", 3, stages=3)
        gates = buf("gates", [P, NQ + 1, TILES, HEADS], F32)
        gain = buf("gain", [P, HEADS], F32)
        m_end = buf("m_end", [P, 2, HEADS], F32)
        raw = buf("raw", [P, 3, TOK], F32)
        qkv = buf("qkv", [P, 3, TILES * P], F32)
        hg = buf("head_gates", [P, NQ + 1, TILES], F32)
        hgain = buf("head_gain", [P, 1], F32)
        num = buf("num", [P, TILES * P], F32)
        den = buf("den", [P, TILES * P], F32)
        sq = buf("sq", [P, 2, UNIT], F32)
        rs = buf("rs", [P, NU, UNIT], F32)
        pe_exp = buf("exponents", [P, BATCHES, P], F32)
        q_scale = buf("q_scale", [P, BATCHES, P], F32)
        floor = buf("floor", [P, 2, BATCHES, P], F32)
        pt = buf("pt", [P, 2, BATCHES, P], F32)
        qs = buf("qs", [MDK, 2, BATCHES, P], F32)
        kw = buf("kw", [P, 2, BATCHES, MDK], F32)
        v_tok = buf("v_tok", [P, 2, BATCHES, DV + 1], F32)
        state = buf("state", [MDK, 2, DV + 1], F32)

        mlstm_prologue(nc, tk, a, w_in, ws, gates, gain, m_end, qkv, v_tok, num[0:2 * HEADS])
        unit_done, evacuated = sem("unit_done"), sem("evacuated")
        taken, cols_done, gain_taken, gated = sem("raw_taken"), sem("cols_done"), sem("gain_taken"), sem("sigmoid_done")
        prep_done, qsc_done, e_done, exp_done = sem("prep_done"), sem("q_scale_done"), sem("e_done"), sem("exp_done")
        floor_done, tok_done, made = sem("floor_done"), sem("tok_done"), sem("p_and_q_made")
        chain, num_done, den_done, s_done = sem("chain"), sem("num_done"), sem("den_done"), sem("s_done")
        s_in, s_out, s_init = sem("state_landed"), sem("state_stored"), sem("state_zeroed")
        sq_done, ss_done, v_done, ln_done, rs_done = (sem("sq_done"), sem("ss_done"), sem("v_done"), sem("ln_done"),
                                                      sem("rs_done"))
        negative_done, den2_done, clamped = sem("negative_done"), sem("den2_done"), sem("clamped")
        o_normed, final_done, m_out = sem("o_normed"), sem("final_done"), sem("m_stored")
        block = ctx.enter_context(nc.Block())

        @block.sync
        def _(sp):
            def weights(t, ahead, b):
                if b == 0:
                    ws.wait_stage(sp, t * B + ahead * B)
                    for h in range(2):
                        sp.dma_start(ws.stage[:, 0, :, h * MDK:(h + 1) * MDK],
                                     w_in[:, :, bass.ds(t * MDK + (ahead * MDK + h * W_QK), MDK)]).then_inc(ws.landed[0], 16)
                else:
                    start = 2 * W_QK + (b - 1) * D + ahead * P
                    ws.load(sp, t * B + (ahead * B + b), b, w_in[:, :, bass.ds(t * P + start, P)])

            def states(t):
                sp.dma_start(state[:, 1, 0:DV], a["state_mlstm_C"][0, 0, t]).then_inc(s_in, 16)
                sp.dma_start(state[:, 1, DV:DV + 1], a["state_mlstm_n"][0, 0, t][:, None]).then_inc(s_in, 16)

            def store(t):
                sp.wait_ge(s_done, t * 9 + 9)
                sp.sem_inc(ws.checked, 1)
                for g, name in enumerate(("p", "s")):
                    sp.dma_start(a[f"{name}_C"][0, 0, t], state[:, g, 0:DV]).then_inc(s_out, 16)
                    sp.dma_start(a[f"{name}_n"][0, 0, t][:, None], state[:, g, DV:DV + 1]).then_inc(s_out, 16)

            for g, name in enumerate(("p", "s")):
                sp.dma_start(a[f"{name}_m"][0], m_end[0:1, g]).then_inc(m_out, 16)
            def head(t, ahead):
                for b in range(1, B) if ahead >= 1 else ():
                    weights(t, 1, b)
                if ahead == 2:
                    weights(t, 2, 0)
                store(t)
                if ahead >= 1:
                    sp.wait_ge(s_out, t * 64 + 128)
                    sp.sem_inc(ws.checked, 1)
                    states(t + 1)

            for b in range(B):
                weights(0, 0, b)
            states(0)
            weights(0, 1, 0)
            with sp.Fori(0, HEADS - 2) as t:
                head(t, 2)
            head(HEADS - 2, 1)
            head(HEADS - 1, 0)
            sp.wait_ge(s_out, HEADS * 64 + 64)
            sp.wait_ge(m_out, 32)

        @block.gpsimd
        def _(pool):
            ws.start(pool)
            pool.sem_inc(evacuated, 2)
            pool.sem_inc(s_out, 64)

            def weights(t, ahead, b):
                if ahead >= 1:
                    pool.wait_ge(unit_done, t * U + ((ahead - 1) * U + NU * (b + 1)))
                dmas = 32 if b == 0 else 16
                ws.split(pool, t * B + (ahead * B + b), b, t * dmas + (ahead * dmas + dmas), b)

            for b in range(B):
                weights(0, 0, b)
            weights(0, 1, 0)
            with pool.Fori(0, HEADS - 2) as t:
                for ahead, b in ((1, 1), (1, 2), (2, 0)):
                    weights(t, ahead, b)
            for b in range(1, B):
                weights(HEADS - 2, 1, b)

        @block.tensor
        def _(pe):
            def piece(t, n):
                u, third = n // 3, n % 3
                b, cols = u // NU, unit_cols(u % NU)
                if n % 9 == 0:
                    ws.wait_ready(pe, t * B + b)
                if third == 0:
                    pe.wait_ge(evacuated, t * U + max(u + 1, 2))
                for k in range(3 * third, min(3 * third + 3, KB)):
                    mm = split_product(pe, ps[:, u % 2, 0:UNIT], ws.hi[:, b, k], ws.lo[:, b, k],
                                       tk.hi[:, k, cols], tk.lo[:, k, cols], k == 0, k == KB - 1)
                if third == 2:
                    mm.then_inc(unit_done, 1)

            def rows_of(bank, q, r):
                for i in range(BATCHES):
                    c = 3 * r + i
                    mm = pe.matmul(ps[:, bank, i * P:(i + 1) * P], hg[:, q, c:c + 1].to_broadcast([P, P]),
                                   tk.ident[:], start=True, stop=True)
                mm.then_inc(prep_done, 1)

            def prepare(t, r, pieces):
                if r > 0:
                    pe.wait_ge(tok_done, t * 6 + 2 * r)
                rows_of(2, 1, r)
                if r > 0:
                    pe.wait_ge(made, t * 6 + 2 * r)
                for i in range(BATCHES):
                    cols = slice((3 * r + i) * P, (3 * r + i + 1) * P)
                    mm = pe.matmul(ps[:, 3, i * P:(i + 1) * P], qkv[0:MDK, 1, cols], qkv[0:MDK, 0, cols],
                                   start=True, stop=True)
                mm.then_inc(prep_done, 1)
                if r > 0:
                    pe.wait_ge(floor_done, t * 3 + r)
                rows_of(4, 2, r)
                for i in range(BATCHES):
                    mm = pe.transpose(ps[:, 5, i * MDK:(i + 1) * MDK], qkv[0:MDK, 1, (3 * r + i) * P:(3 * r + i + 1) * P],
                                      tk.ident[0:MDK, 0:MDK])
                mm.then_inc(prep_done, 1)
                pieces(2)
                pe.wait_ge(qsc_done, t * 3 + (r + 1))
                pe.wait_ge(e_done, t * 3 + (r + 1))
                for i in range(BATCHES):
                    mm = pe.transpose(ps[:, 2, i * P:(i + 1) * P], qkv[:, 2, (3 * r + i) * P:(3 * r + i + 1) * P], tk.ident[:])
                mm.then_inc(prep_done, 1)

            def chunk(t, r, i):
                par, c = r % 2, 3 * r + i
                g = c // 8
                if i == 0:
                    pe.wait_ge(made, t * 6 + (2 * r + 2))
                    pe.wait_ge(tok_done, t * 6 + (2 * r + 2))
                if c == 0:
                    pe.wait_ge(s_init, t + 1)
                else:
                    pe.wait_ge(s_done, t * 9 + c)
                    pe.wait_ge(num_done, t * 9 + c)
                if c == 8:
                    pe.wait_ge(s_in, t * 32 + 32)
                pe.matmul(ps[:, 6, 0:P], state[:, g, 0:DV], qs[:, par, i], start=True, stop=False)
                pe.matmul(ps[:, 6, 0:P], v_tok[:, par, i, 0:DV], pt[:, par, i], start=False, stop=True).then_inc(chain, 1)
                pe.matmul(ps[:, 7, 0:P], state[:, g, DV:DV + 1].to_broadcast([MDK, P]), qs[:, par, i],
                          start=True, stop=False)
                pe.matmul(ps[:, 7, 0:P], tk.ones[:], pt[:, par, i], start=False, stop=True)
                pe.matmul(ps[0:MDK, 7, P:2 * P + 1], kw[:, par, i], v_tok[:, par, i],
                          start=True, stop=True).then_inc(chain, 1)

            def sums(t, n):
                pe.wait_ge(sq_done, t * 3 + (n + 1))
                if n == 0:
                    pe.wait_ge(num_done, t * 9 + 9)
                    pe.wait_ge(s_done, t * 9 + 9)
                if n == 2:
                    pe.wait_ge(v_done, t * 3 + 1)
                pe.matmul(ps[:, 6 + n % 2, 0:UNIT], tk.ones[:], sq[:, n % 2], start=True, stop=True).then_inc(ss_done, 1)

            def head(t, more):
                n = 0

                def pieces(count):
                    nonlocal n
                    for _ in range(count if more else 0):
                        piece(t + 1, n)
                        n += 1

                pe.wait_ge(cols_done, t + 1)
                pe.wait_ge(taken, t * 3 + 3)
                for r in range(BATCHES + 1):
                    if r < BATCHES:
                        prepare(t, r, pieces)
                    for i in range(BATCHES):
                        pieces(FILL[r] // BATCHES + (i < FILL[r] % BATCHES))
                        if r > 0:
                            chunk(t, r - 1, i)
                for u in range(NU):
                    pieces(2)
                    sums(t, u)

            for n in range(27):
                piece(0, n)
            with pe.Fori(0, HEADS - 1) as t:
                head(t, True)
            head(HEADS - 1, False)

        @block.scalar
        def _(act):
            def evacuate(t, u, first):
                act.wait_ge(unit_done, t * U + (u + 1))
                b, n = u // NU, u % NU
                src = ps[:, u % 2, 0:UNIT]
                if b == 2:
                    dst = tk.x[:, bass.ds(t, 1), unit_cols(n)].rearrange("p a t -> p (a t)")
                    act.sem_inc(ws.act_checked, 1)
                    nc.scalar.copy(dst, src).then_inc(evacuated, 1)
                    return
                if not first:
                    act.wait_ge(taken, (t - 1) * 3 + (2 + b))
                if b == 0:
                    nc.scalar.copy(raw[0:MDK, 0, unit_cols(n)], src[0:MDK])
                    nc.scalar.copy(raw[0:MDK, 1, unit_cols(n)], src[MDK:P]).then_inc(evacuated, 1)
                else:
                    nc.scalar.copy(raw[:, 2, unit_cols(n)], src).then_inc(evacuated, 1)

            def gate(t, n):
                act.wait_ge(evacuated, t * U + (2 + 2 * NU + n + 1))
                act.sem_inc(ws.act_checked, 1)
                place = tk.x[:, bass.ds(t, 1), unit_cols(n)].rearrange("p a t -> p (a t)")
                nc.scalar.activation(place, place, ACT.Sigmoid).then_inc(gated, 1)

            def prepare(t, r, pieces):
                par = r % 2
                grid = lambda bank: ps[:, bank, 0:3 * P].rearrange("p (i c) -> p i c", i=3)
                act.wait_ge(prep_done, t * 15 + (5 * r + 1))
                if r > 0:
                    act.wait_ge(made, t * 6 + 2 * r)
                for i in range(BATCHES):
                    c = 3 * r + i
                    op = nc.scalar.activation(q_scale[:, i], ps[:, 2, i * P:(i + 1) * P], ACT.Exp,
                                              bias=hg[:, 4, c:c + 1], scale=-1.0)
                op.then_inc(qsc_done, 1)
                act.wait_ge(e_done, t * 3 + (r + 1))
                nc.scalar.activation(pe_exp[:], pe_exp[:], ACT.Exp, scale=-1.0).then_inc(exp_done, 1)
                act.wait_ge(prep_done, t * 15 + (5 * r + 3))
                if r == 2:
                    act.wait_ge(den_done, t * 9 + 3)
                    act.wait_ge(chain, t * 18 + 6)
                nc.scalar.activation(floor[:, par], grid(4), ACT.Exp, scale=-1.0).then_inc(floor_done, 1)
                act.wait_ge(prep_done, t * 15 + (5 * r + 4))
                for i in range(BATCHES):
                    c = 3 * r + i
                    op = nc.scalar.mul(kw[:, par, i], ps[:, 5, i * MDK:(i + 1) * MDK], hg[:, 3, c:c + 1])
                op.then_inc(tok_done, 1)
                pieces(2)
                act.wait_ge(prep_done, t * 15 + (5 * r + 5))
                nc.scalar.copy(v_tok[:, par, :, 0:DV], grid(2)).then_inc(tok_done, 1)

            def chunk(t, r, i):
                c = 3 * r + i
                act.wait_ge(chain, t * 18 + (2 * c + 1))
                nc.scalar.copy(num[:, c * P:(c + 1) * P], ps[:, 6, 0:P]).then_inc(num_done, 1)

            def head(t, more):
                n = 0

                def pieces(count):
                    nonlocal n
                    for _ in range(count if more else 0):
                        if n % 3 == 2:
                            evacuate(t + 1, n // 3, False)
                        n += 1

                act.wait_ge(cols_done, t + 1)
                for r in range(BATCHES + 1):
                    if r < BATCHES:
                        prepare(t, r, pieces)
                    for i in range(BATCHES):
                        pieces(FILL[r] // BATCHES + (i < FILL[r] % BATCHES))
                        if r > 0:
                            chunk(t, r - 1, i)
                        if (r, i) == (2, 0):
                            for u in range(NU):
                                gate(t, u)
                            nc.scalar.preload_act_table_set("natural_log_exp_and_others")
                act.wait_ge(num_done, t * 9 + 9)
                act.wait_ge(den_done, t * 9 + 9)
                nc.scalar.activation(den[:, 0:TOK], den[:, 0:TOK], ACT.Square,
                                     scale=math.sqrt(DV * RMS_EPS)).then_inc(den2_done, 1)
                for u in range(NU):
                    if u >= 2:
                        act.wait_ge(ss_done, t * 3 + (u - 1))
                    nc.scalar.activation(sq[:, u % 2], num[:, unit_cols(u)], ACT.Square).then_inc(sq_done, 1)
                    pieces(2)
                for u in range(NU):
                    act.wait_ge(clamped, t * 3 + (u + 1))
                    nc.scalar.activation(rs[:, u], rs[:, u], ACT.Ln, scale=1.0 / DV).then_inc(ln_done, 1)
                    act.wait_ge(ln_done, t * 3 + (u + 1))
                    nc.scalar.activation(rs[:, u], rs[:, u], ACT.Exp, scale=-0.5).then_inc(rs_done, 1)

            nc.scalar.preload_act_table_set("natural_log_exp_and_others")
            for u in range(U):
                evacuate(0, u, True)
            with act.Fori(0, HEADS - 1) as t:
                head(t, True)
            head(HEADS - 1, False)

        @block.vector
        def _(dve):
            def take(dst, src):
                return nc.vector.tensor_scalar(dst, src, 1.0, None, ALU.mult)

            def prepare(t, r):
                par = r % 2
                dve.wait_ge(prep_done, t * 15 + (5 * r + 1))
                dve.wait_ge(qsc_done, t * 3 + (r + 1))
                for i in range(BATCHES):
                    c = 3 * r + i
                    op = nc.vector.scalar_tensor_tensor(out=pe_exp[:, i], in0=ps[:, 2, i * P:(i + 1) * P],
                                                        scalar=hg[:, 0, c:c + 1], in1=tk.later_neg[:],
                                                        op0=ALU.subtract, op1=ALU.subtract)
                op.then_inc(e_done, 1)
                dve.wait_ge(exp_done, t * 3 + (r + 1))
                dve.wait_ge(prep_done, t * 15 + (5 * r + 2))
                if r == 2:
                    dve.wait_ge(chain, t * 18 + 6)
                nc.vector.scalar_tensor_tensor(out=pt[:, par].rearrange("p i c -> p (i c)"), in0=ps[:, 3, 0:3 * P],
                                               scalar=MDK ** -0.5, in1=pe_exp[:].rearrange("p i c -> p (i c)"),
                                               op0=ALU.mult, op1=ALU.mult).then_inc(made, 1)
                nc.vector.tensor_tensor(qs[:, par].rearrange("p i c -> p (i c)"),
                                        qkv[0:MDK, 0, 3 * r * P:(3 * r + 3) * P],
                                        q_scale[0:MDK].rearrange("p i c -> p (i c)"), ALU.mult).then_inc(made, 1)

            def chunk(t, r, i):
                par, c = r % 2, 3 * r + i
                g = c // 8
                dve.wait_ge(chain, t * 18 + (2 * c + 2))
                dve.wait_ge(s_done, t * 9 + c) if c else dve.wait_ge(s_init, t + 1)
                nc.vector.scalar_tensor_tensor(out=state[:, g], in0=state[:, g], scalar=hg[0:MDK, 5, c:c + 1],
                                               in1=ps[0:MDK, 7, P:2 * P + 1], op0=ALU.mult, op1=ALU.add)
                dve.wait_ge(floor_done, t * 3 + (r + 1))
                part = den[:, c * P:(c + 1) * P]
                nc.vector.scalar_tensor_tensor(out=part, in0=ps[:, 7, 0:P], scalar=-1.0, in1=floor[:, par, i],
                                               op0=ALU.mult, op1=ALU.max).then_inc(negative_done, 1)
                dve.wait_ge(negative_done, t * 9 + (c + 1))
                nc.vector.tensor_tensor(part, part, ps[:, 7, 0:P], ALU.max).then_inc(den_done, 1)
                dve.wait_ge(den_done, t * 9 + (c + 1))
                dve.sem_inc(s_done, 1)

            def take_columns(h):
                take(hg[:].rearrange("p q c -> p (q c)"),
                     gates[:, :, :, bass.ds(h, 1)].rearrange("p q c a -> p (q c a)")).then_inc(cols_done, 1)

            def take_raw(h, j):
                rows = P if j == 2 else MDK
                dve.wait_ge(evacuated, h * U + (2 + NU * (2 if j == 2 else 1)))
                nc.vector.tensor_copy(qkv[0:rows, j, 0:TOK], raw[0:rows, j]).then_inc(taken, 1)

            def head(t, more):
                for r in range(BATCHES + 1):
                    if r < BATCHES:
                        prepare(t, r)
                    if r == 0:
                        take(hgain[:], gain[:, bass.ds(t, 1)]).then_inc(gain_taken, 1)
                        dve.wait_ge(s_out, t * 64 + 64)
                        nc.vector.memset(state[:, 0], 0.0).then_inc(s_init, 1)
                    for i in range(BATCHES):
                        if r > 0:
                            chunk(t, r - 1, i)
                        if more and (r, i) == (2, 2):
                            dve.wait_ge(prep_done, t * 15 + 15)
                            take_raw(t + 1, 0)
                            take_raw(t + 1, 1)
                        if more and (r, i) == (3, 1):
                            take_raw(t + 1, 2)
                if more:
                    dve.wait_ge(tok_done, t * 6 + 6)
                    take_columns(t + 1)
                for n in range(NU):
                    dve.wait_ge(ss_done, t * 3 + (n + 1))
                    dve.wait_ge(den2_done, t + 1)
                    nc.vector.tensor_tensor(rs[:, n], ps[:, 6 + n % 2, 0:UNIT], den[:, unit_cols(n)],
                                            ALU.add).then_inc(v_done, 1)
                    dve.wait_ge(v_done, t * 3 + (n + 1))
                    nc.vector.tensor_scalar(rs[:, n], rs[:, n], 1e-16, 1e19, ALU.max, ALU.min).then_inc(clamped, 1)
                dve.wait_ge(gain_taken, t + 1)
                for n in range(NU):
                    dve.wait_ge(rs_done, t * 3 + (n + 1))
                    cols = num[:, unit_cols(n)]
                    nc.vector.scalar_tensor_tensor(out=cols, in0=cols, scalar=hgain[:, 0:1], in1=rs[:, n],
                                                   op0=ALU.mult, op1=ALU.mult).then_inc(o_normed, 1)
                    dve.wait_ge(gated, t * 3 + (n + 1))
                    dve.wait_ge(o_normed, t * 3 + (n + 1))
                    dst = tk.x[:, bass.ds(t, 1), unit_cols(n)].rearrange("p a t -> p (a t)")
                    nc.vector.tensor_tensor(dst, dst, cols, ALU.mult).then_inc(final_done, 1)

            take_columns(0)
            for j in range(3):
                take_raw(0, j)
            with dve.Fori(0, HEADS - 1) as t:
                head(t, True)
            head(HEADS - 1, False)


def mlstm_prologue(nc, tk, a, w_in, ws, gates, gain, m_end, qkv, v_tok, ab_t):
    ps = tk.ps
    H = HEADS
    R = TILES * H
    with ExitStack() as ctx:
        sem = semaphores(nc, ctx, "mlp")
        buf = lambda s, *sh: ctx.enter_context(nc.sbuf_tensor(f"mlp_{s}", *sh))
        ab = buf("if", [P, TILES, 2 * H], F32)
        bias_i, bias_f = buf("bias_i", [P, H], F32), buf("bias_f", [P, H], F32)
        out_of = buf("out_of", [P, 1], F32)
        x, e, mn, lf = buf("x", [P, TILES, H], F32), buf("e", [P, TILES, H], F32), buf("mn", [P, TILES, H], F32), buf("lf", [P, TILES, H], F32)
        b, last = buf("b", [P, TILES, H], F32), buf("last", [P, TILES, H], F32)
        rows = buf("rows", [R, 2, P], F32)
        end = buf("end", [P, TILES, H], F32)
        small_in, w_landed = sem("small_in"), sem("w_landed")
        zeroed, w_hi, w_split = sem("zeroed"), sem("w_hi"), sem("w_split")
        ab_done, ab_copied, step = sem("if_done"), sem("if_copied"), sem("steps")
        flat = lambda t: t.rearrange("p c h -> p (c h)")
        block = ctx.enter_context(nc.Block())

        @block.sync
        def _(sp):
            sp.wait_ge(zeroed, 5)
            sp.dma_start(ws.stage[:, 0, :, 0:2 * H], w_in[:, :, 3 * D:3 * D + 2 * H]).then_inc(w_landed, 16)
            sp.dma_start(gain[:], a["ml_norm"][0].rearrange("(h p) -> p h", p=P), allow_slow_non_contiguous=True).then_inc(small_in, 16)
            sp.dma_start(bias_i[:], a["ml_b_i"].to_broadcast([P, H])).then_inc(small_in, 16)
            sp.dma_start(bias_f[:], a["ml_b_f"].to_broadcast([P, H])).then_inc(small_in, 16)
            sp.dma_start(m_end[:, 1], a["state_mlstm_m"][0].to_broadcast([P, H])).then_inc(small_in, 16)
            sp.wait_ge(small_in, 64)

        @block.gpsimd
        def _(pool):
            nc.gpsimd.memset(qkv[:, :, TOK:TILES * P], 0.0).then_inc(zeroed, 1)
            nc.gpsimd.memset(ab_t[:, TOK:TILES * P], 0.0).then_inc(zeroed, 1)
            nc.gpsimd.memset(ws.hi[:, 0].bitcast(F32), 0.0).then_inc(zeroed, 1)
            nc.gpsimd.memset(ws.lo[:, 0].bitcast(F32), 0.0).then_inc(zeroed, 1)
            nc.gpsimd.memset(v_tok[:, :, :, DV:DV + 1], 1.0).then_inc(zeroed, 1)
            pool.wait_ge(zeroed, 5)
            pool.wait_ge(w_landed, 16)
            st = ws.stage[:, 0, :, 0:2 * H]
            nc.gpsimd.tensor_tensor(ws.hi[:, 0, :, 0:2 * H], st,
                                    tk.one[:][:, :, None].to_broadcast([P, KB, 2 * H]), ALU.mult).then_inc(w_hi, 1)
            pool.wait_ge(w_hi, 1)
            nc.gpsimd.tensor_tensor(ws.lo[:, 0, :, 0:2 * H], st, ws.hi[:, 0, :, 0:2 * H].bitcast(F32),
                                    ALU.subtract).then_inc(w_split, 1)

        @block.tensor
        def _(pe):
            pe.wait_ge(w_split, 1)
            for n in range(NU):
                for k in range(KB):
                    mm = split_product(pe, ps[:, n, 0:UNIT], ws.hi[:, 0, k], ws.lo[:, 0, k],
                                       tk.hi[:, k, unit_cols(n)], tk.lo[:, k, unit_cols(n)], k == 0, k == KB - 1)
                mm.then_inc(ab_done, 1)
            pe.wait_ge(ab_copied, NU)
            pe.wait_ge(zeroed, 5)
            for c in range(TILES):
                mm = pe.transpose(ps[:, 3, c * 2 * H:(c + 1) * 2 * H], ab_t[:, c * P:(c + 1) * P],
                                  tk.ident[0:2 * H, 0:2 * H])
            mm.then_inc(step, 1)
            pe.wait_ge(step, 11)
            pe.matmul(ps[:, 4, 0:R], tk.upto[:], flat(lf[:]), start=True, stop=True)
            pe.matmul(ps[:, 5, 0:R], tk.ones[:], flat(lf[:]), start=True, stop=True).then_inc(step, 1)
            pe.wait_ge(step, 15)
            pe.transpose(ps[0:R, 6, 0:P], flat(gates[:, 0]), tk.ident[:]).then_inc(step, 1)
            pe.wait_ge(step, 24)
            pe.transpose(ps[:, 7, 0:R], rows[:, 1], tk.ident[0:R, 0:R]).then_inc(step, 1)
            pe.wait_ge(step, 26)
            pe.matmul(ps[:, 0, 0:R], tk.ident[:, P - 1:P].to_broadcast([P, P]), flat(gates[:, 1]),
                      start=True, stop=True).then_inc(step, 1)

        @block.scalar
        def _(act):
            def do(n, *args, **kw):
                act.wait_ge(step, n - 1)
                nc.scalar.activation(*args, **kw).then_inc(step, 1)
            nc.scalar.preload_act_table_set("natural_log_exp_and_others")
            do(6, e[:], e[:], ACT.Exp)
            do(7, e[:], e[:], ACT.Ln, bias=tk.one[:, 0:1])
            do(51, gates[:, 5], gates[:, 5], ACT.Exp)
            do(53, gates[:, 3], gates[:, 3], ACT.Exp)

        @block.vector
        def _(dve):
            def do(n, op, *args, **kw):
                dve.wait_ge(step, n - 1)
                op(*args, **kw).then_inc(step, 1)
            tt, stt, ts, cp = nc.vector.tensor_tensor, nc.vector.scalar_tensor_tensor, nc.vector.tensor_scalar, nc.vector.tensor_copy
            over = lambda t: t[:][:, None, :].to_broadcast([P, TILES, H])
            for n in range(NU):
                dve.wait_ge(ab_done, n + 1)
                cp(ab_t[:, unit_cols(n)], ps[0:2 * H, n, 0:UNIT]).then_inc(ab_copied, 1)
            dve.wait_ge(small_in, 64)
            do(2, cp, flat(ab[:]), ps[:, 3, 0:TILES * 2 * H])
            do(3, tt, x[:], ab[:, :, H:2 * H], over(bias_f), ALU.add)
            do(4, ts, mn[:], x[:], 0.0, None, ALU.min)
            do(5, stt, out=e[:], in0=mn[:], scalar=2.0, in1=x[:], op0=ALU.mult, op1=ALU.subtract)
            do(8, tt, lf[:], mn[:], e[:], ALU.subtract)
            do(9, ts, out_of[:], tk.upto[:, SAMPLE - 1:SAMPLE], 1.0, -NEG, ALU.subtract, ALU.mult)
            do(10, tt, x[:], ab[:, :, 0:H], over(bias_i), ALU.add)
            do(11, ts, lf[:, TILES - 1], lf[:, TILES - 1], tk.upto[:, SAMPLE - 1:SAMPLE], None, ALU.mult)
            do(13, cp, flat(b[:]), ps[:, 4, 0:R])
            do(14, ts, x[:, TILES - 1], x[:, TILES - 1], out_of[:, 0:1], None, ALU.add)
            do(15, tt, gates[:, 0], x[:], b[:], ALU.subtract)
            do(17, cp, rows[:, 0], ps[0:R, 6, 0:P])
            for l in range(LEVELS):
                w, src, dst = 1 << l, rows[:, l % 2], rows[:, (l + 1) % 2]
                dve.wait_ge(step, 17 + l)
                cp(dst[:, 0:w], src[:, 0:w])
                tt(dst[:, w:], src[:, w:], src[:, 0:P - w], ALU.max).then_inc(step, 1)
            do(26, cp, flat(gates[:, 1]), ps[:, 7, 0:R])
            do(28, cp, flat(last[:]), ps[:, 5, 0:R])
            do(29, cp, flat(end[:]), ps[:, 0, 0:R])
            do(30, nc.vector.memset, gates[:, 4, 0], 0.0)
            n = 31
            for c in range(TILES):
                if c == TILES - 1:
                    do(n, cp, gates[:, 4, c], m_end[:, 1]); n += 1
                do(n, tt, end[:, c], end[:, c], gates[:, 4, c], ALU.max); n += 1
                m_next = gates[:, 4, c + 1] if c < TILES - 2 else m_end[:, c - TILES + 2]
                do(n, tt, m_next, last[:, c], end[:, c], ALU.add); n += 1
            assert n == 50
            do(50, tt, gates[:, 5], gates[:, 4], end[:], ALU.subtract)
            do(52, tt, gates[:, 3], gates[:, 0], end[:], ALU.subtract)
            do(54, tt, gates[:, 1], gates[:, 1], gates[:, 4], ALU.max)
            do(55, tt, gates[:, 2], gates[:, 1], b[:], ALU.add)
            do(56, ts, gates[:, 3], gates[:, 3], MDK ** -0.5, None, ALU.mult)
            dve.wait_ge(step, 56)


def build_trunk(nc, a):
    with ExitStack() as ctx:
        buf = lambda s, *sh: ctx.enter_context(nc.sbuf_tensor(s, *sh))
        tk = Trunk()
        tk.ps = ctx.enter_context(nc.psum_tensor("ps", [P, 8, 512], F32))
        tk.x_dram = nc.dram_tensor("x_kept", (P, KB, TOK), F32).ap()
        tk.ones, tk.ident, tk.upto = buf("ones", [P, P], F32), buf("ident", [P, P], F32), buf("upto", [P, P], F32)
        tk.later_neg = buf("later_neg", [P, P], F32)
        tk.joins = buf("joins", [P, LEVELS, P], BF16)
        tk.eps, tk.one, tk.log_dk = buf("eps", [P, 1], F32), buf("one", [P, 1], F32), buf("log_dk", [P, 1], F32)
        tk.hi, tk.lo = buf("act_hi", [P, KB, TOK], F32R), buf("act_lo", [P, KB, TOK], F32R)

        tk.x = buf("x", [P, KB, TOK], F32)

        load_phase(nc, tk, a["x_prompt"], a["x_sample"])
        norm_phase(nc, tk, a["norm_mix"][0], "norm0", True)
        gdn_phase(nc, tk, a)
        out_phase(nc, tk, a["gdn_w_out"][0], "gdn_out")
        ffn_phase(nc, tk, a["norm_ffn"][0], a["ffn_w_gu"][0], a["ffn_w_down"][0], "ffn0")
        norm_phase(nc, tk, a["norm_mix"][1], "norm2", True)
        mlstm_phase(nc, tk, a)
        out_phase(nc, tk, a["ml_w_out"][0], "ml_out")
        ffn_phase(nc, tk, a["norm_ffn"][1], a["ffn_w_gu"][1], a["ffn_w_down"][1], "ffn1")
        store_phase(nc, tk, a["norm_final"], a["y_prompt"], a["y_sample"])


INPUTS = ["x_prompt", "x_sample", "state_gdn_conv", "state_gdn_S", "state_mlstm_C", "state_mlstm_n", "state_mlstm_m",
          "norm_mix", "gdn_w_in", "gdn_conv_w", "gdn_a_log", "gdn_dt_bias", "gdn_norm", "gdn_w_out", "ml_w_in",
          "ml_b_i", "ml_b_f", "ml_norm", "ml_w_out", "norm_ffn", "ffn_w_gu", "ffn_w_down", "norm_final"]
OUTPUTS = [("y_prompt", (1, PROMPT, D)), ("y_sample", (1, SAMPLE, D)),
           ("p_conv", (1, 1, HIST, 3 * D)), ("p_S", (1, 1, HEADS, DK, DV)), ("p_C", (1, 1, HEADS, MDK, DV)),
           ("p_n", (1, 1, HEADS, MDK)), ("p_m", (1, 1, HEADS)),
           ("s_conv", (1, 1, HIST, 3 * D)), ("s_S", (1, 1, HEADS, DK, DV)), ("s_C", (1, 1, HEADS, MDK, DV)),
           ("s_n", (1, 1, HEADS, MDK)), ("s_m", (1, 1, HEADS))]


def kernel(**inputs):
    import numpy as np
    import concourse.bacc as bacc
    from concourse.bass_utils import run_bass_kernel_spmd

    nc = bacc.Bacc("TRN2", target_bir_lowering=False, num_devices=1)
    arrays, a = {}, {}
    for name in INPUTS:
        arrays[f"in_{name}"] = np.ascontiguousarray(inputs[name])
        a[name] = nc.dram_tensor(f"in_{name}", arrays[f"in_{name}"].shape, F32, kind="ExternalInput").ap()
    for name, shape in OUTPUTS:
        a[name] = nc.dram_tensor(f"out_{name}", shape, F32, kind="ExternalOutput").ap()
    build_trunk(nc, a)
    got = run_bass_kernel_spmd(nc, [arrays], core_ids=[0]).results[0]
    return tuple(got[f"out_{name}"] for name, _ in OUTPUTS)
```

```python
import math
from contextlib import ExitStack

import concourse.bass as bass
from concourse import mybir

ALU = mybir.AluOpType
ACT = mybir.ActivationFunctionType
AX = mybir.AxisListType
F32 = mybir.dt.float32
F32R = mybir.dt.float32r
BF16 = mybir.dt.bfloat16

P = 128
PROMPT = 1024
SAMPLE = 32
TOK = PROMPT + SAMPLE
D = 1024
KB = D // P
NU = 3
UNIT = TOK // NU
HEADS = 8
DK, DV = 128, 128
MDK = 64
FFN = 2816
FB = FFN // P
TILES = 9
BATCHES = 3
HIST = 3
TAPS = 4
GCOL = PROMPT + HIST
CW = GCOL + SAMPLE
CPAD = GCOL + P
CU = CW // NU
LEVELS = 7
RMS_EPS = 1e-6
L2_EPS = 1e-6
NEG = -1e30


def tile_cols(c):
    start = c * P if c < TILES - 1 else GCOL
    return slice(start, start + P)


def unit_cols(n):
    return slice(n * UNIT, (n + 1) * UNIT)


def semaphores(nc, ctx, tag, again=False):
    made = []

    def sem(name):
        if again:
            made.append(nc.alloc_semaphore(name=f"{tag}_{name}"))
            return made[-1]
        return ctx.enter_context(nc.semaphore(f"{tag}_{name}"))

    def zero():
        if made:
            nc.clear_and_free_semaphores(made)
            nc.all_engine_barrier()

    ctx.callback(zero)
    return sem


def split_product(pe, out, w_hi, w_lo, rhs_hi, rhs_lo, first, last):
    pe.matmul(out, w_hi, rhs_hi, start=first, stop=False)
    pe.matmul(out, w_hi, rhs_lo, start=False, stop=False)
    return pe.matmul(out, w_lo, rhs_hi, start=False, stop=last)


class Trunk:
    pass


class Parts:
    pass


class WeightStream:

    def __init__(self, nc, tk, ctx, sem, name, ring, stages=2):
        self.nc, self.ring, self.stages, self.one = nc, ring, stages, tk.one
        buf = lambda s, *a: ctx.enter_context(nc.sbuf_tensor(f"{name}_{s}", *a))
        self.stage = buf("stage", [P, stages, KB, P], F32)
        self.hi = buf("hi", [P, ring, KB, P], F32R)
        self.lo = buf("lo", [P, ring, KB, P], F32R)
        self.landed = [sem(f"w_landed{s}") for s in range(stages)]
        self.hi_done = sem("w_hi_done")
        self.split_done = sem("w_split_done")

        self.checked, self.act_checked = sem("w_checked"), sem("act_checked")

    def start(self, pool):
        pool.sem_inc(self.split_done, self.stages)

    def wait_stage(self, sp, j):
        sp.wait_ge(self.split_done, j + 1)
        sp.sem_inc(self.checked, 1)

    def load(self, sp, j, slot, src):
        self.wait_stage(sp, j)
        sp.dma_start(self.stage[:, slot], src).then_inc(self.landed[slot], 16)

    def split(self, pool, j, stage_slot, landed_count, ring_slot, halves=(0, 1)):
        nc = self.nc
        pool.wait_ge(self.landed[stage_slot], landed_count)
        for h in halves:
            part = slice(h * KB // 2, (h + 1) * KB // 2)
            st, hi, lo = (t[:, s, part] for t, s in ((self.stage, stage_slot), (self.hi, ring_slot), (self.lo, ring_slot)))
            one = self.one[:][:, :, None].to_broadcast([P, KB // 2, P])
            nc.gpsimd.tensor_tensor(hi, st, one, ALU.mult).then_inc(self.hi_done, 1)
            pool.wait_ge(self.hi_done, j * 2 + (h + 1))
            op = nc.gpsimd.tensor_tensor(lo, st, hi.bitcast(F32), ALU.subtract)
        if 1 in halves:
            op.then_inc(self.split_done, 1)

    def wait_ready(self, pe, j):
        pe.wait_ge(self.split_done, j + self.stages + 1)


class Norm:

    BY_POOL = 3
    HALVES = (slice(0, KB // 2), slice(KB // 2, KB))

    def __init__(self, nc, tk, sem, buf, gain, slots, r):
        self.nc, self.tk, self.gain, self.slots, self.r = nc, tk, gain, slots, r
        self.g = buf("g", [P, KB], F32)
        self.g_in = sem("gain_landed")
        self.sq_done, self.ss_done, self.ln_done, self.r_done = sem("sq_done"), sem("ss_done"), sem("ln_done"), sem("r_done")
        self.h_done, self.hi_done = sem("h_done"), sem("hi_done")
        self.lo_done, self.pool_lo_done = sem("lo_done"), sem("pool_lo_done")

    def slot(self, n):
        return self.slots[n % len(self.slots)]

    def sync(self, sp):
        sp.dma_start(self.g[:], self.gain.rearrange("(k p) -> p k", p=P), allow_slow_non_contiguous=True).then_inc(self.g_in, 16)

    def tensor(self, pe):
        half = KB // 2
        for n in range(NU):
            for k in range(KB):
                if k % half == 0:
                    pe.wait_ge(self.sq_done, 2 * n + k // half + 1)
                mm = pe.matmul(self.tk.ps[:, n, 0:UNIT], self.tk.ones[:], self.slot(n)[:, k], start=k == 0, stop=k == KB - 1)
            mm.then_inc(self.ss_done, 1)

    def wait_split(self, engine, n):
        engine.wait_ge(self.lo_done, n + 1)
        engine.wait_ge(self.pool_lo_done, n + 1)

    def scalar(self, act):
        nc, tk, r = self.nc, self.tk, self.r
        nc.scalar.preload_act_table_set("natural_log_exp_and_others")

        def square(n):
            if n >= len(self.slots):
                self.wait_split(act, n - len(self.slots))
            for half in self.HALVES:
                nc.scalar.activation(self.slot(n)[:, half], tk.x[:, half, unit_cols(n)],
                                     ACT.Square).then_inc(self.sq_done, 1)

        def root(n):
            act.wait_ge(self.ss_done, n + 1)
            nc.scalar.activation(r[:, n], tk.ps[:, n, 0:UNIT], ACT.Ln, bias=tk.eps[:, 0:1],
                                 scale=1.0 / D).then_inc(self.ln_done, 1)
            act.wait_ge(self.ln_done, n + 1)
            nc.scalar.activation(r[:, n], r[:, n], ACT.Exp, scale=-0.5).then_inc(self.r_done, 1)

        def high(n):
            for i, half in enumerate(self.HALVES):
                act.wait_ge(self.h_done, 2 * n + i + 1)
                nc.scalar.copy(tk.hi[:, half, unit_cols(n)], self.slot(n)[:, half]).then_inc(self.hi_done, 1)

        for n in range(len(self.slots)):
            square(n)
        root(0)
        root(1)
        high(0)
        if len(self.slots) < NU:
            high(1)
            square(2)
        root(2)
        if len(self.slots) == NU:
            high(1)
        high(2)

    def vector(self, dve):
        nc, tk = self.nc, self.tk

        def low(n):
            dve.wait_ge(self.hi_done, 2 * n + 2)
            cols, mine = unit_cols(n), slice(self.BY_POOL, KB)
            nc.vector.tensor_tensor(tk.lo[:, mine, cols], self.slot(n)[:, mine],
                                    tk.hi[:, mine, cols].bitcast(F32), ALU.subtract).then_inc(self.lo_done, 1)

        dve.wait_ge(self.g_in, 16)
        for n in range(NU):
            if n == len(self.slots):
                low(n - 1)
            dve.wait_ge(self.r_done, n + 1)
            for k in range(KB):
                op = nc.vector.scalar_tensor_tensor(out=self.slot(n)[:, k], in0=tk.x[:, k, unit_cols(n)],
                                                    scalar=self.g[:, k:k + 1], in1=self.r[:, n],
                                                    op0=ALU.mult, op1=ALU.mult)
                if k in (KB // 2 - 1, KB - 1):
                    op.then_inc(self.h_done, 1)
            if 1 <= n < len(self.slots):
                low(n - 1)
        low(NU - 1)

    def gpsimd(self, pool, n):
        pool.wait_ge(self.hi_done, 2 * n + 1)
        cols, mine = unit_cols(n), slice(0, self.BY_POOL)
        self.nc.gpsimd.tensor_tensor(self.tk.lo[:, mine, cols], self.slot(n)[:, mine],
                                     self.tk.hi[:, mine, cols].bitcast(F32), ALU.subtract).then_inc(self.pool_lo_done, 1)


def norm_phase(nc, tk, gain, tag):
    with ExitStack() as ctx:
        sem = semaphores(nc, ctx, tag)
        buf = lambda s, *a: ctx.enter_context(nc.sbuf_tensor(f"{tag}_{s}", *a))
        norm = Norm(nc, tk, sem, buf, gain, [buf(f"slot{n}", [P, KB, UNIT], F32)[:] for n in range(NU)],
                    buf("r", [P, NU, UNIT], F32))
        spilled = sem("x_spilled")
        block = ctx.enter_context(nc.Block())

        @block.sync
        def _(sp):
            norm.sync(sp)
            sp.dma_start(tk.x_dram, tk.x[:]).then_inc(spilled, 16)
            sp.wait_ge(spilled, 16)

        @block.tensor
        def _(pe):
            norm.tensor(pe)

        @block.scalar
        def _(act):
            norm.scalar(act)

        @block.vector
        def _(dve):
            norm.vector(dve)
            norm.wait_split(dve, NU - 1)

        @block.gpsimd
        def _(pool):
            for n in range(NU):
                norm.gpsimd(pool, n)


def ffn_phase(nc, tk, gain, w_gu, w_down, tag):
    TURN = FB // 2
    B = 6
    U = 4 * NU + NU * KB
    ps, x = tk.ps, tk.x
    with ExitStack() as ctx:
        sem = semaphores(nc, ctx, tag)
        buf = lambda s, *a: ctx.enter_context(nc.sbuf_tensor(f"{tag}_{s}", *a))
        ws = WeightStream(nc, tk, ctx, sem, tag, B)
        gu = w_gu.rearrange("(k p) f -> p k f", p=P)
        dn = w_down.rearrange("(j p) (m c) -> p j m c", p=P, c=P)

        def load(sp, t):
            for b in range(4):
                ws.load(sp, t * B + b, b % 2, gu[:, :, bass.ds(t * (2 * P) + (b // 2 * P + b % 2 * FFN), P)])
            for j in range(2):
                ws.load(sp, t * B + (4 + j), j, dn[:, t * 2 + j])

        def split(pool, t, b):
            ws.split(pool, t * B + b, b % 2, t * 48 + (b // 2 * 16 + 16), b)

        silu = buf("silu", [P, NU, UNIT], F32)
        hid = buf("hid", [P, NU, UNIT], F32)
        hid_hi = buf("hid_hi", [P, 2, NU, UNIT], F32R)
        hid_lo = buf("hid_lo", [P, 2, NU, UNIT], F32R)
        slots = [buf(f"slot{n}", [P, KB, UNIT], F32)[:] for n in range(2)]
        norm = Norm(nc, tk, sem, buf, gain, slots, silu)
        unit_done = sem("unit_done")
        silu_done = sem("silu_done")
        hid_done = sem("hid_done")
        hi_done = sem("hid_hi_done")
        lo_done = sem("hid_lo_done")
        added = sem("added")
        DOWN = (6, 7, 1, 2)
        block = ctx.enter_context(nc.Block())

        @block.sync
        def _(sp):
            norm.sync(sp)
            load(sp, 0)
            with sp.Fori(1, TURN) as t:
                load(sp, t)

        @block.gpsimd
        def _(pool):
            ws.start(pool)
            pool.sem_inc(unit_done, U)
            pool.sem_inc(silu_done, NU)
            pool.sem_inc(hid_done, NU)
            pool.sem_inc(lo_done, NU)
            pool.sem_inc(added, 4)
            split(pool, 0, 0)
            split(pool, 0, 1)
            norm.gpsimd(pool, 0)
            split(pool, 0, 2)
            norm.gpsimd(pool, 1)
            norm.gpsimd(pool, 2)
            for b in range(3, B):
                split(pool, 0, b)
            with pool.Fori(1, TURN) as t:
                for b in range(B):
                    pool.wait_ge(unit_done, t * U + (NU * (b + 1) if b < 4 else U))
                    split(pool, t, b)

        @block.tensor
        def _(pe):
            norm.tensor(pe)
            with pe.Fori(0, TURN) as t:
                for b in range(4):
                    ws.wait_ready(pe, t * B + b)
                    for n in range(NU):
                        pe.wait_ge(hid_done if b % 2 else silu_done, t * 6 + (b // 2 * NU + n + 1))
                        if b == 0:
                            norm.wait_split(pe, n)
                        if b == 0 and n >= 1:
                            pe.wait_ge(added, t * (NU * KB) + 4)
                        out = ps[:, b % 2 * NU + n, 0:UNIT]
                        for k in range(KB):
                            mm = split_product(pe, out, ws.hi[:, b, k], ws.lo[:, b, k],
                                               tk.hi[:, k, unit_cols(n)], tk.lo[:, k, unit_cols(n)],
                                               k == 0, k == KB - 1)
                        mm.then_inc(unit_done, 1)
                ws.wait_ready(pe, t * B + 5)
                for n in range(NU):
                    pe.wait_ge(hi_done, t * 6 + (NU + n + 1))
                    pe.wait_ge(lo_done, t * 6 + (2 * NU + n + 1))
                    for m in range(KB):
                        pe.wait_ge(added, t * (NU * KB) + (n * KB + m + 1))
                        for j in range(2):
                            mm = split_product(pe, ps[:, DOWN[m % 4], 0:UNIT],
                                               ws.hi[:, 4 + j, m], ws.lo[:, 4 + j, m],
                                               hid_hi[:, j, n], hid_lo[:, j, n], j == 0, j == 1)
                        mm.then_inc(unit_done, 1)

        @block.scalar
        def _(act):
            norm.scalar(act)
            with act.Fori(0, TURN) as t:
                for j in range(2):
                    for n in range(NU):
                        act.wait_ge(unit_done, t * U + (U + 6 * j + n + 1))
                        act.wait_ge(hid_done, t * 6 + (j * NU + n + 1))
                        nc.scalar.activation(silu[:, n], ps[:, n, 0:UNIT], ACT.Silu).then_inc(silu_done, 1)
                    for n in range(NU):
                        act.wait_ge(hid_done, t * 6 + (j * NU + NU + n + 1))
                        act.wait_ge(unit_done, t * U + U)
                        nc.scalar.copy(hid_hi[:, j, n], hid[:, n]).then_inc(hi_done, 1)

        @block.vector
        def _(dve):
            norm.vector(dve)
            with dve.Fori(0, TURN) as t:
                for j in range(2):
                    for n in range(NU):
                        dve.wait_ge(unit_done, t * U + (U + 6 * j + NU + n + 1))
                        dve.wait_ge(silu_done, t * 6 + (j * NU + NU + n + 1))
                        dve.wait_ge(lo_done, t * 6 + (j * NU + n + 1))
                        nc.vector.tensor_tensor(hid[:, n], silu[:, n], ps[:, NU + n, 0:UNIT],
                                                ALU.mult).then_inc(hid_done, 1)
                        dve.wait_ge(hi_done, t * 6 + (j * NU + n + 1))
                        nc.vector.tensor_tensor(hid_lo[:, j, n], hid[:, n], hid_hi[:, j, n].bitcast(F32),
                                                ALU.subtract).then_inc(lo_done, 1)
                for n in range(NU):
                    for m in range(KB):
                        dve.wait_ge(unit_done, t * U + (U + 4 * NU + n * KB + m + 1))
                        dve.wait_ge(added, t * (NU * KB) + 4)
                        nc.vector.tensor_tensor(x[:, m, unit_cols(n)], x[:, m, unit_cols(n)],
                                                ps[:, DOWN[m % 4], 0:UNIT], ALU.add).then_inc(added, 1)


def load_phase(nc, tk, x_prompt, x_sample):
    ps, x = tk.ps, tk.x
    with ExitStack() as ctx:
        sem = semaphores(nc, ctx, "load")
        buf = lambda s, *a: ctx.enter_context(nc.sbuf_tensor(f"load_{s}", *a))
        rows = buf("rows", [P, 3, D], F32)
        landed = [sem(f"rows_landed{s}") for s in range(3)]
        made, turned, copied = sem("constants_made"), sem("turned"), sem("copied")
        block = ctx.enter_context(nc.Block())

        def size(c):
            return P if c < TILES - 1 else SAMPLE

        @block.sync
        def _(sp):
            for c in range(TILES):
                if c >= 3:
                    sp.wait_ge(turned, 2 * (c - 2))
                src = x_prompt[0, c * P:(c + 1) * P] if c < TILES - 1 else x_sample[0]
                sp.dma_start(rows[0:size(c), c % 3], src).then_inc(landed[c % 3], 16)

        @block.gpsimd
        def _(pool):
            n = 0
            def step(op):
                nonlocal n
                n += 1
                op.then_inc(made, 1)
                pool.wait_ge(made, n)
            step(nc.gpsimd.memset(tk.ones[:], 1.0))
            step(nc.gpsimd.memset(tk.eps[:], RMS_EPS))
            step(nc.gpsimd.memset(tk.one[:], 1.0))
            step(nc.gpsimd.memset(tk.log_dk[:], -0.5 * math.log(DK)))
            step(nc.gpsimd.affine_select(out=tk.ident[:], in_=tk.ones[:], compare_op=ALU.is_equal, fill=0.0,
                                         base=0, pattern=[[1, P]], channel_multiplier=-1))
            step(nc.gpsimd.affine_select(out=tk.upto[:], in_=tk.ones[:], compare_op=ALU.is_ge, fill=0.0,
                                         base=0, pattern=[[1, P]], channel_multiplier=-1))
            step(nc.gpsimd.memset(tk.later_neg[:], 0.0))
            step(nc.gpsimd.affine_select(out=tk.later_neg[:], in_=tk.later_neg[:], compare_op=ALU.is_ge, fill=NEG,
                                         base=0, pattern=[[1, P]], channel_multiplier=-1))
            step(nc.gpsimd.memset(tk.joins[:], 0.0))
            for l in range(LEVELS):
                s = 1 << l
                blocks = P // (2 * s)
                view = tk.joins[:, l].rearrange("p (b h c) -> p b h c", b=blocks, h=2)
                step(nc.gpsimd.memset(view[:, :, 1], 1.0))
                step(nc.gpsimd.affine_select(out=view[:, :, 1], in_=view[:, :, 1], compare_op=ALU.is_ge, fill=0.0,
                                             base=0, pattern=[[-2 * s, blocks], [0, s]], channel_multiplier=1))
                step(nc.gpsimd.affine_select(out=view[:, :, 1], in_=view[:, :, 1], compare_op=ALU.is_ge, fill=0.0,
                                             base=s - 1, pattern=[[2 * s, blocks], [0, s]], channel_multiplier=-1))

        @block.tensor
        def _(pe):
            pe.wait_ge(made, 5)
            for c in range(TILES):
                pe.wait_ge(landed[c % 3], 16 * (c // 3 + 1))
                for half in range(2):
                    if c >= 2:
                        pe.wait_ge(copied, 2 * (c - 2) + half + 1)
                    for k in range(4):
                        mm = pe.transpose(ps[:, (c % 2) * 2 + half, k * P:k * P + size(c)],
                                          rows[0:size(c), c % 3, (half * 4 + k) * P:(half * 4 + k + 1) * P],
                                          tk.ident[0:size(c), 0:size(c)])
                    mm.then_inc(turned, 1)

        @block.vector
        def _(dve):
            for c in range(TILES):
                for half in range(2):
                    dve.wait_ge(turned, 2 * c + half + 1)
                    src = ps[:, (c % 2) * 2 + half].rearrange("p (k t) -> p k t", k=4)[:, :, 0:size(c)]
                    nc.vector.tensor_copy(x[:, half * 4:half * 4 + 4, c * P:c * P + size(c)], src).then_inc(copied, 1)
            dve.wait_ge(copied, 2 * TILES)


def store_phase(nc, tk, gain, y_prompt, y_sample):
    ps, x = tk.ps, tk.x
    H = KB // 2
    with ExitStack() as ctx:
        sem = semaphores(nc, ctx, "store")
        buf = lambda s, *a: ctx.enter_context(nc.sbuf_tensor(f"store_{s}", *a))
        g = buf("g", [P, KB], F32)
        sq = buf("sq", [P, 2, KB, UNIT], F32)
        r = buf("r", [P, TOK], F32)
        rows = buf("rows", [P, 2, D], F32)
        g_in, sq_done, ss_done, ln_done, r_done, y_done = (
            sem("gain_landed"), sem("sq_done"), sem("ss_done"), sem("ln_done"), sem("r_done"), sem("y_done"))
        turned, copied, stored = sem("turned"), [sem("copied_by_act"), sem("copied_by_dve")], [sem("stored0"), sem("stored1")]
        block = ctx.enter_context(nc.Block())

        def size(c):
            return P if c < TILES - 1 else SAMPLE

        def unit_of(c):
            return (c * P + size(c) - 1) // UNIT

        def turn_back(engine, copy, half):
            for c in range(TILES):
                if c >= 2:
                    engine.wait_ge(stored[c % 2], 16 * (c // 2))
                engine.wait_ge(turned, 2 * c + half + 1)
                copy(rows[0:size(c), c % 2, half * 512:(half + 1) * 512],
                     ps[0:size(c), (c % 2) * 2 + half]).then_inc(copied[half], 1)

        @block.sync
        def _(sp):
            sp.dma_start(g[:], gain.rearrange("(k p) -> p k", p=P), allow_slow_non_contiguous=True).then_inc(g_in, 16)
            for c in range(TILES):
                sp.wait_ge(copied[0], c + 1)
                sp.wait_ge(copied[1], c + 1)
                dst = y_prompt[0, c * P:(c + 1) * P] if c < TILES - 1 else y_sample[0]
                sp.dma_start(dst, rows[0:size(c), c % 2]).then_inc(stored[c % 2], 16)
            sp.wait_ge(stored[0], 16 * 5)
            sp.wait_ge(stored[1], 16 * 4)

        @block.tensor
        def _(pe):
            def sums(n):
                for k in range(KB):
                    if k % H == 0:
                        pe.wait_ge(sq_done, 2 * n + k // H + 1)
                    mm = pe.matmul(ps[:, 4 + n, 0:UNIT], tk.ones[:], sq[:, n % 2, k], start=k == 0, stop=k == KB - 1)
                mm.then_inc(ss_done, 1)

            for n in range(NU):
                sums(n)
            for c in range(TILES):
                if c == 0 or unit_of(c) != unit_of(c - 1):
                    pe.wait_ge(y_done, unit_of(c) + 1)
                for half in range(2):
                    if c >= 2:
                        pe.wait_ge(copied[half], c - 1)
                    for k in range(4):
                        mm = pe.transpose(ps[0:size(c), (c % 2) * 2 + half, k * P:(k + 1) * P],
                                          x[:, half * 4 + k, c * P:c * P + size(c)], tk.ident[:])
                    mm.then_inc(turned, 1)

        @block.scalar
        def _(act):
            nc.scalar.preload_act_table_set("natural_log_exp_and_others")

            def square(n):
                if n >= 2:
                    act.wait_ge(ss_done, n - 1)
                for half in (slice(0, H), slice(H, KB)):
                    nc.scalar.activation(sq[:, n % 2, half], x[:, half, unit_cols(n)], ACT.Square).then_inc(sq_done, 1)

            def root(n):
                act.wait_ge(ss_done, n + 1)
                nc.scalar.activation(r[:, unit_cols(n)], ps[:, 4 + n, 0:UNIT], ACT.Ln, bias=tk.eps[:, 0:1],
                                     scale=1.0 / D).then_inc(ln_done, 1)
                act.wait_ge(ln_done, n + 1)
                nc.scalar.activation(r[:, unit_cols(n)], r[:, unit_cols(n)], ACT.Exp, scale=-0.5).then_inc(r_done, 1)

            square(0)
            square(1)
            root(0)
            square(2)
            root(1)
            root(2)
            turn_back(act, nc.scalar.copy, 0)

        @block.vector
        def _(dve):
            dve.wait_ge(g_in, 16)
            for n in range(NU):
                dve.wait_ge(r_done, n + 1)
                for k in range(KB):
                    op = nc.vector.scalar_tensor_tensor(out=x[:, k, unit_cols(n)], in0=x[:, k, unit_cols(n)],
                                                        scalar=g[:, k:k + 1], in1=r[:, unit_cols(n)],
                                                        op0=ALU.mult, op1=ALU.mult)
                op.then_inc(y_done, 1)
            turn_back(dve, nc.vector.tensor_copy, 1)


def out_phase(nc, tk, w_out, tag):
    ps, x = tk.ps, tk.x
    with ExitStack() as ctx:
        sem = semaphores(nc, ctx, tag)
        buf = lambda s, *a: ctx.enter_context(nc.sbuf_tensor(f"{tag}_{s}", *a))
        ws = WeightStream(nc, tk, ctx, sem, tag, 2)
        x_in = sem("x_landed")
        unit_done = sem("unit_done")
        added = sem("added")
        hi_done, lo_done = sem("o_hi_done"), sem("o_lo_done")
        w = w_out.rearrange("(k p) f -> p k f", p=P)
        block = ctx.enter_context(nc.Block())

        @block.sync
        def _(sp):
            def load(t):
                for b in range(2):
                    ws.load(sp, t * 2 + b, b, w[:, :, bass.ds(t * (2 * P) + b * P, P)])

            load(0)
            sp.wait_ge(lo_done, NU)
            sp.dma_start(x[:], tk.x_dram).then_inc(x_in, 16)
            with sp.Fori(1, KB // 2) as t:
                load(t)

        @block.gpsimd
        def _(pool):
            ws.start(pool)
            pool.sem_inc(unit_done, 6)
            pool.sem_inc(added, 6)
            with pool.Fori(0, KB // 2) as t:
                for b in range(2):
                    pool.wait_ge(unit_done, t * 6 + (3 * b + 3))
                    ws.split(pool, t * 2 + b, b, t * 16 + 16, b)

        @block.scalar
        def _(act):
            for n in range(NU):
                nc.scalar.copy(tk.hi[:, :, unit_cols(n)], x[:, :, unit_cols(n)]).then_inc(hi_done, 1)

        @block.tensor
        def _(pe):
            def turn(t, first):
                for b in range(2):
                    ws.wait_ready(pe, t * 2 + b)
                    for n in range(NU):
                        pe.wait_ge(added, t * 6 + (3 * b + n + 1))
                        if first and b == 0:
                            pe.wait_ge(lo_done, n + 1)
                        for k in range(KB):
                            mm = split_product(pe, ps[:, 3 * b + n, 0:UNIT], ws.hi[:, b, k], ws.lo[:, b, k],
                                               tk.hi[:, k, unit_cols(n)], tk.lo[:, k, unit_cols(n)],
                                               k == 0, k == KB - 1)
                        mm.then_inc(unit_done, 1)

            turn(0, True)
            with pe.Fori(1, KB // 2) as t:
                turn(t, False)

        @block.vector
        def _(dve):
            for n in range(NU):
                dve.wait_ge(hi_done, n + 1)
                nc.vector.tensor_tensor(tk.lo[:, :, unit_cols(n)], x[:, :, unit_cols(n)],
                                        tk.hi[:, :, unit_cols(n)].bitcast(F32), ALU.subtract).then_inc(lo_done, 1)
            dve.wait_ge(x_in, 16)
            with dve.Fori(0, KB // 2) as t:
                for b in range(2):
                    for n in range(NU):
                        dve.wait_ge(unit_done, t * 6 + (6 + 3 * b + n + 1))
                        cols = x[:, bass.ds(t * 2 + b, 1), unit_cols(n)].rearrange("p a t -> p (a t)")
                        nc.vector.tensor_tensor(cols, cols, ps[:, 3 * b + n, 0:UNIT],
                                                ALU.add).then_inc(added, 1)


def gdn_phase(nc, tk, a):
    ps = tk.ps
    B = 4
    U = B * NU
    w_in = a["gdn_w_in"][0].rearrange("(k p) f -> p k f", p=P)
    

    def fill(r, l, place):
        if r == BATCHES:
            return {"A": 1, "B": 1, "T": 7}[place] if l < 4 else 0
        return {"P": (8, 5, 5)[r], "A": 2, "B": 1}[place]

    taps = {}
    for ch, start in enumerate((LEVELS, 2 * LEVELS, 2 * LEVELS + 4)):
        for tap in range(TAPS):
            taps[divmod(start + tap, LEVELS)] = (ch, tap)
    SUMS = ((0, 1), (2, 3), (), (4,), (5,), (), ())
    SQUARES = ((2, 3), (), (4, 5), (), (), (), ())
    ROOTS = ((), (0,), (1,), (2, 3), (4,), (5,), ())
    SCALED = ((), (), (0,), (1,), (2, 3), (4,), (5,))
    O_SUMS = ((), (), (), (), (), (0, 1), ())
    O_SQUARES = ((0,), (1,), (), (), (), (), ())
    O_ROOTS = ((), (), (), (), (), (0,), (1,))
    NQ = 5
    with ExitStack() as ctx:
        sem = semaphores(nc, ctx, "gdn", again=True)
        buf = lambda s, *a: ctx.enter_context(nc.sbuf_tensor(f"gdn_{s}", *a))
        ws = WeightStream(nc, tk, ctx, sem, "gdn", 2)
        gates = buf("gates", [P, NQ + 1, TILES, HEADS], F32)
        conv_w = buf("conv_w", [P, TAPS * 3, HEADS], F32)
        hist = buf("hist", [P, HIST * 3, HEADS], F32)
        tails = buf("tails", [P, 2, HIST * 3, HEADS], F32)
        tail_rows = buf("tail_rows", [P, 2, P], F32)
        R = HIST * 3 * HEADS
        tails_turned, tails_copied, tails_out = sem("tails_turned"), sem("tails_copied"), sem("tails_out")
        gain = buf("gain", [P, 1], F32)
        raw = buf("raw", [P, 2, PROMPT + 2 * HIST + SAMPLE], F32)
        qkv = buf("qkv", [P, 3, CPAD], F32)
        conv = buf("conv", [P, 2, CW], F32)
        o = buf("o", [P, TOK], F32)
        hw = buf("head_conv_w", [P, TAPS * 3], F32)
        hg = buf("head_gates", [P, NQ + 1, TILES], F32)
        sq = buf("sq", [P, 2, CU], F32)
        rs = buf("rs", [P, 2, CU], F32)
        gam = buf("gam", [P, BATCHES, P], F32)
        exp_d = buf("exp_d", [P, BATCHES, P], F32)
        mt = buf("mt", [P, BATCHES, P], F32)
        mt_l = buf("mt_level", [P, 2, BATCHES, P], F32)
        wz = buf("wz", [P, BATCHES, P], F32)
        z = buf("z", [P, 2, 2, BATCHES, P], F32)
        att = buf("att", [P, 2, BATCHES, P], F32)
        qd = buf("qd", [P, 2, BATCHES, P], F32)
        k_tail = buf("k_tail", [P, 2, BATCHES, P], F32)
        v_tok = buf("v_tok", [P, 2, BATCHES, P], F32)
        y = buf("y", [P, P], F32)
        v_new = buf("v_new", [P, P], F32)
        state = buf("state", [P, 2, DV], F32)

        o_work = [b.rearrange("p i c -> p (i c)")[:, 0:UNIT] for b in (mt[:], mt_l[:, 0], mt_l[:, 1])]

        def load(sp, t, ahead, b):
            ws.load(sp, t * B + (ahead * B + b), b % 2, w_in[:, :, bass.ds(t * P + (ahead * P + b * D), P)])

        pro = gdn_prologue(nc, tk, sem, buf, a, w_in, ws, gates, conv_w, hist, gain, raw, qkv, tail_rows,
                           conv[0:2 * HEADS].rearrange("p a c -> p (a c)"))
        unit_done, evacuated = sem("unit_done"), sem("evacuated")
        conv_steps, conv_done, silu_done, z_silu_done = (sem("conv_steps"), sem("conv_done"), sem("silu_done"),
                                                         sem("z_silu_done"))
        taps_taken, frames_taken, cols_taken = sem("taps_taken"), sem("frames_taken"), sem("cols_taken")
        sq_done, ss_done, ln_done, rs_done, unit_len = (sem("sq_done"), sem("ss_done"), sem("ln_done"),
                                                        sem("rs_done"), sem("unit_len_done"))
        osq_done, oss_done, oln_done, ors_done = sem("osq_done"), sem("oss_done"), sem("oln_done"), sem("ors_done")
        prep_done, expd_done, e_done, gam_done = sem("prep_done"), sem("expd_done"), sem("e_done"), sem("gam_done")
        made = sem("att_mt_qd_done")
        tok_done = sem("tok_done")
        level_masked, z_first, z_done = sem("level_masked"), sem("z_first_done"), sem("z_done")
        wz_done, wz_copied, pz_done = sem("wz_done"), sem("wz_copied"), sem("pz_done")
        chain, y_done, vn_done, o_done, s_done = (sem("chain"), sem("y_done"), sem("vn_done"), sem("o_done"),
                                                  sem("s_done"))
        s_in, s_out, s_init = sem("state_landed"), sem("state_stored"), sem("state_zeroed")
        o_normed, final_done = sem("o_normed"), sem("final_done")
        block = ctx.enter_context(nc.Block())

        @block.sync
        def _(sp):
            def weights(t, ahead, b):
                load(sp, t, ahead, b)

            def states(t):
                sp.dma_start(state[:, 1], a["state_gdn_S"][0, 0, t]).then_inc(s_in, 16)

            def store(t):
                sp.wait_ge(s_done, t * 9 + 9)
                sp.sem_inc(ws.checked, 1)
                sp.dma_start(a["p_S"][0, 0, t], state[:, 0]).then_inc(s_out, 16)
                sp.dma_start(a["s_S"][0, 0, t], state[:, 1]).then_inc(s_out, 16)

            def head(t, ahead):
                for b in range(1, B) if ahead >= 1 else ():
                    weights(t, 1, b)
                if ahead == 2:
                    weights(t, 2, 0)
                store(t)
                if ahead >= 1:
                    sp.wait_ge(s_out, t * 32 + 64)
                    sp.sem_inc(ws.checked, 1)
                    states(t + 1)

            pro.sync(sp)
            weights(0, 0, 0)
            sp.wait_ge(pro.w_split, 1)
            for b in range(1, B):
                weights(0, 0, b)
            states(0)
            weights(0, 1, 0)
            with sp.Fori(0, HEADS - 2) as t:
                head(t, 2)
            head(HEADS - 2, 1)
            head(HEADS - 1, 0)
            for g, dst in enumerate((a["p_conv"], a["s_conv"])):
                sp.wait_ge(tails_copied, g + 1)
                sp.dma_start(dst[0, 0].rearrange("f (r c) -> (f r) c", c=P), tail_rows[0:R, g]).then_inc(tails_out, 16)
            sp.wait_ge(s_out, HEADS * 32 + 32)
            sp.wait_ge(tails_out, 32)

        @block.gpsimd
        def _(pool):
            pro.gpsimd(pool)
            pool.sem_inc(evacuated, 2)
            pool.sem_inc(s_out, 32)

            def weights(t, ahead, b, halves):
                if 0 in halves and (b >= 2 or ahead >= 1):
                    pool.wait_ge(unit_done, t * U + (ahead * U + NU * (b - 1)))
                ws.split(pool, t * B + (ahead * B + b), b % 2, t * 32 + (ahead * 32 + b // 2 * 16 + 16), b % 2, halves)

            def mask(t, r, l):
                i = r * LEVELS + l
                pool.wait_ge(made, t * 9 + 3 * r + 3)
                if r > 0 or l >= 2:
                    pool.wait_ge(wz_done, t * 21 + (i - 1))
                nc.gpsimd.tensor_tensor(mt_l[:, i % 2], mt[:],
                                        tk.joins[:, l][:, None, :].to_broadcast([P, BATCHES, P]),
                                        ALU.mult).then_inc(level_masked, 1)

            def head(t, ahead):
                for r in range(BATCHES):
                    for l in range(LEVELS):
                        mask(t, r, l)
                        for first, k, b in ((2, 1, 1), (LEVELS + 1, 1, 2), (2 * LEVELS, 1, 3), (2 * LEVELS + 4, 2, 0)):
                            half = r * LEVELS + l - first
                            if half in (0, 1) and ahead >= k:
                                weights(t, k, b, (half,))

            weights(0, 0, 0, (0, 1))
            pool.wait_ge(pro.ab_done, NU)
            for b in range(1, B):
                weights(0, 0, b, (0, 1))
            weights(0, 1, 0, (0, 1))
            with pool.Fori(0, HEADS - 2) as t:
                head(t, 2)
            head(HEADS - 2, 1)
            head(HEADS - 1, 0)

        @block.tensor
        def _(pe):
            def piece(t, n, only_third=None):
                u, k = n // KB, n % KB
                b, cols = u // NU, unit_cols(u % NU)
                if n % (NU * KB) == 0:
                    ws.wait_ready(pe, t * B + b)
                if k == 0:
                    pe.wait_ge(evacuated, t * U + (u + 1))
                mm = split_product(pe, ps[:, u % 2, 0:UNIT], ws.hi[:, b % 2, k], ws.lo[:, b % 2, k],
                                   tk.hi[:, k, cols], tk.lo[:, k, cols], k == 0, k == KB - 1)
                if k == KB - 1:
                    mm.then_inc(unit_done, 1)

            def sums(h, i):
                pe.wait_ge(sq_done, h * 6 + (i + 1))
                if i >= 4:
                    pe.wait_ge(ln_done, h * 6 + (i - 3))
                pe.matmul(ps[:, 2 + i % 4, 0:CU], tk.ones[:], sq[:, i % 2], start=True, stop=True).then_inc(ss_done, 1)

            def o_sums(t, n, more):
                pe.wait_ge(osq_done, t * 3 + (n + 1))
                bank = (4, 5, 6)[n]
                if n == 2:
                    pe.wait_ge(s_done, t * 9 + 9)
                else:
                    pe.wait_ge(z_done, t * 24 + 24)
                    if more:
                        pe.wait_ge(ln_done, t * 6 + (6 + 3 + n))
                pe.matmul(ps[:, bank, 0:UNIT], tk.ones[:], o_work[n], start=True, stop=True).then_inc(oss_done, 1)

            def prepare(t, r, pieces):
                if r > 0:
                    pe.wait_ge(tok_done, t * 6 + 2 * r)
                for i in range(BATCHES):
                    mm = pe.matmul(ps[:, 2, i * P:(i + 1) * P],
                                   hg[:, NQ, 3 * r + i:3 * r + i + 1].to_broadcast([P, P]), tk.upto[:],
                                   start=True, stop=True)
                mm.then_inc(prep_done, 1)
                for bank, ch in ((3, 1), (4, 0)):
                    if r > 0 and bank == 4:
                        pe.wait_ge(z_done, t * 24 + 8 * r)
                    for i in range(BATCHES):
                        cols = tile_cols(3 * r + i)
                        mm = pe.matmul(ps[:, bank, i * P:(i + 1) * P], qkv[:, 1, cols], qkv[:, ch, cols],
                                       start=True, stop=True)
                    mm.then_inc(prep_done, 1)
                for i in range(BATCHES):
                    mm = pe.transpose(ps[:, 5, i * P:(i + 1) * P], qkv[:, 1, tile_cols(3 * r + i)], tk.ident[:])
                mm.then_inc(prep_done, 1)
                pieces(r, 0, "P")
                pe.wait_ge(expd_done, t * 3 + (r + 1))
                pe.wait_ge(e_done, t * 3 + (r + 1))
                for i in range(BATCHES):
                    mm = pe.transpose(ps[:, 2, i * P:(i + 1) * P], qkv[:, 2, tile_cols(3 * r + i)], tk.ident[:])
                mm.then_inc(prep_done, 1)

            def join_w(t, r, l):
                par, i = r % 2, r * LEVELS + l
                pe.wait_ge(level_masked, t * 21 + (i + 1))
                pe.wait_ge(z_first, t * 18 + (r * 6 + l)) if l else pe.wait_ge(z_done, t * 24 + (r * 8 + 1))
                if l == 0:
                    pe.wait_ge(made, t * 9 + (3 * r + 3))
                for i in range(BATCHES):
                    mm = pe.matmul(ps[:, 3, i * P:(i + 1) * P], mt_l[:, (r * LEVELS + l) % 2, i], z[:, par, 0, i],
                                   start=True, stop=True)
                mm.then_inc(wz_done, 1)

            def join_z(t, r, l, pieces):
                par, i = r % 2, r * LEVELS + l
                pe.wait_ge(wz_copied, t * 21 + (i + 1))
                pe.wait_ge(z_done, t * 24 + (r * 8 + l + 1))
                if l == 0:
                    pe.wait_ge(tok_done, t * 6 + (2 * r + 2))
                if 0 < l < LEVELS - 1:
                    for i in range(BATCHES):
                        mm = pe.matmul(ps[:, 4, i * P:(i + 1) * P], z[:, par, 1, i], wz[:, i], start=True, stop=True)
                    mm.then_inc(pz_done, 1)
                for i in range(BATCHES):
                    mm = pe.matmul(ps[:, 5, i * P:(i + 1) * P], wz[:, i], z[:, par, 1, i], start=True, stop=True)
                mm.then_inc(pz_done, 1)
                pieces(r, l, "B")

            def chain_step(t, r, s):
                par, i = r % 2, s // 3
                c = 3 * r + i
                g = c // 8
                if s % 3 == 0:
                    if c == 0:
                        pe.wait_ge(s_init, t + 1)
                    elif c < 8:
                        pe.wait_ge(s_done, t * 9 + c)
                    else:
                        pe.wait_ge(s_in, t * 16 + 16)
                        pe.wait_ge(s_done, t * 9 + c)
                    pe.matmul(ps[:, 6, 0:P], qkv[:, 1, tile_cols(c)], state[:, g],
                              start=True, stop=True).then_inc(chain, 1)
                elif s % 3 == 1:
                    pe.wait_ge(y_done, t * 9 + (c + 1))
                    pe.matmul(ps[:, 6, P:2 * P], z[:, par, 1, i], y[:], start=True, stop=True).then_inc(chain, 1)
                else:
                    if c >= 1:
                        pe.wait_ge(o_done, t * 9 + c)
                    pe.matmul(ps[:, 7, 0:P], state[:, g], qd[:, par, i], start=True, stop=False)
                    pe.wait_ge(vn_done, t * 9 + (c + 1))
                    pe.matmul(ps[:, 7, 0:P], v_new[:], att[:, par, i], start=False, stop=True)
                    pe.matmul(ps[:, 6, 2 * P:3 * P], k_tail[:, par, i], v_new[:],
                              start=True, stop=True).then_inc(chain, 1)

            def head(t, more):
                n = 0

                def pieces(r, l, place):
                    nonlocal n
                    for _ in range(fill(r, l, place) if more else 0):
                        piece(t + 1, n)
                        n += 1

                pe.wait_ge(cols_taken, t + 1)
                pe.wait_ge(unit_len, t * 6 + 6)
                pe.wait_ge(silu_done, t * 3 + 3)
                for r in range(BATCHES + 1):
                    if r < BATCHES:
                        prepare(t, r, pieces)
                    for l in range(LEVELS):
                        if r < BATCHES:
                            join_w(t, r, l)
                        pieces(r, l, "A")
                        if r > 0 and 2 * l < 9:
                            chain_step(t, r - 1, 2 * l)
                        if r < BATCHES:
                            join_z(t, r, l, pieces)
                        else:
                            pieces(r, l, "B")
                        if r > 0 and 2 * l + 1 < 9:
                            chain_step(t, r - 1, 2 * l + 1)
                        if more and r == BATCHES:
                            if l == 0:
                                pe.wait_ge(tok_done, t * 6 + 6)
                                pe.wait_ge(wz_copied, t * 21 + 21)
                                pe.wait_ge(z_done, t * 24 + 24)
                            for i in SUMS[l]:
                                sums(t + 1, i)
                        for u in O_SUMS[l] if r == BATCHES else ():
                            o_sums(t, u, more)
                pieces(BATCHES, 0, "T")
                o_sums(t, 2, more)

            pro.tensor(pe)
            for n in range(U * KB):
                if n == 2 * KB:
                    pro.tensor_last(pe)
                piece(0, n)
            for i in range(6):
                sums(0, i)
            with pe.Fori(0, HEADS - 1) as t:
                head(t, True)
            head(HEADS - 1, False)
            pe.wait_ge(frames_taken, HEADS * 9)
            pe.wait_ge(oln_done, HEADS * 3)
            for g in range(2):
                pe.transpose(ps[0:R, g, 0:P], tails[:, g].rearrange("p f h -> p (f h)"), tk.ident[:]).then_inc(tails_turned, 1)

        @block.scalar
        def _(act):
            def evacuate(t, u, first):
                act.wait_ge(unit_done, t * U + (u + 1))
                b, n = u // NU, u % NU
                src = ps[:, u % 2, 0:UNIT]
                if b == 3:
                    dst = tk.x[:, bass.ds(t, 1), unit_cols(n)].rearrange("p a t -> p (a t)")
                    act.sem_inc(ws.act_checked, 1)
                    nc.scalar.copy(dst, src).then_inc(evacuated, 1)
                    return
                if b == 2:
                    act.wait_ge(conv_done, t * 3 + 1)
                elif not first:
                    act.wait_ge(conv_done, (t - 1) * 3 + (3, 2)[b])
                start = HIST + n * UNIT
                if n < NU - 1:
                    nc.scalar.copy(raw[:, b % 2, start:start + UNIT], src).then_inc(evacuated, 1)
                else:
                    cut = PROMPT - n * UNIT
                    nc.scalar.copy(raw[:, b % 2, start:start + cut], src[:, 0:cut])
                    nc.scalar.copy(raw[:, b % 2, PROMPT + 2 * HIST:], src[:, cut:]).then_inc(evacuated, 1)

            def silu(h, ch):
                act.wait_ge(conv_done, h * 3 + (ch + 1))
                place = conv[:, ch] if ch < 2 else qkv[:, 2, 0:CW]
                nc.scalar.activation(place, place, ACT.Silu).then_inc(silu_done, 1)

            def z_silu(h, n):
                act.wait_ge(evacuated, h * U + (2 + 3 * NU + n + 1))
                act.sem_inc(ws.act_checked, 1)
                place = tk.x[:, bass.ds(h, 1), unit_cols(n)].rearrange("p a t -> p (a t)")
                nc.scalar.activation(place, place, ACT.Silu).then_inc(z_silu_done, 1)

            def square(h, i):
                if i < 2:
                    act.wait_ge(silu_done, h * 3 + 2)
                else:
                    act.wait_ge(ss_done, h * 6 + (i - 1))
                nc.scalar.activation(sq[:, i % 2], conv[:, i // 3, i % 3 * CU:(i % 3 + 1) * CU],
                                     ACT.Square).then_inc(sq_done, 1)

            def root(h, i):
                act.wait_ge(ss_done, h * 6 + (i + 1))
                if i >= 2:
                    act.wait_ge(unit_len, h * 6 + (i - 1))
                dst = rs[:, i % 2]
                nc.scalar.activation(dst, ps[:, 2 + i % 4, 0:CU], ACT.Ln, bias=tk.eps[:, 0:1]).then_inc(ln_done, 1)
                act.wait_ge(ln_done, h * 6 + (i + 1))
                if i < 3:
                    nc.scalar.activation(dst, dst, ACT.Exp, scale=-0.5, bias=tk.log_dk[:, 0:1]).then_inc(rs_done, 1)
                else:
                    nc.scalar.activation(dst, dst, ACT.Exp, scale=-0.5).then_inc(rs_done, 1)

            def o_square(t, n):
                if n == 0:
                    act.wait_ge(wz_done, t * 21 + 21)
                    act.wait_ge(level_masked, t * 21 + 21)
                act.wait_ge(o_done, t * 9 + (3, 6, 9)[n])
                nc.scalar.activation(o_work[n], o[:, unit_cols(n)], ACT.Square).then_inc(osq_done, 1)

            def o_root(t, n):
                act.wait_ge(oss_done, t * 3 + (n + 1))
                nc.scalar.activation(o_work[n], ps[:, 4 + n, 0:UNIT], ACT.Ln, bias=tk.eps[:, 0:1],
                                     scale=1.0 / DV).then_inc(oln_done, 1)
                act.wait_ge(oln_done, t * 3 + (n + 1))
                nc.scalar.activation(o_work[n], o_work[n], ACT.Exp, scale=-0.5).then_inc(ors_done, 1)

            def prepare(t, r, pieces):
                act.wait_ge(e_done, t * 3 + (r + 1))
                nc.scalar.activation(gam[:], gam[:], ACT.Exp).then_inc(gam_done, 1)
                act.wait_ge(prep_done, t * 15 + (5 * r + 1))
                if r > 0:
                    act.wait_ge(made, t * 9 + 3 * r)
                d = ps[:, 2, 0:3 * P].rearrange("p (i c) -> p i c", i=3)
                nc.scalar.activation(exp_d[:], d, ACT.Exp).then_inc(expd_done, 1)
                if r == 2:
                    act.wait_ge(chain, t * 27 + 9)
                    act.wait_ge(y_done, t * 9 + 3)
                act.wait_ge(prep_done, t * 15 + (5 * r + 4))
                par = r % 2
                for i in range(BATCHES):
                    op = nc.scalar.mul(k_tail[:, par, i], ps[:, 5, i * P:(i + 1) * P],
                                       hg[:, 3, 3 * r + i:3 * r + i + 1])
                op.then_inc(tok_done, 1)
                pieces(r, 0, "P")
                act.wait_ge(prep_done, t * 15 + (5 * r + 5))
                nc.scalar.copy(v_tok[:, par], ps[:, 2, 0:3 * P].rearrange("p (i c) -> p i c", i=3)).then_inc(tok_done, 1)

            def copy_w(t, r, l):
                i = r * LEVELS + l
                act.wait_ge(wz_done, t * 21 + (i + 1))
                nc.scalar.copy(wz[:], ps[:, 3, 0:3 * P].rearrange("p (i c) -> p i c", i=3)).then_inc(wz_copied, 1)

            def chain_step(t, r, s):
                c = 3 * r + s // 3
                if s % 3 == 1:
                    act.wait_ge(chain, t * 27 + (3 * c + 2))
                    nc.scalar.copy(v_new[:], ps[:, 6, P:2 * P]).then_inc(vn_done, 1)
                elif s % 3 == 2:
                    act.wait_ge(chain, t * 27 + (3 * c + 3))
                    w = P if c < 8 else SAMPLE
                    nc.scalar.copy(o[:, c * P:c * P + w], ps[:, 7, 0:w]).then_inc(o_done, 1)

            def head(t, more):
                n = 0

                def pieces(r, l, place):
                    nonlocal n
                    for _ in range(fill(r, l, place) if more else 0):
                        if n % KB == KB - 1:
                            evacuate(t + 1, n // KB, False)
                        n += 1

                nc.scalar.preload_act_table_set("natural_log_exp_and_others")
                act.wait_ge(cols_taken, t + 1)
                for r in range(BATCHES + 1):
                    if r < BATCHES:
                        prepare(t, r, pieces)
                    for l in range(LEVELS):
                        if r < BATCHES:
                            copy_w(t, r, l)
                        pieces(r, l, "A")
                        if r > 0 and 2 * l < 9:
                            chain_step(t, r - 1, 2 * l)
                        pieces(r, l, "B")
                        if r > 0 and 2 * l + 1 < 9:
                            chain_step(t, r - 1, 2 * l + 1)
                        if r == 2 and 1 <= l < 1 + NU:
                            z_silu(t, l - 1)
                        if r == BATCHES:
                            for u in O_SQUARES[l]:
                                o_square(t, u)
                        if more and (r, l) == (2, 2):
                            silu(t + 1, 0)
                        if not more and (r, l) == (2, 4):
                            nc.scalar.preload_act_table_set("natural_log_exp_and_others")
                        if more and (r, l) == (2, 4):
                            silu(t + 1, 1)
                        if more and (r, l) == (2, 5):
                            square(t + 1, 0)
                            square(t + 1, 1)
                        if more and r == BATCHES:
                            for i in SQUARES[l]:
                                square(t + 1, i)
                            if l == 1:
                                silu(t + 1, 2)
                                nc.scalar.preload_act_table_set("natural_log_exp_and_others")
                            for i in ROOTS[l]:
                                root(t + 1, i)
                        if r == BATCHES:
                            for u in O_ROOTS[l]:
                                o_root(t, u)
                pieces(BATCHES, 0, "T")
                o_square(t, 2)
                o_root(t, 2)

            pro.scalar(act)
            for u in range(3 * NU):
                if u == 2:
                    pro.scalar_last(act)
                evacuate(0, u, True)
            for ch in range(3):
                silu(0, ch)
                evacuate(0, 3 * NU + ch, True)
            nc.scalar.preload_act_table_set("natural_log_exp_and_others")
            for i in range(6):
                square(0, i)
                if i >= 1:
                    root(0, i - 1)
            root(0, 5)
            with act.Fori(0, HEADS - 1) as t:
                head(t, True)
            head(HEADS - 1, False)

        @block.vector
        def _(dve):
            def take(dst, src):
                return nc.vector.tensor_scalar(dst, src, 1.0, None, ALU.mult)

            def take_taps(h):
                take(hw[:], conv_w[:, :, bass.ds(h, 1)].rearrange("p k a -> p (k a)")).then_inc(taps_taken, 1)

            def take_columns(h):
                take(hg[:].rearrange("p q c -> p (q c)"),
                     gates[:, :, :, bass.ds(h, 1)].rearrange("p q c a -> p (q c a)")).then_inc(cols_taken, 1)

            def convolve(h, ch, tap):
                src, slot = raw[:, ch % 2], ch % 2
                out = conv[:, ch] if ch < 2 else qkv[:, 2, 0:CW]
                if tap == 0:
                    dve.wait_ge(evacuated, h * U + (2 + NU * (ch + 1)))
                    past = hist[:, :, bass.ds(h, 1)].rearrange("p (f c) a -> p c (f a)", c=3)[:, ch]
                    take(raw[:, slot, GCOL:GCOL + HIST], past).then_inc(frames_taken, 1)
                    for g, start in ((0, PROMPT), (1, PROMPT + HIST + SAMPLE)):
                        dst = tails[:, g, :, bass.ds(h, 1)].rearrange("p (f c) a -> p c (f a)", c=3)[:, ch]
                        take(dst, raw[:, slot, start:start + HIST]).then_inc(frames_taken, 1)
                    dve.wait_ge(frames_taken, h * 9 + 3 * (ch + 1))
                    dve.wait_ge(taps_taken, h + 1)
                    nc.vector.tensor_scalar(out, src[:, 0:CW], hw[:, ch:ch + 1], None,
                                            ALU.mult).then_inc(conv_steps, 1)
                    return
                dve.wait_ge(conv_steps, h * 9 + (3 * ch + tap))
                nc.vector.scalar_tensor_tensor(
                    out=out, in0=src[:, tap:tap + CW], scalar=hw[:, tap * 3 + ch:tap * 3 + ch + 1],
                    in1=out, op0=ALU.mult, op1=ALU.add).then_inc(conv_done if tap == TAPS - 1 else conv_steps, 1)

            def scale(h, i):
                cols = slice(i % 3 * CU, (i % 3 + 1) * CU)
                dve.wait_ge(rs_done, h * 6 + (i + 1))
                nc.vector.tensor_tensor(qkv[:, i // 3, cols], conv[:, i // 3, cols], rs[:, i % 2],
                                        ALU.mult).then_inc(unit_len, 1)

            def prepare(t, r):
                par = r % 2
                dve.wait_ge(prep_done, t * 15 + (5 * r + 1))
                for i in range(BATCHES):
                    c = 3 * r + i
                    op = nc.vector.scalar_tensor_tensor(out=gam[:, i], in0=ps[:, 2, i * P:(i + 1) * P],
                                                        scalar=hg[:, 1, c:c + 1], in1=tk.later_neg[:],
                                                        op0=ALU.subtract, op1=ALU.add)
                op.then_inc(e_done, 1)
                if r == 2:
                    dve.wait_ge(chain, t * 27 + 9)
                for i in range(BATCHES):
                    c = 3 * r + i
                    op = nc.vector.tensor_scalar(z[:, par, :, i], tk.ident[:][:, None, :].to_broadcast([P, 2, P]),
                                                 hg[:, 0, c:c + 1], -1.0, ALU.mult, ALU.mult)
                op.then_inc(z_done, 1)
                dve.wait_ge(gam_done, t * 3 + (r + 1))
                dve.wait_ge(prep_done, t * 15 + (5 * r + 3))
                if r > 0:
                    dve.wait_ge(level_masked, t * 21 + 7 * r)
                grid = lambda bank: ps[:, bank, 0:3 * P].rearrange("p (i c) -> p i c", i=3)
                nc.vector.tensor_tensor(mt[:], grid(3), gam[:], ALU.mult).then_inc(made, 1)
                nc.vector.tensor_tensor(att[:, par], grid(4), gam[:], ALU.mult).then_inc(made, 1)
                dve.wait_ge(expd_done, t * 3 + (r + 1))
                if r < 2:
                    op = nc.vector.tensor_tensor(qd[:, par].rearrange("p i c -> p (i c)"),
                                                 qkv[:, 0, 3 * r * P:(3 * r + 3) * P],
                                                 exp_d[:].rearrange("p i c -> p (i c)"), ALU.mult)
                else:
                    for i in range(BATCHES):
                        op = nc.vector.tensor_tensor(qd[:, par, i], qkv[:, 0, tile_cols(3 * r + i)], exp_d[:, i], ALU.mult)
                op.then_inc(made, 1)

            def join(t, r, l):
                par, i = r % 2, r * LEVELS + l
                flat = lambda h: z[:, par, h].rearrange("p i c -> p (i c)")
                dve.wait_ge(z_done, t * 24 + (8 * r + l + 1))
                if l == 0:
                    dve.wait_ge(wz_copied, t * 21 + (i + 1))
                    for j in range(BATCHES):
                        c = 3 * r + j
                        op = nc.vector.scalar_tensor_tensor(out=z[:, par, 0, j], in0=wz[:, j], scalar=hg[:, 0, c:c + 1],
                                                            in1=z[:, par, 0, j], op0=ALU.mult, op1=ALU.add)
                    op.then_inc(z_first, 1)
                elif l < LEVELS - 1:
                    dve.wait_ge(pz_done, t * 36 + (12 * r + 2 * l))
                    nc.vector.tensor_tensor(flat(0), flat(0), ps[:, 4, 0:3 * P], ALU.subtract).then_inc(z_first, 1)
                dve.wait_ge(pz_done, t * 36 + (12 * r + min(2 * l + 1, 12)))
                nc.vector.tensor_tensor(flat(1), flat(1), ps[:, 5, 0:3 * P], ALU.subtract).then_inc(z_done, 1)

            def chain_step(t, r, s):
                par, i = r % 2, s // 3
                c = 3 * r + i
                g = c // 8
                if s % 3 == 0:
                    dve.wait_ge(chain, t * 27 + (3 * c + 1))
                    dve.wait_ge(tok_done, t * 6 + (2 * r + 2))
                    nc.vector.scalar_tensor_tensor(out=y[:], in0=ps[:, 6, 0:P], scalar=hg[:, 2, c:c + 1],
                                                   in1=v_tok[:, par, i], op0=ALU.mult, op1=ALU.add).then_inc(y_done, 1)
                elif s % 3 == 2:
                    dve.wait_ge(chain, t * 27 + (3 * c + 3))
                    dve.wait_ge(s_done, t * 9 + c) if c else dve.wait_ge(s_init, t + 1)
                    nc.vector.scalar_tensor_tensor(out=state[:, g], in0=state[:, g], scalar=hg[:, 4, c:c + 1],
                                                   in1=ps[:, 6, 2 * P:3 * P], op0=ALU.mult, op1=ALU.add).then_inc(s_done, 1)

            def finish(t, n):
                dve.wait_ge(ors_done, t * 3 + (n + 1))
                cols = o[:, unit_cols(n)]
                nc.vector.scalar_tensor_tensor(out=cols, in0=cols, scalar=gain[:, 0:1], in1=o_work[n],
                                               op0=ALU.mult, op1=ALU.mult).then_inc(o_normed, 1)
                dve.wait_ge(z_silu_done, t * 3 + (n + 1))
                dve.wait_ge(o_normed, t * 3 + (n + 1))
                dst = tk.x[:, bass.ds(t, 1), unit_cols(n)].rearrange("p a t -> p (a t)")
                nc.vector.tensor_tensor(dst, dst, cols, ALU.mult).then_inc(final_done, 1)

            def head(t, more):
                for r in range(BATCHES + 1):
                    if r < BATCHES:
                        prepare(t, r)
                    for l in range(LEVELS):
                        if r > 0 and 2 * l < 9:
                            chain_step(t, r - 1, 2 * l)
                        if r < BATCHES:
                            join(t, r, l)
                        if r > 0 and 2 * l + 1 < 9:
                            chain_step(t, r - 1, 2 * l + 1)
                        if (r, l) == (0, 2):
                            dve.wait_ge(s_out, t * 32 + 32)
                            nc.vector.memset(state[:, 0], 0.0).then_inc(s_init, 1)
                            if more:
                                take_taps(t + 1)
                        if more and (r, l) in taps:
                            if (r, l) == (2, 1):
                                dve.wait_ge(prep_done, t * 15 + 15)
                            convolve(t + 1, *taps[r, l])
                        if more and r == BATCHES:
                            for i in SCALED[l]:
                                if i == 3:
                                    dve.wait_ge(chain, t * 27 + 25)
                                scale(t + 1, i)
                finish(t, 0)
                if more:
                    dve.wait_ge(tok_done, t * 6 + 6)
                    take_columns(t + 1)
                finish(t, 1)
                finish(t, 2)

            pro.vector(dve)
            take_taps(0)
            take_columns(0)
            for ch in range(3):
                for tap in range(TAPS):
                    convolve(0, ch, tap)
            for i in range(6):
                scale(0, i)
            with dve.Fori(0, HEADS - 1) as t:
                head(t, True)
            head(HEADS - 1, False)

            for g in range(2):
                dve.wait_ge(tails_turned, g + 1)
                nc.vector.tensor_copy(tail_rows[0:R, g], ps[0:R, g, 0:P]).then_inc(tails_copied, 1)


def gdn_prologue(nc, tk, sem, buf, a, w_in, ws, gates, conv_w, hist, gain, raw, qkv, rows, ab_t):
    ps = tk.ps
    R, RH = TAPS * 3 * HEADS, HIST * 3 * HEADS
    ab = buf("p_ab", [P, TILES, 2 * HEADS], F32)
    rate = buf("p_rate", [P, HEADS], F32)
    dtb = buf("p_dtb", [P, HEADS], F32)
    tmp = buf("p_tmp", [P, 4, TILES, HEADS], F32)
    small_in, w_landed = sem("p_small_in"), sem("p_w_landed")
    zeroed, w_hi, w_split = sem("p_zeroed"), sem("p_w_hi"), sem("p_w_split")
    turned, copied, ab_done, ab_copied = sem("p_turned"), sem("p_copied"), sem("p_ab_done"), sem("p_ab_copied")
    step = sem("p_gate_steps")
    H = HEADS

    def sync(sp):
        sp.dma_start(ws.stage[:, 1, :, 0:2 * H], w_in[:, :, 4 * D:4 * D + 2 * H]).then_inc(w_landed, 16)
        sp.dma_start(rows[0:R, 0], a["gdn_conv_w"][0].rearrange("f (r c) -> (f r) c", c=P)).then_inc(small_in, 16)
        sp.dma_start(rows[0:RH, 1], a["state_gdn_conv"][0, 0].rearrange("f (r c) -> (f r) c", c=P)).then_inc(small_in, 16)
        sp.dma_start(gain[:], a["gdn_norm"].rearrange("a p -> p a"), allow_slow_non_contiguous=True).then_inc(small_in, 16)
        sp.dma_start(rate[:], a["gdn_a_log"].to_broadcast([P, H])).then_inc(small_in, 16)
        sp.dma_start(dtb[:], a["gdn_dt_bias"].to_broadcast([P, H])).then_inc(small_in, 16)

    def gpsimd(pool):
        ws.start(pool)
        nc.gpsimd.memset(ws.hi[:, 1].bitcast(F32), 0.0).then_inc(zeroed, 1)
        nc.gpsimd.memset(ws.lo[:, 1].bitcast(F32), 0.0).then_inc(zeroed, 1)
        pool.wait_ge(zeroed, 2)
        pool.wait_ge(w_landed, 16)
        st = ws.stage[:, 1, :, 0:2 * H]
        nc.gpsimd.tensor_tensor(ws.hi[:, 1, :, 0:2 * H], st,
                                tk.one[:][:, :, None].to_broadcast([P, KB, 2 * H]), ALU.mult).then_inc(w_hi, 1)
        pool.wait_ge(w_hi, 1)
        nc.gpsimd.tensor_tensor(ws.lo[:, 1, :, 0:2 * H], st, ws.hi[:, 1, :, 0:2 * H].bitcast(F32),
                                ALU.subtract).then_inc(w_split, 1)
        nc.gpsimd.memset(raw[:, :, 0:HIST], 0.0).then_inc(zeroed, 1)
        nc.gpsimd.memset(qkv[:, :, CW:CPAD], 0.0).then_inc(zeroed, 1)
        nc.gpsimd.memset(ab_t[:, TOK:TILES * P], -80.0).then_inc(zeroed, 1)

    def tensor(pe):
        pe.wait_ge(w_split, 1)
        for n in range(NU):
            for k in range(KB):
                mm = split_product(pe, ps[:, 4 + n, 0:UNIT], ws.hi[:, 1, k], ws.lo[:, 1, k],
                                   tk.hi[:, k, unit_cols(n)], tk.lo[:, k, unit_cols(n)], k == 0, k == KB - 1)
            mm.then_inc(ab_done, 1)
        pe.wait_ge(small_in, 80)
        pe.transpose(ps[:, 7, 0:R], rows[0:R, 0], tk.ident[0:R, 0:R]).then_inc(turned, 1)
        pe.transpose(ps[:, 7, R:R + RH], rows[0:RH, 1], tk.ident[0:RH, 0:RH]).then_inc(turned, 1)
        pe.wait_ge(ab_copied, NU)
        pe.wait_ge(zeroed, 5)
        for c in range(TILES):
            mm = pe.transpose(ps[:, 3, c * 2 * H:(c + 1) * 2 * H], ab_t[:, c * P:(c + 1) * P],
                              tk.ident[0:2 * H, 0:2 * H])
        mm.then_inc(step, 1)

    def tensor_last(pe):
        pe.wait_ge(step, 15)
        g = gates[:, 5].rearrange("p c h -> p (c h)")
        pe.matmul(ps[:, 6, 0:TILES * H], tk.upto[:], g, start=True, stop=True)
        pe.matmul(ps[:, 7, 0:TILES * H], tk.ones[:], g, start=True, stop=True).then_inc(step, 1)

    def do(act, n, *args, **kw):
        act.wait_ge(step, n - 1)
        nc.scalar.activation(*args, **kw).then_inc(step, 1)

    def scalar(act):
        nc.scalar.preload_act_table_set("natural_log_exp_and_others")
        do(act, 5, tmp[:, 1], tmp[:, 1], ACT.Exp)
        do(act, 6, tmp[:, 1], tmp[:, 1], ACT.Ln, bias=tk.one[:, 0:1])
        do(act, 8, rate[:], rate[:], ACT.Exp)
        do(act, 11, tmp[:, 2], ab[:, :, H:2 * H], ACT.Exp, scale=-1.0)

    def scalar_last(act):
        do(act, 19, tmp[:, 0], gates[:, 1], ACT.Exp)
        do(act, 20, gates[:, 3], gates[:, 3], ACT.Exp)
        do(act, 22, gates[:, 4], ps[:, 7, 0:TILES * H].rearrange("p (c h) -> p c h", c=TILES), ACT.Exp)

    def vector(dve):
        def after(n):
            dve.wait_ge(step, n - 1)
        dve.wait_ge(turned, 2)
        nc.vector.tensor_copy(conv_w[:].rearrange("p f h -> p (f h)"), ps[:, 7, 0:R]).then_inc(copied, 1)
        nc.vector.tensor_copy(hist[:].rearrange("p f h -> p (f h)"), ps[:, 7, R:R + RH]).then_inc(copied, 1)
        for n in range(NU):
            dve.wait_ge(ab_done, n + 1)
            nc.vector.tensor_copy(ab_t[:, unit_cols(n)], ps[0:2 * H, 4 + n, 0:UNIT]).then_inc(ab_copied, 1)
        dve.wait_ge(small_in, 80)
        after(2)
        nc.vector.tensor_copy(ab[:].rearrange("p c h -> p (c h)"), ps[:, 3, 0:TILES * 2 * H]).then_inc(step, 1)
        after(3)
        nc.vector.tensor_tensor(tmp[:, 0], ab[:, :, 0:H], dtb[:][:, None, :].to_broadcast([P, TILES, H]),
                                ALU.add).then_inc(step, 1)
        after(4)
        nc.vector.tensor_scalar(tmp[:, 3], tmp[:, 0], 0.0, None, ALU.max).then_inc(copied, 1)
        dve.wait_ge(copied, 3)
        nc.vector.scalar_tensor_tensor(out=tmp[:, 1], in0=tmp[:, 3], scalar=-2.0, in1=tmp[:, 0],
                                       op0=ALU.mult, op1=ALU.add).then_inc(step, 1)
        after(7)
        nc.vector.tensor_tensor(tmp[:, 0], tmp[:, 3], tmp[:, 1], ALU.add).then_inc(step, 1)
        after(9)
        nc.vector.scalar_tensor_tensor(out=gates[:, 5], in0=tmp[:, 0], scalar=-1.0,
                                       in1=rate[:][:, None, :].to_broadcast([P, TILES, H]),
                                       op0=ALU.mult, op1=ALU.mult).then_inc(step, 1)
        after(10)
        nc.vector.tensor_scalar(gates[:, 5, TILES - 1], gates[:, 5, TILES - 1],
                                tk.upto[:, SAMPLE - 1:SAMPLE], None, ALU.mult).then_inc(step, 1)
        after(12)
        nc.vector.tensor_scalar(tmp[:, 3], tmp[:, 2], 1.0, -1.0, ALU.add, ALU.mult).then_inc(step, 1)
        after(13)
        nc.vector.reciprocal(gates[:, 0], tmp[:, 3]).then_inc(step, 1)
        after(14)
        nc.vector.tensor_scalar(gates[:, 0, TILES - 1], gates[:, 0, TILES - 1],
                                tk.upto[:, SAMPLE - 1:SAMPLE], None, ALU.mult).then_inc(step, 2)
        after(17)
        nc.vector.tensor_copy(gates[:, 1].rearrange("p c h -> p (c h)"), ps[:, 6, 0:TILES * H]).then_inc(step, 1)
        after(18)
        nc.vector.scalar_tensor_tensor(out=gates[:, 3].rearrange("p c h -> p (c h)"),
                                       in0=gates[:, 1].rearrange("p c h -> p (c h)"), scalar=-1.0,
                                       in1=ps[:, 7, 0:TILES * H], op0=ALU.mult, op1=ALU.add).then_inc(step, 1)
        after(21)
        nc.vector.tensor_scalar(gates[:, 2], tmp[:, 0], -1.0, None, ALU.mult).then_inc(step, 1)
        dve.wait_ge(step, 22)

    pro = Parts()
    pro.sync, pro.gpsimd, pro.tensor, pro.tensor_last, pro.scalar = sync, gpsimd, tensor, tensor_last, scalar
    pro.scalar_last, pro.vector, pro.w_split, pro.ab_done = scalar_last, vector, w_split, ab_done
    return pro




def mlstm_phase(nc, tk, a):
    ps = tk.ps
    B = 3
    U = B * NU
    FILL = (3, 4, 4, 4)
    W_QK = HEADS * MDK
    w_in = a["ml_w_in"][0].rearrange("(k p) f -> p k f", p=P)
    NQ = 5
    with ExitStack() as ctx:
        sem = semaphores(nc, ctx, "ml", again=True)
        buf = lambda s, *sh: ctx.enter_context(nc.sbuf_tensor(f"ml_{s}", *sh))
        ws = WeightStream(nc, tk, ctx, sem, "ml", 3, stages=3)
        gates = buf("gates", [P, NQ + 1, TILES, HEADS], F32)
        gain = buf("gain", [P, HEADS], F32)
        m_end = buf("m_end", [P, 2, HEADS], F32)
        raw = buf("raw", [P, 3, TOK], F32)
        qkv = buf("qkv", [P, 3, TILES * P], F32)
        hg = buf("head_gates", [P, NQ + 1, TILES], F32)
        hgain = buf("head_gain", [P, 1], F32)
        num = buf("num", [P, TILES * P], F32)
        den = buf("den", [P, TILES * P], F32)
        sq = buf("sq", [P, 2, UNIT], F32)
        rs = buf("rs", [P, NU, UNIT], F32)
        pe_exp = buf("exponents", [P, BATCHES, P], F32)
        q_scale = buf("q_scale", [P, BATCHES, P], F32)
        floor = buf("floor", [P, 2, BATCHES, P], F32)
        pt = buf("pt", [P, 2, BATCHES, P], F32)
        qs = buf("qs", [MDK, 2, BATCHES, P], F32)
        kw = buf("kw", [P, 2, BATCHES, MDK], F32)
        v_tok = buf("v_tok", [P, 2, BATCHES, DV + 1], F32)
        state = buf("state", [MDK, 2, DV + 1], F32)

        def load(sp, t, ahead, b):
            if b == 0:
                ws.wait_stage(sp, t * B + ahead * B)
                for h in range(2):
                    sp.dma_start(ws.stage[:, 0, :, h * MDK:(h + 1) * MDK],
                                 w_in[:, :, bass.ds(t * MDK + (ahead * MDK + h * W_QK), MDK)]).then_inc(ws.landed[0], 16)
            else:
                start = 2 * W_QK + (b - 1) * D + ahead * P
                ws.load(sp, t * B + (ahead * B + b), b, w_in[:, :, bass.ds(t * P + start, P)])

        pro = mlstm_prologue(nc, tk, sem, buf, a, w_in, ws, gates, gain, m_end, qkv, v_tok, num[0:2 * HEADS])
        unit_done, evacuated = sem("unit_done"), sem("evacuated")
        taken, cols_done, gain_taken, gated = sem("raw_taken"), sem("cols_done"), sem("gain_taken"), sem("sigmoid_done")
        prep_done, qsc_done, e_done, exp_done = sem("prep_done"), sem("q_scale_done"), sem("e_done"), sem("exp_done")
        floor_done, tok_done, made = sem("floor_done"), sem("tok_done"), sem("p_and_q_made")
        chain, num_done, den_done, s_done = sem("chain"), sem("num_done"), sem("den_done"), sem("s_done")
        s_in, s_out, s_init = sem("state_landed"), sem("state_stored"), sem("state_zeroed")
        sq_done, ss_done, v_done, ln_done, rs_done = (sem("sq_done"), sem("ss_done"), sem("v_done"), sem("ln_done"),
                                                      sem("rs_done"))
        negative_done, den2_done, clamped = sem("negative_done"), sem("den2_done"), sem("clamped")
        o_normed, final_done, m_out = sem("o_normed"), sem("final_done"), sem("m_stored")
        block = ctx.enter_context(nc.Block())

        @block.sync
        def _(sp):
            def weights(t, ahead, b):
                load(sp, t, ahead, b)

            def states(t):
                sp.dma_start(state[:, 1, 0:DV], a["state_mlstm_C"][0, 0, t]).then_inc(s_in, 16)
                sp.dma_start(state[:, 1, DV:DV + 1], a["state_mlstm_n"][0, 0, t][:, None]).then_inc(s_in, 16)

            def store(t):
                sp.wait_ge(s_done, t * 9 + 9)
                sp.sem_inc(ws.checked, 1)
                for g, name in enumerate(("p", "s")):
                    sp.dma_start(a[f"{name}_C"][0, 0, t], state[:, g, 0:DV]).then_inc(s_out, 16)
                    sp.dma_start(a[f"{name}_n"][0, 0, t][:, None], state[:, g, DV:DV + 1]).then_inc(s_out, 16)

            def head(t, ahead):
                for b in range(1, B) if ahead >= 1 else ():
                    weights(t, 1, b)
                if ahead == 2:
                    weights(t, 2, 0)
                store(t)
                if ahead >= 1:
                    sp.wait_ge(s_out, t * 64 + 128)
                    sp.sem_inc(ws.checked, 1)
                    states(t + 1)

            pro.sync(sp)
            weights(0, 0, 0)
            weights(0, 0, 1)
            sp.wait_ge(pro.w_split, 1)
            weights(0, 0, 2)
            states(0)
            weights(0, 1, 0)
            with sp.Fori(0, HEADS - 2) as t:
                head(t, 2)
            head(HEADS - 2, 1)
            head(HEADS - 1, 0)
            sp.wait_ge(pro.step, 56)
            for g, name in enumerate(("p", "s")):
                sp.dma_start(a[f"{name}_m"][0], m_end[0:1, g]).then_inc(m_out, 16)
            sp.wait_ge(s_out, HEADS * 64 + 64)
            sp.wait_ge(m_out, 32)

        @block.gpsimd
        def _(pool):
            pro.gpsimd(pool)
            pool.sem_inc(evacuated, 2)
            pool.sem_inc(s_out, 64)

            def weights(t, ahead, b):
                if ahead >= 1:
                    pool.wait_ge(unit_done, t * U + ((ahead - 1) * U + NU * (b + 1)))
                dmas = 32 if b == 0 else 16
                ws.split(pool, t * B + (ahead * B + b), b, t * dmas + (ahead * dmas + dmas), b)

            weights(0, 0, 0)
            weights(0, 0, 1)
            pool.wait_ge(pro.ab_done, NU)
            weights(0, 0, 2)
            weights(0, 1, 0)
            with pool.Fori(0, HEADS - 2) as t:
                for ahead, b in ((1, 1), (1, 2), (2, 0)):
                    weights(t, ahead, b)
            for b in range(1, B):
                weights(HEADS - 2, 1, b)

        @block.tensor
        def _(pe):
            def piece(t, n):
                u, third = n // 3, n % 3
                b, cols = u // NU, unit_cols(u % NU)
                if n % 9 == 0:
                    ws.wait_ready(pe, t * B + b)
                if third == 0:
                    pe.wait_ge(evacuated, t * U + max(u + 1, 2))
                for k in range(3 * third, min(3 * third + 3, KB)):
                    mm = split_product(pe, ps[:, u % 2, 0:UNIT], ws.hi[:, b, k], ws.lo[:, b, k],
                                       tk.hi[:, k, cols], tk.lo[:, k, cols], k == 0, k == KB - 1)
                if third == 2:
                    mm.then_inc(unit_done, 1)

            def rows_of(bank, q, r):
                for i in range(BATCHES):
                    c = 3 * r + i
                    mm = pe.matmul(ps[:, bank, i * P:(i + 1) * P], hg[:, q, c:c + 1].to_broadcast([P, P]),
                                   tk.ident[:], start=True, stop=True)
                mm.then_inc(prep_done, 1)

            def prepare(t, r, pieces):
                if r > 0:
                    pe.wait_ge(tok_done, t * 6 + 2 * r)
                rows_of(2, 1, r)
                if r > 0:
                    pe.wait_ge(made, t * 6 + 2 * r)
                for i in range(BATCHES):
                    cols = slice((3 * r + i) * P, (3 * r + i + 1) * P)
                    mm = pe.matmul(ps[:, 3, i * P:(i + 1) * P], qkv[0:MDK, 1, cols], qkv[0:MDK, 0, cols],
                                   start=True, stop=True)
                mm.then_inc(prep_done, 1)
                if r > 0:
                    pe.wait_ge(floor_done, t * 3 + r)
                rows_of(4, 2, r)
                for i in range(BATCHES):
                    mm = pe.transpose(ps[:, 5, i * MDK:(i + 1) * MDK], qkv[0:MDK, 1, (3 * r + i) * P:(3 * r + i + 1) * P],
                                      tk.ident[0:MDK, 0:MDK])
                mm.then_inc(prep_done, 1)
                pieces(2)
                pe.wait_ge(qsc_done, t * 3 + (r + 1))
                pe.wait_ge(e_done, t * 3 + (r + 1))
                for i in range(BATCHES):
                    mm = pe.transpose(ps[:, 2, i * P:(i + 1) * P], qkv[:, 2, (3 * r + i) * P:(3 * r + i + 1) * P], tk.ident[:])
                mm.then_inc(prep_done, 1)

            def chunk(t, r, i):
                par, c = r % 2, 3 * r + i
                g = c // 8
                if i == 0:
                    pe.wait_ge(made, t * 6 + (2 * r + 2))
                    pe.wait_ge(tok_done, t * 6 + (2 * r + 2))
                if c == 0:
                    pe.wait_ge(s_init, t + 1)
                else:
                    pe.wait_ge(s_done, t * 9 + c)
                    pe.wait_ge(num_done, t * 9 + c)
                if c == 8:
                    pe.wait_ge(s_in, t * 32 + 32)
                pe.matmul(ps[:, 6, 0:P], state[:, g, 0:DV], qs[:, par, i], start=True, stop=False)
                pe.matmul(ps[:, 6, 0:P], v_tok[:, par, i, 0:DV], pt[:, par, i], start=False, stop=True).then_inc(chain, 1)
                pe.matmul(ps[:, 7, 0:P], state[:, g, DV:DV + 1].to_broadcast([MDK, P]), qs[:, par, i],
                          start=True, stop=False)
                pe.matmul(ps[:, 7, 0:P], tk.ones[:], pt[:, par, i], start=False, stop=True)
                pe.matmul(ps[0:MDK, 7, P:2 * P + 1], kw[:, par, i], v_tok[:, par, i],
                          start=True, stop=True).then_inc(chain, 1)

            def sums(t, n):
                pe.wait_ge(sq_done, t * 3 + (n + 1))
                if n == 0:
                    pe.wait_ge(num_done, t * 9 + 9)
                    pe.wait_ge(s_done, t * 9 + 9)
                if n == 2:
                    pe.wait_ge(v_done, t * 3 + 1)
                pe.matmul(ps[:, 6 + n % 2, 0:UNIT], tk.ones[:], sq[:, n % 2], start=True, stop=True).then_inc(ss_done, 1)

            def head(t, more):
                n = 0

                def pieces(count):
                    nonlocal n
                    for _ in range(count if more else 0):
                        piece(t + 1, n)
                        n += 1

                pe.wait_ge(cols_done, t + 1)
                pe.wait_ge(taken, t * 3 + 3)
                for r in range(BATCHES + 1):
                    if r < BATCHES:
                        prepare(t, r, pieces)
                    for i in range(BATCHES):
                        pieces(FILL[r] // BATCHES + (i < FILL[r] % BATCHES))
                        if r > 0:
                            chunk(t, r - 1, i)
                for u in range(NU):
                    pieces(2)
                    sums(t, u)

            gate_steps = pro.tensor(pe)
            for n in range(27):
                if n % 3 == 0:
                    next(gate_steps, None)
                piece(0, n)
            with pe.Fori(0, HEADS - 1) as t:
                head(t, True)
            head(HEADS - 1, False)

        @block.scalar
        def _(act):
            def evacuate(t, u, first):
                act.wait_ge(unit_done, t * U + (u + 1))
                b, n = u // NU, u % NU
                src = ps[:, u % 2, 0:UNIT]
                if b == 2:
                    dst = tk.x[:, bass.ds(t, 1), unit_cols(n)].rearrange("p a t -> p (a t)")
                    act.sem_inc(ws.act_checked, 1)
                    nc.scalar.copy(dst, src).then_inc(evacuated, 1)
                    return
                if not first:
                    act.wait_ge(taken, (t - 1) * 3 + (2 + b))
                if b == 0:
                    nc.scalar.copy(raw[0:MDK, 0, unit_cols(n)], src[0:MDK])
                    nc.scalar.copy(raw[0:MDK, 1, unit_cols(n)], src[MDK:P]).then_inc(evacuated, 1)
                else:
                    nc.scalar.copy(raw[:, 2, unit_cols(n)], src).then_inc(evacuated, 1)

            def gate(t, n):
                act.wait_ge(evacuated, t * U + (2 + 2 * NU + n + 1))
                act.sem_inc(ws.act_checked, 1)
                place = tk.x[:, bass.ds(t, 1), unit_cols(n)].rearrange("p a t -> p (a t)")
                nc.scalar.activation(place, place, ACT.Sigmoid).then_inc(gated, 1)

            def prepare(t, r, pieces):
                par = r % 2
                grid = lambda bank: ps[:, bank, 0:3 * P].rearrange("p (i c) -> p i c", i=3)
                act.wait_ge(prep_done, t * 15 + (5 * r + 1))
                if r > 0:
                    act.wait_ge(made, t * 6 + 2 * r)
                for i in range(BATCHES):
                    c = 3 * r + i
                    op = nc.scalar.activation(q_scale[:, i], ps[:, 2, i * P:(i + 1) * P], ACT.Exp,
                                              bias=hg[:, 4, c:c + 1], scale=-1.0)
                op.then_inc(qsc_done, 1)
                act.wait_ge(e_done, t * 3 + (r + 1))
                nc.scalar.activation(pe_exp[:], pe_exp[:], ACT.Exp, scale=-1.0).then_inc(exp_done, 1)
                act.wait_ge(prep_done, t * 15 + (5 * r + 3))
                if r == 2:
                    act.wait_ge(den_done, t * 9 + 3)
                    act.wait_ge(chain, t * 18 + 6)
                nc.scalar.activation(floor[:, par], grid(4), ACT.Exp, scale=-1.0).then_inc(floor_done, 1)
                act.wait_ge(prep_done, t * 15 + (5 * r + 4))
                for i in range(BATCHES):
                    c = 3 * r + i
                    op = nc.scalar.mul(kw[:, par, i], ps[:, 5, i * MDK:(i + 1) * MDK], hg[:, 3, c:c + 1])
                op.then_inc(tok_done, 1)
                pieces(2)
                act.wait_ge(prep_done, t * 15 + (5 * r + 5))
                nc.scalar.copy(v_tok[:, par, :, 0:DV], grid(2)).then_inc(tok_done, 1)

            def chunk(t, r, i):
                c = 3 * r + i
                act.wait_ge(chain, t * 18 + (2 * c + 1))
                nc.scalar.copy(num[:, c * P:(c + 1) * P], ps[:, 6, 0:P]).then_inc(num_done, 1)

            def head(t, more):
                n = 0

                def pieces(count):
                    nonlocal n
                    for _ in range(count if more else 0):
                        if n % 3 == 2:
                            evacuate(t + 1, n // 3, False)
                        n += 1

                act.wait_ge(cols_done, t + 1)
                for r in range(BATCHES + 1):
                    if r < BATCHES:
                        prepare(t, r, pieces)
                    for i in range(BATCHES):
                        pieces(FILL[r] // BATCHES + (i < FILL[r] % BATCHES))
                        if r > 0:
                            chunk(t, r - 1, i)
                        if (r, i) == (2, 0):
                            for u in range(NU):
                                gate(t, u)
                            nc.scalar.preload_act_table_set("natural_log_exp_and_others")
                act.wait_ge(num_done, t * 9 + 9)
                act.wait_ge(den_done, t * 9 + 9)
                nc.scalar.activation(den[:, 0:TOK], den[:, 0:TOK], ACT.Square,
                                     scale=math.sqrt(DV * RMS_EPS)).then_inc(den2_done, 1)
                for u in range(NU):
                    if u >= 2:
                        act.wait_ge(ss_done, t * 3 + (u - 1))
                    nc.scalar.activation(sq[:, u % 2], num[:, unit_cols(u)], ACT.Square).then_inc(sq_done, 1)
                    pieces(2)
                for u in range(NU):
                    act.wait_ge(clamped, t * 3 + (u + 1))
                    nc.scalar.activation(rs[:, u], rs[:, u], ACT.Ln, scale=1.0 / DV).then_inc(ln_done, 1)
                    act.wait_ge(ln_done, t * 3 + (u + 1))
                    nc.scalar.activation(rs[:, u], rs[:, u], ACT.Exp, scale=-0.5).then_inc(rs_done, 1)

            pro.scalar(act)
            for u in range(U):
                if u == 3:
                    pro.scalar_last(act)
                evacuate(0, u, True)
            with act.Fori(0, HEADS - 1) as t:
                head(t, True)
            head(HEADS - 1, False)

        @block.vector
        def _(dve):
            def take(dst, src):
                return nc.vector.tensor_scalar(dst, src, 1.0, None, ALU.mult)

            def prepare(t, r):
                par = r % 2
                dve.wait_ge(prep_done, t * 15 + (5 * r + 1))
                dve.wait_ge(qsc_done, t * 3 + (r + 1))
                for i in range(BATCHES):
                    c = 3 * r + i
                    op = nc.vector.scalar_tensor_tensor(out=pe_exp[:, i], in0=ps[:, 2, i * P:(i + 1) * P],
                                                        scalar=hg[:, 0, c:c + 1], in1=tk.later_neg[:],
                                                        op0=ALU.subtract, op1=ALU.subtract)
                op.then_inc(e_done, 1)
                dve.wait_ge(exp_done, t * 3 + (r + 1))
                dve.wait_ge(prep_done, t * 15 + (5 * r + 2))
                if r == 2:
                    dve.wait_ge(chain, t * 18 + 6)
                nc.vector.scalar_tensor_tensor(out=pt[:, par].rearrange("p i c -> p (i c)"), in0=ps[:, 3, 0:3 * P],
                                               scalar=MDK ** -0.5, in1=pe_exp[:].rearrange("p i c -> p (i c)"),
                                               op0=ALU.mult, op1=ALU.mult).then_inc(made, 1)
                nc.vector.tensor_tensor(qs[:, par].rearrange("p i c -> p (i c)"),
                                        qkv[0:MDK, 0, 3 * r * P:(3 * r + 3) * P],
                                        q_scale[0:MDK].rearrange("p i c -> p (i c)"), ALU.mult).then_inc(made, 1)

            def chunk(t, r, i):
                par, c = r % 2, 3 * r + i
                g = c // 8
                dve.wait_ge(chain, t * 18 + (2 * c + 2))
                dve.wait_ge(s_done, t * 9 + c) if c else dve.wait_ge(s_init, t + 1)
                nc.vector.scalar_tensor_tensor(out=state[:, g], in0=state[:, g], scalar=hg[0:MDK, 5, c:c + 1],
                                               in1=ps[0:MDK, 7, P:2 * P + 1], op0=ALU.mult, op1=ALU.add)
                dve.wait_ge(floor_done, t * 3 + (r + 1))
                part = den[:, c * P:(c + 1) * P]
                nc.vector.scalar_tensor_tensor(out=part, in0=ps[:, 7, 0:P], scalar=-1.0, in1=floor[:, par, i],
                                               op0=ALU.mult, op1=ALU.max).then_inc(negative_done, 1)
                dve.wait_ge(negative_done, t * 9 + (c + 1))
                nc.vector.tensor_tensor(part, part, ps[:, 7, 0:P], ALU.max).then_inc(den_done, 1)
                dve.wait_ge(den_done, t * 9 + (c + 1))
                dve.sem_inc(s_done, 1)

            def take_columns(h):
                take(hg[:].rearrange("p q c -> p (q c)"),
                     gates[:, :, :, bass.ds(h, 1)].rearrange("p q c a -> p (q c a)")).then_inc(cols_done, 1)

            def take_raw(h, j):
                rows = P if j == 2 else MDK
                dve.wait_ge(evacuated, h * U + (2 + NU * (2 if j == 2 else 1)))
                nc.vector.tensor_copy(qkv[0:rows, j, 0:TOK], raw[0:rows, j]).then_inc(taken, 1)

            def head(t, more):
                for r in range(BATCHES + 1):
                    if r < BATCHES:
                        prepare(t, r)
                    if r == 0:
                        take(hgain[:], gain[:, bass.ds(t, 1)]).then_inc(gain_taken, 1)
                        dve.wait_ge(s_out, t * 64 + 64)
                        nc.vector.memset(state[:, 0], 0.0).then_inc(s_init, 1)
                    for i in range(BATCHES):
                        if r > 0:
                            chunk(t, r - 1, i)
                        if more and (r, i) == (2, 2):
                            dve.wait_ge(prep_done, t * 15 + 15)
                            take_raw(t + 1, 0)
                            take_raw(t + 1, 1)
                        if more and (r, i) == (3, 1):
                            take_raw(t + 1, 2)
                if more:
                    dve.wait_ge(tok_done, t * 6 + 6)
                    take_columns(t + 1)
                for n in range(NU):
                    dve.wait_ge(ss_done, t * 3 + (n + 1))
                    dve.wait_ge(den2_done, t + 1)
                    nc.vector.tensor_tensor(rs[:, n], ps[:, 6 + n % 2, 0:UNIT], den[:, unit_cols(n)],
                                            ALU.add).then_inc(v_done, 1)
                    dve.wait_ge(v_done, t * 3 + (n + 1))
                    nc.vector.tensor_scalar(rs[:, n], rs[:, n], 1e-16, 1e19, ALU.max, ALU.min).then_inc(clamped, 1)
                dve.wait_ge(gain_taken, t + 1)
                for n in range(NU):
                    dve.wait_ge(rs_done, t * 3 + (n + 1))
                    cols = num[:, unit_cols(n)]
                    nc.vector.scalar_tensor_tensor(out=cols, in0=cols, scalar=hgain[:, 0:1], in1=rs[:, n],
                                                   op0=ALU.mult, op1=ALU.mult).then_inc(o_normed, 1)
                    dve.wait_ge(gated, t * 3 + (n + 1))
                    dve.wait_ge(o_normed, t * 3 + (n + 1))
                    dst = tk.x[:, bass.ds(t, 1), unit_cols(n)].rearrange("p a t -> p (a t)")
                    nc.vector.tensor_tensor(dst, dst, cols, ALU.mult).then_inc(final_done, 1)

            pro.vector(dve)
            take_columns(0)
            for j in range(3):
                take_raw(0, j)
            with dve.Fori(0, HEADS - 1) as t:
                head(t, True)
            head(HEADS - 1, False)


def mlstm_prologue(nc, tk, sem, buf, a, w_in, ws, gates, gain, m_end, qkv, v_tok, ab_t):
    ps = tk.ps
    H = HEADS
    R = TILES * H
    ab = buf("p_if", [P, TILES, 2 * H], F32)
    bias_i, bias_f = buf("p_bias_i", [P, H], F32), buf("p_bias_f", [P, H], F32)
    out_of = buf("p_out_of", [P, 1], F32)
    x, e, mn, lf = buf("p_x", [P, TILES, H], F32), buf("p_e", [P, TILES, H], F32), buf("p_mn", [P, TILES, H], F32), buf("p_lf", [P, TILES, H], F32)
    b, last = buf("p_b", [P, TILES, H], F32), buf("p_last", [P, TILES, H], F32)
    rows = buf("p_rows", [R, 2, P], F32)
    end = buf("p_end", [P, TILES, H], F32)
    small_in, w_landed = sem("p_small_in"), sem("p_w_landed")
    zeroed, w_hi, w_split = sem("p_zeroed"), sem("p_w_hi"), sem("p_w_split")
    ab_done, ab_copied, step = sem("p_if_done"), sem("p_if_copied"), sem("p_steps")
    flat = lambda t: t.rearrange("p c h -> p (c h)")

    def sync(sp):
        sp.dma_start(ws.stage[:, 2, :, 0:2 * H], w_in[:, :, 3 * D:3 * D + 2 * H]).then_inc(w_landed, 16)
        sp.dma_start(gain[:], a["ml_norm"][0].rearrange("(h p) -> p h", p=P), allow_slow_non_contiguous=True).then_inc(small_in, 16)
        sp.dma_start(bias_i[:], a["ml_b_i"].to_broadcast([P, H])).then_inc(small_in, 16)
        sp.dma_start(bias_f[:], a["ml_b_f"].to_broadcast([P, H])).then_inc(small_in, 16)
        sp.dma_start(m_end[:, 1], a["state_mlstm_m"][0].to_broadcast([P, H])).then_inc(small_in, 16)

    def gpsimd(pool):
        ws.start(pool)
        nc.gpsimd.memset(ws.hi[:, 2].bitcast(F32), 0.0).then_inc(zeroed, 1)
        nc.gpsimd.memset(ws.lo[:, 2].bitcast(F32), 0.0).then_inc(zeroed, 1)
        pool.wait_ge(zeroed, 2)
        pool.wait_ge(w_landed, 16)
        st = ws.stage[:, 2, :, 0:2 * H]
        nc.gpsimd.tensor_tensor(ws.hi[:, 2, :, 0:2 * H], st,
                                tk.one[:][:, :, None].to_broadcast([P, KB, 2 * H]), ALU.mult).then_inc(w_hi, 1)
        pool.wait_ge(w_hi, 1)
        nc.gpsimd.tensor_tensor(ws.lo[:, 2, :, 0:2 * H], st, ws.hi[:, 2, :, 0:2 * H].bitcast(F32),
                                ALU.subtract).then_inc(w_split, 1)
        nc.gpsimd.memset(qkv[:, :, TOK:TILES * P], 0.0).then_inc(zeroed, 1)
        nc.gpsimd.memset(ab_t[:, TOK:TILES * P], 0.0).then_inc(zeroed, 1)
        nc.gpsimd.memset(v_tok[:, :, :, DV:DV + 1], 1.0).then_inc(zeroed, 1)

    def tensor(pe):
        pe.wait_ge(w_split, 1)
        for n in range(NU):
            for k in range(KB):
                mm = split_product(pe, ps[:, 4 + n, 0:UNIT], ws.hi[:, 2, k], ws.lo[:, 2, k],
                                   tk.hi[:, k, unit_cols(n)], tk.lo[:, k, unit_cols(n)], k == 0, k == KB - 1)
            mm.then_inc(ab_done, 1)
        pe.wait_ge(ab_copied, NU)
        pe.wait_ge(zeroed, 5)
        for c in range(TILES):
            mm = pe.transpose(ps[:, 3, c * 2 * H:(c + 1) * 2 * H], ab_t[:, c * P:(c + 1) * P],
                              tk.ident[0:2 * H, 0:2 * H])
        mm.then_inc(step, 1)
        yield
        pe.wait_ge(step, 11)
        pe.matmul(ps[:, 4, 0:R], tk.upto[:], flat(lf[:]), start=True, stop=True)
        pe.matmul(ps[:, 5, 0:R], tk.ones[:], flat(lf[:]), start=True, stop=True).then_inc(step, 1)
        yield
        pe.wait_ge(step, 15)
        pe.transpose(ps[0:R, 6, 0:P], flat(gates[:, 0]), tk.ident[:]).then_inc(step, 1)
        yield
        pe.wait_ge(step, 24)
        pe.transpose(ps[:, 7, 0:R], rows[:, 1], tk.ident[0:R, 0:R]).then_inc(step, 1)
        pe.wait_ge(step, 26)
        pe.matmul(ps[:, 3, 0:R], tk.ident[:, P - 1:P].to_broadcast([P, P]), flat(gates[:, 1]),
                  start=True, stop=True).then_inc(step, 1)

    def do(act, n, *args, **kw):
        act.wait_ge(step, n - 1)
        nc.scalar.activation(*args, **kw).then_inc(step, 1)

    def scalar(act):
        nc.scalar.preload_act_table_set("natural_log_exp_and_others")
        do(act, 6, e[:], e[:], ACT.Exp)
        do(act, 7, e[:], e[:], ACT.Ln, bias=tk.one[:, 0:1])

    def scalar_last(act):
        do(act, 51, gates[:, 5], gates[:, 5], ACT.Exp)
        do(act, 53, gates[:, 3], gates[:, 3], ACT.Exp)

    def vector(dve):
        def do(n, op, *args, **kw):
            dve.wait_ge(step, n - 1)
            op(*args, **kw).then_inc(step, 1)
        tt, stt, ts, cp = nc.vector.tensor_tensor, nc.vector.scalar_tensor_tensor, nc.vector.tensor_scalar, nc.vector.tensor_copy
        over = lambda t: t[:][:, None, :].to_broadcast([P, TILES, H])
        for n in range(NU):
            dve.wait_ge(ab_done, n + 1)
            cp(ab_t[:, unit_cols(n)], ps[0:2 * H, 4 + n, 0:UNIT]).then_inc(ab_copied, 1)
        dve.wait_ge(small_in, 64)
        do(2, cp, flat(ab[:]), ps[:, 3, 0:TILES * 2 * H])
        do(3, tt, x[:], ab[:, :, H:2 * H], over(bias_f), ALU.add)
        do(4, ts, mn[:], x[:], 0.0, None, ALU.min)
        do(5, stt, out=e[:], in0=mn[:], scalar=2.0, in1=x[:], op0=ALU.mult, op1=ALU.subtract)
        do(8, tt, lf[:], mn[:], e[:], ALU.subtract)
        do(9, ts, out_of[:], tk.upto[:, SAMPLE - 1:SAMPLE], 1.0, -NEG, ALU.subtract, ALU.mult)
        do(10, tt, x[:], ab[:, :, 0:H], over(bias_i), ALU.add)
        do(11, ts, lf[:, TILES - 1], lf[:, TILES - 1], tk.upto[:, SAMPLE - 1:SAMPLE], None, ALU.mult)
        do(13, cp, flat(b[:]), ps[:, 4, 0:R])
        do(14, ts, x[:, TILES - 1], x[:, TILES - 1], out_of[:, 0:1], None, ALU.add)
        do(15, tt, gates[:, 0], x[:], b[:], ALU.subtract)
        do(17, cp, rows[:, 0], ps[0:R, 6, 0:P])
        for l in range(LEVELS):
            w, src, dst = 1 << l, rows[:, l % 2], rows[:, (l + 1) % 2]
            dve.wait_ge(step, 17 + l)
            cp(dst[:, 0:w], src[:, 0:w])
            tt(dst[:, w:], src[:, w:], src[:, 0:P - w], ALU.max).then_inc(step, 1)
        do(26, cp, flat(gates[:, 1]), ps[:, 7, 0:R])
        do(28, cp, flat(last[:]), ps[:, 5, 0:R])
        do(29, cp, flat(end[:]), ps[:, 3, 0:R])
        do(30, nc.vector.memset, gates[:, 4, 0], 0.0)
        n = 31
        for c in range(TILES):
            if c == TILES - 1:
                do(n, cp, gates[:, 4, c], m_end[:, 1]); n += 1
            do(n, tt, end[:, c], end[:, c], gates[:, 4, c], ALU.max); n += 1
            m_next = gates[:, 4, c + 1] if c < TILES - 2 else m_end[:, c - TILES + 2]
            do(n, tt, m_next, last[:, c], end[:, c], ALU.add); n += 1
        assert n == 50
        do(50, tt, gates[:, 5], gates[:, 4], end[:], ALU.subtract)
        do(52, tt, gates[:, 3], gates[:, 0], end[:], ALU.subtract)
        do(54, tt, gates[:, 1], gates[:, 1], gates[:, 4], ALU.max)
        do(55, tt, gates[:, 2], gates[:, 1], b[:], ALU.add)
        do(56, ts, gates[:, 3], gates[:, 3], MDK ** -0.5, None, ALU.mult)
        dve.wait_ge(step, 56)

    pro = Parts()
    pro.sync, pro.gpsimd, pro.tensor, pro.scalar, pro.scalar_last = sync, gpsimd, tensor, scalar, scalar_last
    pro.vector, pro.w_split, pro.ab_done, pro.step = vector, w_split, ab_done, step
    return pro




def build_trunk(nc, a):
    with ExitStack() as ctx:
        buf = lambda s, *sh: ctx.enter_context(nc.sbuf_tensor(s, *sh))
        tk = Trunk()
        tk.ps = ctx.enter_context(nc.psum_tensor("ps", [P, 8, 512], F32))
        tk.x_dram = nc.dram_tensor("x_kept", (P, KB, TOK), F32).ap()
        tk.ones, tk.ident, tk.upto = buf("ones", [P, P], F32), buf("ident", [P, P], F32), buf("upto", [P, P], F32)
        tk.later_neg = buf("later_neg", [P, P], F32)
        tk.joins = buf("joins", [P, LEVELS, P], BF16)
        tk.eps, tk.one, tk.log_dk = buf("eps", [P, 1], F32), buf("one", [P, 1], F32), buf("log_dk", [P, 1], F32)
        tk.hi, tk.lo = buf("act_hi", [P, KB, TOK], F32R), buf("act_lo", [P, KB, TOK], F32R)

        tk.x = buf("x", [P, KB, TOK], F32)

        load_phase(nc, tk, a["x_prompt"], a["x_sample"])
        norm_phase(nc, tk, a["norm_mix"][0], "norm0")
        gdn_phase(nc, tk, a)
        out_phase(nc, tk, a["gdn_w_out"][0], "gdn_out")
        ffn_phase(nc, tk, a["norm_ffn"][0], a["ffn_w_gu"][0], a["ffn_w_down"][0], "ffn0")
        norm_phase(nc, tk, a["norm_mix"][1], "norm2")
        mlstm_phase(nc, tk, a)
        out_phase(nc, tk, a["ml_w_out"][0], "ml_out")
        ffn_phase(nc, tk, a["norm_ffn"][1], a["ffn_w_gu"][1], a["ffn_w_down"][1], "ffn1")
        store_phase(nc, tk, a["norm_final"], a["y_prompt"], a["y_sample"])


INPUTS = ["x_prompt", "x_sample", "state_gdn_conv", "state_gdn_S", "state_mlstm_C", "state_mlstm_n", "state_mlstm_m",
          "norm_mix", "gdn_w_in", "gdn_conv_w", "gdn_a_log", "gdn_dt_bias", "gdn_norm", "gdn_w_out", "ml_w_in",
          "ml_b_i", "ml_b_f", "ml_norm", "ml_w_out", "norm_ffn", "ffn_w_gu", "ffn_w_down", "norm_final"]
OUTPUTS = [("y_prompt", (1, PROMPT, D)), ("y_sample", (1, SAMPLE, D)),
           ("p_conv", (1, 1, HIST, 3 * D)), ("p_S", (1, 1, HEADS, DK, DV)), ("p_C", (1, 1, HEADS, MDK, DV)),
           ("p_n", (1, 1, HEADS, MDK)), ("p_m", (1, 1, HEADS)),
           ("s_conv", (1, 1, HIST, 3 * D)), ("s_S", (1, 1, HEADS, DK, DV)), ("s_C", (1, 1, HEADS, MDK, DV)),
           ("s_n", (1, 1, HEADS, MDK)), ("s_m", (1, 1, HEADS))]


def kernel(**inputs):
    import numpy as np
    import concourse.bacc as bacc
    from concourse.bass_utils import run_bass_kernel_spmd

    nc = bacc.Bacc("TRN2", target_bir_lowering=False, num_devices=1)
    arrays, a = {}, {}
    for name in INPUTS:
        arrays[f"in_{name}"] = np.ascontiguousarray(inputs[name])
        a[name] = nc.dram_tensor(f"in_{name}", arrays[f"in_{name}"].shape, F32, kind="ExternalInput").ap()
    for name, shape in OUTPUTS:
        a[name] = nc.dram_tensor(f"out_{name}", shape, F32, kind="ExternalOutput").ap()
    build_trunk(nc, a)
    got = run_bass_kernel_spmd(nc, [arrays], core_ids=[0]).results[0]
    return tuple(got[f"out_{name}"] for name, _ in OUTPUTS)
```
